# Optimizing a Trainium2 kernel written in Bass

```python
import math
import jax, jax.numpy as jnp
from jax import lax
import numpy as np

D_MODEL = 1024
BATCH = 1
SEQ = 256
DEPTH = 2

N_A = DEPTH // 2
N_B = DEPTH - N_A

H_A = 4
DK_A = D_MODEL // H_A
DV_A = 2 * DK_A
WIDTH_A = H_A * DV_A
CHUNK = 128
ROPE_BASE_A = 10000.0

H_B = 16
QK_NOPE = 128
QK_ROPE = 64
V_HEAD = 128
Q_LORA = 768
KV_LORA = 512
WIDTH_B = H_B * V_HEAD
Q_BLOCK = 128
ROPE_BASE_B = 10000.0

IN_A = H_A * DK_A * 2 + WIDTH_A + WIDTH_A
IN_B = Q_LORA + WIDTH_B

DEEPNORM_ALPHA = (2.0 * DEPTH) ** 0.25
DEEPNORM_BETA = (8.0 * DEPTH) ** -0.25


def _layer_norm(x, g, b, eps=1e-5):
    xf = x.astype(jnp.float32)
    mu = jnp.mean(xf, axis=-1, keepdims=True)
    var = jnp.mean(jnp.square(xf - mu), axis=-1, keepdims=True)
    return ((xf - mu) * lax.rsqrt(var + eps)).astype(x.dtype) * g + b

def _rms_norm(x, g, eps=1e-6):
    xf = x.astype(jnp.float32)
    return (xf * lax.rsqrt(jnp.mean(jnp.square(xf), axis=-1, keepdims=True) + eps)).astype(x.dtype) * g

def _rope(x, base):
    s, d = x.shape[1], x.shape[-1]
    half = d // 2
    inv = base ** (-jnp.arange(half, dtype=jnp.float32) / half)
    ang = jnp.arange(s, dtype=jnp.float32)[:, None] * inv[None, :]
    shp = (s,) + (1,) * (x.ndim - 3) + (half,)
    cos = jnp.cos(ang).reshape(shp).astype(x.dtype)
    sin = jnp.sin(ang).reshape(shp).astype(x.dtype)
    x1, x2 = x[..., :half], x[..., half:]
    return jnp.concatenate([x1 * cos - x2 * sin, x2 * cos + x1 * sin], axis=-1)

def _chunkwise_retention(q, k, v):
    b, s, h, dk = q.shape
    dv = v.shape[-1]
    n = s // CHUNK

    def to_chunks(t):
        return t.astype(jnp.float32).reshape(b, n, CHUNK, h, t.shape[-1]).transpose(1, 0, 3, 2, 4)

    qc, kc, vc = to_chunks(q), to_chunks(k), to_chunks(v)
    lg = jnp.log1p(-jnp.exp2(-5.0 - jnp.arange(h, dtype=jnp.float32)))
    idx = jnp.arange(CHUNK, dtype=jnp.float32)
    diff = idx[:, None] - idx[None, :]
    causal = diff >= 0
    dmat = jnp.where(causal, jnp.exp(jnp.where(causal, diff, 0.0)[None] * lg[:, None, None]), 0.0)
    qdec = jnp.exp((idx + 1.0)[None, :] * lg[:, None])
    kdec = jnp.exp((CHUNK - 1.0 - idx)[None, :] * lg[:, None])
    cdec = jnp.exp(CHUNK * lg)

    def step(state, inp):
        qi, ki, vi = inp
        scores = jnp.einsum('bhcd,bhed->bhce', qi, ki) * dmat
        inner = jnp.einsum('bhce,bhev->bhcv', scores, vi)
        cross = jnp.einsum('bhcd,bhdv->bhcv', qi * qdec[None, :, :, None], state)
        state = state * cdec[None, :, None, None] + jnp.einsum(
            'bhcd,bhcv->bhdv', ki * kdec[None, :, :, None], vi)
        return state, inner + cross

    init = jnp.zeros((b, h, dk, dv), jnp.float32)
    _, out = lax.scan(step, init, (qc, kc, vc))
    return out.transpose(1, 0, 3, 2, 4).reshape(b, s, h, dv)

def _retention_layer(x, w_in, w_out):
    b, s, _ = x.shape
    hproj = x @ w_in
    qk = H_A * DK_A
    q = hproj[..., :qk].reshape(b, s, H_A, DK_A)
    k = hproj[..., qk:2 * qk].reshape(b, s, H_A, DK_A)
    v = hproj[..., 2 * qk:2 * qk + WIDTH_A].reshape(b, s, H_A, DV_A)
    gate = hproj[..., 2 * qk + WIDTH_A:]
    q = _rope(q, ROPE_BASE_A)
    k = _rope(k, ROPE_BASE_A) * (DK_A ** -0.5)
    o = _chunkwise_retention(q, k, v)
    mu = jnp.mean(o, axis=-1, keepdims=True)
    var = jnp.mean(jnp.square(o - mu), axis=-1, keepdims=True)
    o = ((o - mu) * lax.rsqrt(var + 1e-5)).astype(x.dtype).reshape(b, s, WIDTH_A)
    return (o * jax.nn.silu(gate)) @ w_out

def _shared_latent_kv(x, w_down, kv_norm, w_up):
    b, s, _ = x.shape
    c = x @ w_down
    lat = _rms_norm(c[..., :KV_LORA], kv_norm)
    k_rope = _rope(c[..., KV_LORA:], ROPE_BASE_B)
    kv = (lat @ w_up).reshape(b, s, H_B, QK_NOPE + V_HEAD)
    return kv[..., :QK_NOPE], k_rope, kv[..., QK_NOPE:]

def _causal_block_attention(q_nope, q_rope, k_nope, k_rope, v):
    b, s, h, _ = q_nope.shape
    nb = s // Q_BLOCK
    scale = (QK_NOPE + QK_ROPE) ** -0.5
    qn_b = q_nope.reshape(b, nb, Q_BLOCK, h, QK_NOPE).transpose(1, 0, 2, 3, 4)
    qr_b = q_rope.reshape(b, nb, Q_BLOCK, h, QK_ROPE).transpose(1, 0, 2, 3, 4)
    kpos = jnp.arange(s)

    def block(args):
        qn_i, qr_i, i = args
        sc = (jnp.einsum('bqhd,bkhd->bhqk', qn_i, k_nope)
              + jnp.einsum('bqhr,bkr->bhqk', qr_i, k_rope)).astype(jnp.float32) * scale
        qpos = i * Q_BLOCK + jnp.arange(Q_BLOCK)
        sc = jnp.where(kpos[None, :] <= qpos[:, None], sc, -jnp.inf)
        p = jax.nn.softmax(sc, axis=-1).astype(v.dtype)
        return jnp.einsum('bhqk,bkhd->bqhd', p, v)

    out = lax.map(block, (qn_b, qr_b, jnp.arange(nb)))
    return out.transpose(1, 0, 2, 3, 4).reshape(b, s, h, V_HEAD)

def _mla_layer(x, w_in, q_norm, w_uq, w_out, k_nope, k_rope, v):
    b, s, _ = x.shape
    hproj = x @ w_in
    q_lat, gate = hproj[..., :Q_LORA], hproj[..., Q_LORA:]
    q = (_rms_norm(q_lat, q_norm) @ w_uq).reshape(b, s, H_B, QK_NOPE + QK_ROPE)
    q_nope = q[..., :QK_NOPE]
    q_rope = _rope(q[..., QK_NOPE:], ROPE_BASE_B)
    o = _causal_block_attention(q_nope, q_rope, k_nope, k_rope, v).reshape(b, s, WIDTH_B)
    return (o * jax.nn.silu(gate)) @ w_out

def first_inputs(seed: int = 0) -> dict:
    key = jax.random.key(seed)
    ks = jax.random.split(key, 16)
    nrm = jax.random.normal
    f32 = jnp.float32
    return {
        "x": nrm(ks[0], (BATCH, SEQ, D_MODEL), f32),
        "a_w_in": nrm(ks[1], (N_A, D_MODEL, IN_A), f32) * D_MODEL ** -0.5,
        "a_w_out": nrm(ks[2], (N_A, WIDTH_A, D_MODEL), f32) * (WIDTH_A ** -0.5 * DEEPNORM_BETA),
        "b_w_in": nrm(ks[3], (N_B, D_MODEL, IN_B), f32) * D_MODEL ** -0.5,
        "b_q_norm": 1.0 + 0.02 * nrm(ks[4], (N_B, Q_LORA), f32),
        "b_w_uq": nrm(ks[5], (N_B, Q_LORA, H_B * (QK_NOPE + QK_ROPE)), f32) * Q_LORA ** -0.5,
        "b_w_out": nrm(ks[6], (N_B, WIDTH_B, D_MODEL), f32) * (WIDTH_B ** -0.5 * DEEPNORM_BETA),
        "kv_w_down": nrm(ks[7], (D_MODEL, KV_LORA + QK_ROPE), f32) * D_MODEL ** -0.5,
        "kv_norm": 1.0 + 0.02 * nrm(ks[8], (KV_LORA,), f32),
        "kv_w_up": nrm(ks[9], (KV_LORA, H_B * (QK_NOPE + V_HEAD)), f32) * KV_LORA ** -0.5,
        "ln_g": 1.0 + 0.02 * nrm(ks[10], (DEPTH, D_MODEL), f32),
        "ln_b": 0.02 * nrm(ks[11], (DEPTH, D_MODEL), f32),
    }

def first_block(x, a_w_in, a_w_out, b_w_in, b_q_norm, b_w_uq, b_w_out,
              kv_w_down, kv_norm, kv_w_up, ln_g, ln_b):
    shared = None
    for layer in range(DEPTH):
        if layer < N_A:
            y = _retention_layer(x, a_w_in[layer], a_w_out[layer])
        else:
            j = layer - N_A
            if j == 0:
                shared = _shared_latent_kv(x, kv_w_down, kv_norm, kv_w_up)
            y = _mla_layer(x, b_w_in[j], b_q_norm[j], b_w_uq[j], b_w_out[j], *shared)
        x = _layer_norm(DEEPNORM_ALPHA * x + y, ln_g[layer], ln_b[layer])
    return x


DEPTH_2 = 1

CHUNK_2 = 64
D_RNN = 1024
RNN_BLOCKS = 16
RNN_BLOCK_DIM = D_RNN // RNN_BLOCKS
CONV_WIDTH = 4
LRU_C = 8.0
N_HEADS = 16
N_KV_HEADS = 4
HEAD_DIM = 64
D_ATTN = N_HEADS * HEAD_DIM
D_KV = N_KV_HEADS * HEAD_DIM
IDX_HEADS = 8
IDX_DIM = 64
TOPK_MAX = 256
D_FF = 4 * D_MODEL
N_BRANCHES = 2
EPS = 1e-6
SPLITS = (D_RNN, D_RNN, D_ATTN, D_KV, D_KV, IDX_HEADS * IDX_DIM, IDX_DIM, IDX_HEADS, N_BRANCHES * D_MODEL)
D_IN = D_RNN + D_RNN + D_ATTN + D_KV + D_KV + IDX_HEADS * IDX_DIM + IDX_DIM + IDX_HEADS + N_BRANCHES * D_MODEL


def rms_norm(x, w):
    xf = x.astype(jnp.float32)
    y = xf * lax.rsqrt(jnp.mean(xf * xf, axis=-1, keepdims=True) + EPS)
    return (y * w.astype(jnp.float32)).astype(x.dtype)

def causal_depthwise_conv(x, w, b):
    T = x.shape[1]
    xp = jnp.pad(x, ((0, 0), (CONV_WIDTH - 1, 0), (0, 0)))
    out = b
    for j in range(CONV_WIDTH):
        out = out + xp[:, j:j + T] * w[j]
    return out

def block_diag_linear(x, w, b):
    xb = x.reshape(x.shape[:-1] + (RNN_BLOCKS, RNN_BLOCK_DIM))
    y = jnp.einsum('btnd,nde->btne', xb, w)
    return y.reshape(x.shape) + b

def rg_lru(x, wa, ba, wx, bx, lam):
    r = jax.nn.sigmoid(block_diag_linear(x, wa, ba).astype(jnp.float32))
    i = jax.nn.sigmoid(block_diag_linear(x, wx, bx).astype(jnp.float32))
    log_a = -LRU_C * r * jax.nn.softplus(-lam.astype(jnp.float32))
    a = jnp.exp(log_a)
    mult = jnp.sqrt(-jnp.expm1(2.0 * log_a))
    u = mult * (i * x.astype(jnp.float32))

    def combine(c1, c2):
        a1, b1 = c1
        a2, b2 = c2
        return a1 * a2, a2 * b1 + b2

    _, h = lax.associative_scan(combine, (a, u), axis=1)
    return h.astype(x.dtype)

def dsa_attention(q, k, v, iq, ik, iw):
    B, T = q.shape[0], q.shape[1]
    n_chunks = T // CHUNK_2
    top_k = min(TOPK_MAX, T // 4)
    group = N_HEADS // N_KV_HEADS
    scale = HEAD_DIM ** -0.5
    idx_scale = (IDX_DIM ** -0.5) * (IDX_HEADS ** -0.5)
    key_pos = jnp.arange(T)

    def one_chunk(c):
        start = c * CHUNK_2
        qc = lax.dynamic_slice_in_dim(q, start, CHUNK_2, axis=1)
        iqc = lax.dynamic_slice_in_dim(iq, start, CHUNK_2, axis=1)
        iwc = lax.dynamic_slice_in_dim(iw, start, CHUNK_2, axis=1)
        limit = start + CHUNK_2
        visible = key_pos < limit
        rel = jax.nn.relu(jnp.einsum('bqhd,bsd->bqhs', iqc, ik).astype(jnp.float32))
        score = jnp.einsum('bqhs,bqh->bqs', rel, iwc.astype(jnp.float32)) * idx_scale
        score = jnp.where(visible, score, -jnp.inf)
        _, idx = lax.top_k(score, top_k)
        valid = idx < limit
        k_sel = jax.vmap(lambda kb, ib: kb[ib])(k, idx)
        v_sel = jax.vmap(lambda vb, ib: vb[ib])(v, idx)
        qg = qc.reshape(B, CHUNK_2, N_KV_HEADS, group, HEAD_DIM)
        s = jnp.einsum('bqgrd,bqkgd->bqgrk', qg, k_sel).astype(jnp.float32) * scale
        s = jnp.where(valid[:, :, None, None, :], s, -jnp.inf)
        p = jax.nn.softmax(s, axis=-1).astype(v.dtype)
        o = jnp.einsum('bqgrk,bqkgd->bqgrd', p, v_sel)
        return o.reshape(B, CHUNK_2, D_ATTN)

    out = lax.map(one_chunk, jnp.arange(n_chunks))
    return out.transpose(1, 0, 2, 3).reshape(B, T, D_ATTN)

def hybrid_layer(x, norm1_w, w_in, conv_w, conv_b, rg_wa, rg_ba, rg_wx, rg_bx, rg_lambda,
                 q_norm_w, k_norm_w, idx_k_norm_w, w_o_rnn, w_o_attn, gate_b, w_out,
                 norm2_w, w_ff_in, w_ff_out):
    B, T, _ = x.shape
    h = rms_norm(x, norm1_w)
    u = h @ w_in
    offsets = np.cumsum(SPLITS)[:-1].tolist()
    rnn_x, rnn_gate, q, k, v, iq, ik, iw, g = jnp.split(u, offsets, axis=-1)

    xc = causal_depthwise_conv(rnn_x, conv_w, conv_b)
    y_rnn = rg_lru(xc, rg_wa, rg_ba, rg_wx, rg_bx, rg_lambda) * jax.nn.gelu(rnn_gate)

    q = rms_norm(q.reshape(B, T, N_HEADS, HEAD_DIM), q_norm_w)
    k = rms_norm(k.reshape(B, T, N_KV_HEADS, HEAD_DIM), k_norm_w)
    v = v.reshape(B, T, N_KV_HEADS, HEAD_DIM)
    iq = iq.reshape(B, T, IDX_HEADS, IDX_DIM)
    ik = rms_norm(ik, idx_k_norm_w)
    y_attn = dsa_attention(q, k, v, iq, ik, iw)

    gates = jax.nn.sigmoid((g + gate_b.reshape(-1)).astype(jnp.float32)).astype(x.dtype)
    gates = gates.reshape(B, T, N_BRANCHES, D_MODEL)
    merged = gates[:, :, 0] * (y_rnn @ w_o_rnn) + gates[:, :, 1] * (y_attn @ w_o_attn)
    x = x + merged @ w_out

    h2 = rms_norm(x, norm2_w)
    x = x + jnp.square(jax.nn.relu(h2 @ w_ff_in)) @ w_ff_out
    return x

def second_inputs(seed: int = 0) -> dict:
    key = jax.random.key(seed)
    ks = jax.random.split(key, 24)
    f32 = jnp.float32

    def nrm(k, shape, scale):
        return jax.random.normal(k, shape, f32) * scale

    a0 = jax.random.uniform(ks[9], (DEPTH_2, D_RNN), f32, 0.9, 0.999) ** (1.0 / LRU_C)
    rg_lambda = jnp.log(a0) - jnp.log1p(-a0)
    return {
        "x": nrm(ks[0], (BATCH, SEQ, D_MODEL), 1.0),
        "norm1_w": 1.0 + nrm(ks[1], (DEPTH_2, D_MODEL), 0.02),
        "w_in": nrm(ks[2], (DEPTH_2, D_MODEL, D_IN), D_MODEL ** -0.5),
        "conv_w": nrm(ks[3], (DEPTH_2, CONV_WIDTH, D_RNN), CONV_WIDTH ** -0.5),
        "conv_b": nrm(ks[4], (DEPTH_2, D_RNN), 0.02),
        "rg_wa": nrm(ks[5], (DEPTH_2, RNN_BLOCKS, RNN_BLOCK_DIM, RNN_BLOCK_DIM), RNN_BLOCK_DIM ** -0.5),
        "rg_ba": nrm(ks[6], (DEPTH_2, D_RNN), 0.02),
        "rg_wx": nrm(ks[7], (DEPTH_2, RNN_BLOCKS, RNN_BLOCK_DIM, RNN_BLOCK_DIM), RNN_BLOCK_DIM ** -0.5),
        "rg_bx": nrm(ks[8], (DEPTH_2, D_RNN), 0.02),
        "rg_lambda": rg_lambda,
        "q_norm_w": 1.0 + nrm(ks[10], (DEPTH_2, HEAD_DIM), 0.02),
        "k_norm_w": 1.0 + nrm(ks[11], (DEPTH_2, HEAD_DIM), 0.02),
        "idx_k_norm_w": 1.0 + nrm(ks[12], (DEPTH_2, IDX_DIM), 0.02),
        "w_o_rnn": nrm(ks[13], (DEPTH_2, D_RNN, D_MODEL), D_RNN ** -0.5),
        "w_o_attn": nrm(ks[14], (DEPTH_2, D_ATTN, D_MODEL), D_ATTN ** -0.5),
        "gate_b": nrm(ks[15], (DEPTH_2, N_BRANCHES, D_MODEL), 0.02),
        "w_out": nrm(ks[16], (DEPTH_2, D_MODEL, D_MODEL), D_MODEL ** -0.5),
        "norm2_w": 1.0 + nrm(ks[17], (DEPTH_2, D_MODEL), 0.02),
        "w_ff_in": nrm(ks[18], (DEPTH_2, D_MODEL, D_FF), D_MODEL ** -0.5),
        "w_ff_out": nrm(ks[19], (DEPTH_2, D_FF, D_MODEL), D_FF ** -0.5),
    }

def second_block(x, norm1_w, w_in, conv_w, conv_b, rg_wa, rg_ba, rg_wx, rg_bx, rg_lambda,
              q_norm_w, k_norm_w, idx_k_norm_w, w_o_rnn, w_o_attn, gate_b, w_out,
              norm2_w, w_ff_in, w_ff_out):
    for l in range(DEPTH_2):
        x = hybrid_layer(x, norm1_w[l], w_in[l], conv_w[l], conv_b[l], rg_wa[l], rg_ba[l],
                         rg_wx[l], rg_bx[l], rg_lambda[l], q_norm_w[l], k_norm_w[l],
                         idx_k_norm_w[l], w_o_rnn[l], w_o_attn[l], gate_b[l], w_out[l],
                         norm2_w[l], w_ff_in[l], w_ff_out[l])
    return x


def setup_inputs(seed=0):
    out = dict(first_inputs(seed))
    for name, value in second_inputs(seed + 1).items():
        if name != "x":
            out[name + "_2"] = value
    return out


def reference(
    x, a_w_in, a_w_out, b_w_in, b_q_norm, b_w_uq, b_w_out, kv_w_down, kv_norm, kv_w_up, ln_g,
    ln_b, norm1_w_2, w_in_2, conv_w_2, conv_b_2, rg_wa_2, rg_ba_2, rg_wx_2, rg_bx_2,
    rg_lambda_2, q_norm_w_2, k_norm_w_2, idx_k_norm_w_2, w_o_rnn_2, w_o_attn_2, gate_b_2,
    w_out_2, norm2_w_2, w_ff_in_2, w_ff_out_2,
):
    x = first_block(
        x, a_w_in, a_w_out, b_w_in, b_q_norm, b_w_uq, b_w_out, kv_w_down, kv_norm, kv_w_up,
        ln_g, ln_b,
    )
    return second_block(
        x, norm1_w_2, w_in_2, conv_w_2, conv_b_2, rg_wa_2, rg_ba_2, rg_wx_2, rg_bx_2,
        rg_lambda_2, q_norm_w_2, k_norm_w_2, idx_k_norm_w_2, w_o_rnn_2, w_o_attn_2, gate_b_2,
        w_out_2, norm2_w_2, w_ff_in_2, w_ff_out_2,
    )


_drawn_inputs = setup_inputs


def setup_inputs(seed=0):
    import zlib

    import numpy as np

    out = dict(_drawn_inputs(seed))
    spreads = {}
    factors = {'b_q_norm': 8.0,
     'kv_norm': 8.0,
     'norm1_w_2': 3.254,
     'rg_ba_2': 8.0,
     'rg_bx_2': 8.0,
     'q_norm_w_2': 8.0,
     'k_norm_w_2': 8.0,
     'idx_k_norm_w_2': 4.378,
     'gate_b_2': 8.0,
     'norm2_w_2': 3.208}
    for name, (base, spread) in spreads.items():
        noise = np.random.default_rng([zlib.crc32(name.encode()), seed]).standard_normal(out[name].shape)
        drawn = base * np.exp(spread * noise) if base else spread * noise
        out[name] = __import__('jax').numpy.asarray(drawn.astype(out[name].dtype))
    for name, factor in factors.items():
        out[name] = (out[name] * factor).astype(out[name].dtype)
    return out
```

```python
import numpy as np
import concourse.bass as bass
from concourse import mybir

F32 = mybir.dt.float32
F32R = mybir.dt.float32r
ACT = mybir.ActivationFunctionType
ALU = mybir.AluOpType
AX = mybir.AxisListType

P = 128
D = 1024
S = 256
NT = S // P
KD = D // P

HA, DKA, DVA = 4, 256, 512
WA = HA * DVA
HB, NOPE, ROPE, VH = 16, 128, 64, 128
QL, KVL = 768, 512
WB = HB * VH
SCALE_B = float(NOPE + ROPE) ** -0.5
ALPHA = 4.0 ** 0.25
DR, HC, HKV, DC = 1024, 16, 4, 64
IH, ID = 8, 64
TOPK = 64
CH = 64
DFF = 4096
SCALE_C = float(DC) ** -0.5
IDX_SCALE = (float(ID) ** -0.5) * (float(IH) ** -0.5)

RING = 4
SLOT = 2048
AHEAD = 2


class Signal:

    def __init__(self, nc, name):
        self.sem = nc.alloc_semaphore(name)
        self.base, self.i, self.per, self.k = 0, 0, 0, 0

    def __call__(self, instruction):
        instruction.then_inc(self.sem, 1)
        self.k += 1
        return self.now()

    def now(self, back=0):
        return (self.sem, self.base + self.i * self.per + (self.k - back))

    def enter(self, i, per):
        self.base, self.k = self.base + self.k, 0
        self.i, self.per = i, per

    def leave(self, count):
        if self.k != self.per:
            raise ValueError(f"a loop's body signals {self.k}, {self.per} were declared")
        self.base, self.i, self.per, self.k = self.base + count * self.per, 0, 0, 0


def wait(engine, *tokens):
    for sem, value in tokens:
        engine.wait_ge(sem, value)


class Core:

    def __init__(self, nc):
        self.nc = nc
        self.T, self.V, self.A, self.G, self.SP = nc.tensor, nc.vector, nc.scalar, nc.gpsimd, nc.sync
        self.pe, self.dve, self.act, self.pool = (Signal(nc, n) for n in ("pe", "dve", "act", "pool"))
        self.landed = [nc.alloc_semaphore(f"w_landed{r}") for r in range(RING)]
        self.w_hi, self.w_lo, self.w_used = (nc.alloc_semaphore(n) for n in ("w_hi", "w_lo", "w_used"))
        self.unit0, self.it, self.upi = 0, 0, 0
        self.V.sem_inc(self.w_lo, RING)
        self.T.sem_inc(self.w_used, RING)
        self.last_unit = None
        self.top = (nc.sbuf_base + 31) // 32 * 32
        self.at = {}

    def place(self, name, shape, dtype=F32, at=None):
        at = self.top if at is None else at
        size = int(np.prod(shape[1:])) * 4
        t = self.nc.alloc_sbuf_tensor_at(name, shape, dtype, offset=at)
        self.top = at + (size + 31) // 32 * 32
        if self.top > self.nc.sbuf_usable_end:
            raise ValueError(f"{name} ends {self.top - self.nc.sbuf_usable_end} bytes after the SBUF")
        self.at[name] = at
        return t

    def loop(self, name, count, upi):
        return _Loop(self, name, count, upi)

    def unit(self, j):
        return self.unit0 + self.it * self.upi + j

    def load(self, j, src):
        slot = j % RING
        if len(src.shape) == 3:
            src = src.rearrange("a p n -> (a p) n")
        self.SP.wait_ge(self.w_lo, self.unit(j) + 1)
        self.SP.dma_start(self.raw[slot][:, 0:src.shape[-1]], src).then_inc(self.landed[slot], 16)

    def split(self, j):
        if self.last_unit is not None and j >= self.last_unit:
            return
        slot = j % RING
        u = self.unit(j)
        self.A.wait_ge(self.landed[slot], 16 * (self.unit0 // RING + 1 + j // RING) + self.it * (16 * (self.upi // RING)))
        self.A.wait_ge(self.w_used, u + 1)
        self.A.activation(self.hi[:, slot, :], self.raw[slot][:, :], ACT.Copy).then_inc(self.w_hi, 1)
        self.V.wait_ge(self.w_hi, u + 1)
        self.V.tensor_tensor(self.lo[:, slot, :], self.raw[slot][:, :], self.hi[:, slot, :].bitcast(F32),
                             ALU.subtract).then_inc(self.w_lo, 1)

    def advance(self, units):
        self.unit0 += units

    def used(self, j):
        return (self.w_used, RING + self.unit(j) + 1)

    def w_used_now(self):
        return (self.w_used, RING + self.unit(0))

    def use(self, j):
        self.T.wait_ge(self.w_lo, RING + self.unit(j) + 1)
        return self.hi[:, j % RING, :], self.lo[:, j % RING, :]

    def mm3(self, out, lhs, rhs, start, stop, used=False):
        (lh, ll), (rh, rl) = lhs, rhs
        self.T.matmul(out, lh, rh, start=start, stop=False, skip_group_check=True)
        self.T.matmul(out, lh, rl, start=False, stop=False, skip_group_check=True)
        m = self.T.matmul(out, ll, rh, start=False, stop=stop, skip_group_check=True)
        return m

    def token_major(self, j, xT, k0, nk, cols, outs, first, last):
        wh, wl = (w.rearrange("p (k n) -> p k n", k=nk) if nk * cols == SLOT
                  else w[:, 0:nk * cols].rearrange("p (k n) -> p k n", k=nk) for w in self.use(j))
        for k in range(nk):
            for t in range(NT):
                x = tuple(z[:, k0 + k, t * P:(t + 1) * P] for z in xT)
                m = self.mm3(outs[t], x, (wh[:, k, :], wl[:, k, :]), first and k == 0, last and k == nk - 1)
        m.then_inc(self.w_used, 1)
        return self.used(j)

    def feature_major(self, j, xT, k0, nk, cols, outs, first, last):
        wh, wl = (w[:, 0:nk * cols].rearrange("p (k n) -> p k n", k=nk) for w in self.use(j))
        for c, out in enumerate(outs):
            for k in range(nk):
                w = tuple(z[:, k, c * P:(c + 1) * P] for z in (wh, wl))
                x = tuple(z[:, k0 + k, :] for z in xT)
                m = self.mm3(out, w, x, first and k == 0 and c % 2 == 0, last and k == nk - 1)
        m.then_inc(self.w_used, 1)
        return self.used(j)


class _Loop:
    def __init__(self, core, name, count, upi):
        self.c, self.name, self.count, self.upi, self.per = core, name, count, upi, LOOPS[name]
        nc = core.nc
        engines = [e.engine for e in (nc.sync, nc.scalar, nc.vector, nc.tensor, nc.gpsimd)]
        self.fori = nc.Fori(0, count, engines=engines)

    def __enter__(self):
        c = self.c
        i = self.fori.__enter__()
        for n, k in self.per.items():
            {"pe": c.pe, "dve": c.dve, "act": c.act, "pool": c.pool}[n].enter(i, k)
        c.it, c.upi = i, self.upi
        return i

    def __exit__(self, *e):
        c = self.c
        self.fori.__exit__(*e)
        if e[0] is not None:
            return False
        got = {n: s.k for n, s in (("pe", c.pe), ("dve", c.dve), ("act", c.act), ("pool", c.pool))}
        if got != self.per:
            raise ValueError(f"LOOPS[{self.name!r}] = {got}")
        for s in (c.pe, c.dve, c.act, c.pool):
            s.leave(self.count)
        c.unit0, c.it, c.upi = c.unit0 + self.count * self.upi, 0, 0
        c.ended = self.name


def table(c, queue, name, src, shape):
    t = c.place(name, shape)
    sem = c.nc.alloc_semaphore("s_" + name)
    queue.dma_start(t[tuple(slice(None) for _ in shape)], src).then_inc(sem, 16)
    return t, (sem, 16)


def transpose_in(c, src, nk, hi, lo, after, banks=(4, 5, 6, 7), weight=None):
    tokens = []
    for n in range(0, nk, 2):
        b = c.ps[:, banks[n // 2 % len(banks)], :]
        if n == 0:
            wait(c.T, *after)
        if n // 2 >= len(banks):
            wait(c.T, tokens[n // 2 - len(banks)])
        for k in range(2):
            for t in range(NT):
                m = c.T.transpose(b[:, (2 * k + t) * P:(2 * k + t + 1) * P], src(t, n + k), c.ident[:, :])
        turned = c.pe(m)
        wait(c.A, turned)
        if weight is None:
            rounded = c.act(c.A.activation(hi(n, 2), b.rearrange("p (k s) -> p k s", k=2), ACT.Copy))
            wait(c.V, rounded)
            tokens.append(c.dve(c.V.tensor_tensor(lo(n, 2), b.rearrange("p (k s) -> p k s", k=2),
                                                  hi(n, 2).bitcast(F32), ALU.subtract)))
        else:
            for k in range(2):
                part = b[:, k * S:(k + 1) * S]
                rounded = c.act(c.A.activation(hi(n + k, 1)[:, 0, :], part, ACT.Copy, scale=weight[:, n + k:n + k + 1]))
            wait(c.V, rounded)
            for k in range(2):
                part = b[:, k * S:(k + 1) * S]
                last = c.V.scalar_tensor_tensor(lo(n + k, 1)[:, 0, :], part, weight[:, n + k:n + k + 1],
                                                hi(n + k, 1)[:, 0, :].bitcast(F32), ALU.mult, ALU.subtract)
            tokens.append(c.dve(last))
    return tokens[-1]


def whole(t):
    return lambda n, k: t[:, n:n + k, :]


def rsqrt(c, var, out, eps, tmp, scale=1.0):
    a = c.dve(c.V.tensor_scalar(tmp[0], var, scale, eps, ALU.mult, ALU.add))
    wait(c.A, a)
    r = c.act(c.A.activation(tmp[1], tmp[0], ACT.Sqrt))
    wait(c.V, r)
    a = c.dve(c.V.reciprocal(out, tmp[1]))
    wait(c.V, a)
    a = c.dve(c.V.tensor_tensor(tmp[1], out, out, ALU.mult))
    wait(c.V, a)
    a = c.dve(c.V.tensor_tensor(tmp[1], tmp[1], tmp[0], ALU.mult))
    wait(c.V, a)
    a = c.dve(c.V.tensor_scalar(tmp[1], tmp[1], -0.5, 1.5, ALU.mult, ALU.add))
    wait(c.V, a)
    return c.dve(c.V.tensor_tensor(out, out, tmp[1], ALU.mult))


def retention_layer(c, d):
    oT = [c.place("a_oT_hi", [P, WA // P, S], F32R, at=c.phase), c.place("a_oT_lo", [P, WA // P, S], F32R)]
    raw = c.place("a_qk_raw", [P, 4, S])
    tcos = c.place("a_tcos", [P, 4, S])
    tsin = c.place("a_tsin", [P, 4, S])
    qk = c.place("a_qk", [P, 4, S])
    sm = c.place("a_scores", [P, 3 * P])
    v = c.place("a_v", [P, NT, DVA])
    g = c.place("a_gate", [P, NT, DVA])
    o = c.place("a_o", [P, NT, DVA])
    st = c.place("a_stats", [P, NT, 6])
    mv = c.place("a_mv", [P, NT, 2])
    rs = c.place("a_rs", [P, NT])
    tmp = [c.place(f"a_tmp{n}", [P, NT]) for n in range(2)]
    ropeA, t_rope = table(c, c.A, "ropeA", d["k_ropeA"], [P, 2, S])
    decay, t_decay = table(c, c.A, "decay", d["k_decay"], [P, HA, 3 * P])
    wait(c.V, t_rope, t_decay)
    wait(c.G, t_rope)
    w = d["a_w_in"]
    cos, sin = (ropeA[:, n:n + 1, :].broadcast_to([P, 4, S]) for n in range(2))
    ps = c.ps

    def turn(head, after):
        wait(c.T, *after)
        for n in range(2):
            b = ps[:, 4 + n, :]
            for k in range(2):
                for t in range(NT):
                    m = c.T.transpose(b[:, (2 * k + t) * P:(2 * k + t + 1) * P],
                                      o[:, t, (2 * n + k) * P:(2 * n + k + 1) * P], c.ident[:, :])
            turned = c.pe(m)
            at = bass.ds(head * 4 + 2 * n, 2)
            b = b.rearrange("p (k s) -> p k s", k=2)
            wait(c.A, turned)
            rounded = c.act(c.A.activation(oT[0][:, at, :], b, ACT.Copy))
            wait(c.V, rounded)
            read = c.dve(c.V.tensor_tensor(oT[1][:, at, :], b, oT[0][:, at, :].bitcast(F32), ALU.subtract))
        return turned, read

    with c.loop("retention", 2, 12) as i:
        t0, v0, a0, g0 = c.pe.now(), c.dve.now(), c.act.now(), c.pool.now()
        wait(c.T, v0, a0, g0)
        wait(c.A, t0, v0, g0)
        wait(c.V, t0, a0, g0)
        wait(c.G, v0, a0)
        scores_read = roped = o_in = turned_read = v0
        gate_in, gated, turned = a0, g0, t0
        todo = None
        for a in range(2):
            u = 6 * a
            for n in range(6):
                c.load(u + n, w[bass.ds(i * 2 + a, 1), n])

            wait(c.T, scores_read)
            for half in range(2):
                c.split(u + half + AHEAD)
                done = c.feature_major(u + half, c.xT, 0, KD, DKA, HALVES(ps[:, half, :]), True, True)
            wait(c.A, done, roped, gated)
            for n in range(2):
                raw_in = c.act(c.A.activation(raw[:, 2 * n:2 * n + 2, :], ps[:, n, :].rearrange("p (k s) -> p k s", k=2),
                                              ACT.Copy))
            if todo:
                turned, turned_read = turn(*todo)
            wait(c.G, raw_in, roped)
            sines = c.pool(c.G.tensor_tensor(tsin[:, :, :], raw[:, :, :], sin, ALU.mult))
            wait(c.V, raw_in)
            cosines = c.dve(c.V.tensor_tensor(tcos[:, :, :], raw[:, :, :], cos, ALU.mult))
            wait(c.V, sines, cosines)
            c.V.tensor_tensor(qk[:, 0::2, :], tcos[:, 0::2, :], tsin[:, 1::2, :], ALU.subtract)
            roped = c.dve(c.V.tensor_tensor(qk[:, 1::2, :], tcos[:, 1::2, :], tsin[:, 0::2, :], ALU.add))

            v_out = [ps[:, 4 + t, :] for t in range(NT)]
            wait(c.T, turned_read)
            c.split(u + 2 + AHEAD)
            c.token_major(u + 2, c.xT, 0, 4, 512, v_out, True, False)
            wait(c.T, roped)
            for e, cols in enumerate((slice(0, 2 * P), slice(2 * P, 3 * P))):
                for k in range(2):
                    m = c.T.matmul(ps[:, 0, cols], qk[:, 2 + k, e * P:(e + 1) * P], qk[:, k, e * P:2 * P],
                                   start=e == 0 and k == 0, stop=k == 1, skip_group_check=True)
            scored = c.pe(m)
            c.split(u + 3 + AHEAD)
            wait(c.V, scored)
            scores_read = c.dve(c.V.tensor_tensor(sm[:, :], ps[:, 0, 0:3 * P],
                                                  decay[:, bass.ds(i * 2 + a, 1), :].rearrange("p a n -> p (a n)"), ALU.mult))
            done = c.token_major(u + 3, c.xT, 4, 4, 512, v_out, False, True)
            wait(c.A, done)
            v_in0 = c.act(c.A.activation(v[:, 0, :], v_out[0], ACT.Copy))
            wait(c.V, done)
            v_in1 = c.dve(c.V.tensor_copy(v[:, 1, :], v_out[1]))

            g_out = [ps[:, 2 + t, :] for t in range(NT)]
            c.split(u + 4 + AHEAD)
            wait(c.T, gate_in)
            c.token_major(u + 4, c.xT, 0, 4, 512, g_out, True, False)
            wait(c.T, scores_read, v_in0, v_in1, o_in)
            c.T.matmul(ps[:, 6, :], sm[:, 0:P], v[:, 0, :], start=True, stop=True)
            c.T.matmul(ps[:, 7, :], sm[:, P:2 * P], v[:, 0, :], start=True, stop=False)
            inner = c.pe(c.T.matmul(ps[:, 7, :], sm[:, 2 * P:3 * P], v[:, 1, :], start=False, stop=True))
            c.split(u + 5 + AHEAD)
            done = c.token_major(u + 5, c.xT, 4, 4, 512, g_out, False, True)
            wait(c.V, inner)
            for t in range(NT):
                s_ = c.dve(c.V.bn_stats(st[:, t, :], ps[:, 6 + t, :]))
            wait(c.V, s_)
            c.V.memset(tmp[0][:, :], 0.0)
            for t in range(NT):
                s_ = c.dve(c.V.bn_aggr(mv[:, t, :], st[:, t, :]))
            wait(c.V, s_)
            r = rsqrt(c, mv[:, :, 1], rs[:, :], 1e-5, [t[:, :] for t in tmp])
            wait(c.V, r, turned)
            for t in range(NT):
                o_in = c.dve(c.V.tensor_scalar(o[:, t, :], ps[:, 6 + t, :], mv[:, t, 0:1], rs[:, t:t + 1],
                                               ALU.subtract, ALU.mult))
            wait(c.A, done, gated)
            for t in range(NT):
                gate_in = c.act(c.A.activation(g[:, t, :], g_out[t], ACT.Silu))
            wait(c.G, gate_in, o_in)
            gated = c.pool(c.G.tensor_tensor(o[:, 0, :], o[:, 0, :], g[:, 0, :], ALU.mult))
            wait(c.V, gate_in, o_in)
            gated1 = c.dve(c.V.tensor_tensor(o[:, 1, :], o[:, 1, :], g[:, 1, :], ALU.mult))
            todo = (i * 2 + a, (gated, gated1))
            roped = gated1
        turn(*todo)
    return oT


def norm_stats(c, res, st, mv, chunks=2):
    for t in range(NT):
        for n in range(chunks):
            s_ = c.dve(c.V.bn_stats(st[:, t, n, :], res[:, t, n * 512:(n + 1) * 512]))
    wait(c.V, s_)
    for t in range(NT):
        s_ = c.dve(c.V.bn_aggr(mv[:, t, :], st[:, t, :, :].rearrange("p a b -> p (a b)")))
    wait(c.V, s_)
    return s_


def layer_norm(c, layer, d, lnw, after):
    lnw, arrived = lnw
    wait(c.V, *after)
    norm_stats(c, c.res, c.st, c.mv)
    r = rsqrt(c, c.mv[:, :, 1], c.rs[:, :], 1e-5, c.tmp)
    wait(c.V, r, arrived)
    t0 = c.dve(c.V.tensor_scalar(c.res[:, 1, :], c.res[:, 1, :], c.mv[:, 1, 0:1], c.rs[:, 1:2], ALU.subtract, ALU.mult))
    wait(c.G, t0, arrived)
    p = c.pool(c.G.tensor_tensor(c.res[:, 1, :], c.res[:, 1, :], lnw[:, 0, :], ALU.mult))
    wait(c.G, p)
    p = c.pool(c.G.tensor_tensor(c.res[:, 1, :], c.res[:, 1, :], lnw[:, 1, :], ALU.add))
    t0 = c.dve(c.V.tensor_scalar(c.res[:, 0, :], c.res[:, 0, :], c.mv[:, 0, 0:1], c.rs[:, 0:1], ALU.subtract, ALU.mult))
    wait(c.V, t0)
    t0 = c.dve(c.V.tensor_tensor(c.res[:, 0, :], c.res[:, 0, :], lnw[:, 0, :], ALU.mult))
    wait(c.V, t0)
    t0 = c.dve(c.V.tensor_tensor(c.res[:, 0, :], c.res[:, 0, :], lnw[:, 1, :], ALU.add))
    return t0, p


def load_ln(c, layer, d, at, after):
    lnw = c.place(f"lnw{layer}", [P, 2, D], at=at)
    sem = c.nc.alloc_semaphore(f"s_lnw{layer}")
    wait(c.A, *after)
    for n, name in enumerate(("ln_g", "ln_b")):
        c.A.dma_start(lnw[:, n, :], d[name][layer:layer + 1, :].broadcast_to([P, D])).then_inc(sem, 16)
    return lnw, (sem, 32)


def out_projection(c, w, oT, alpha, name):
    wait(c.T, c.dve.now(), c.act.now(), c.pool.now())
    if True:
        for b in range(2):
            out = [c.ps[:, 2 * b + t, :] for t in range(NT)]
            for q in range(4):
                j = 4 * b + q
                c.load(j, w[b, q])
                c.split(j + AHEAD)
                done = c.token_major(j, oT, 4 * q, 4, 512, out, q == 0, q == 3)
            wait(c.V, done)
            for t in range(NT):
                r = c.res[:, t, b * 512:(b + 1) * 512]
                added = c.dve(c.V.scalar_tensor_tensor(r, r, alpha, out[t], ALU.mult, ALU.add))
        c.advance(8)
    return added


def HALVES(*banks):
    return [b[:, n * S:(n + 1) * S] for b in banks for n in range(2)]


def latent_attention_layer(c, d):
    ps = c.ps
    oT = [c.place("b_oT_hi", [P, HB, S], F32R, at=c.phase), c.place("b_oT_lo", [P, HB, S], F32R)]
    end = c.top
    lat = c.place("b_lat", [P, NT, KVL], at=c.phase)
    qlat = c.place("b_qlat", [P, NT, QL])
    junk = c.place("b_junk", [P, 4, 512])
    c.top = end
    qlatT = [c.place("b_qlatT_hi", [P, QL // P, S], F32R), c.place("b_qlatT_lo", [P, QL // P, S], F32R)]
    c.ln_at = qlatT_at = end
    latT = [c.place("b_latT_hi", [P, KVL // P, S], F32R), c.place("b_latT_lo", [P, KVL // P, S], F32R)]
    rope, t_rope = table(c, c.A, "ropeB", d["k_ropeB"], [P, 2, S])
    rot, t_rot = table(c, c.A, "rotB", d["k_rotB"], [P, P])
    mask, t_mask = table(c, c.A, "maskB", d["k_maskB"], [P, 3 * P])
    qnorm, t_qn = table(c, c.A, "qnorm", d["b_q_norm"], [P, QL // P])
    kvnorm, t_kn = table(c, c.A, "kvnorm", d["kv_norm"], [P, KVL // P])
    kr = c.place("b_kr", [P, 2, S])
    both = lambda name, *shape: c.place(name, [P, 2, *shape])
    qn, kn, v, gate = both("b_qn", 2, S), both("b_kn", 2, S), both("b_v", NT, 2 * VH), both("b_gate", 2, S)
    qr, p, pT = both("b_qr", S), both("b_p", 3 * P), both("b_pT", 3 * P)
    xr, xc, xs = (c.place(n, [P, S]) for n in ("b_xr", "b_xc", "b_xs"))
    og = c.place("b_og", [P, 2, S])
    few = c.place("b_few", [P, 5, 2, 2])
    sq, sq2, nmax, sums, rsum = (few[:, n, :, :] for n in range(5))
    wait(c.V, t_rope, t_mask, t_qn, t_kn)
    wait(c.G, t_rope)
    wait(c.A, t_qn, t_kn)
    wait(c.T, t_rot)
    zero = c.dve(c.V.memset(kr[:, :, :], 0.0))

    w = d["b_w_qlat"]
    wait(c.T, c.dve.now(), c.act.now())
    for b in range(2):
        for half in range(2):
            j = 2 * b + half
            c.load(j, w[b, half])
            c.split(j + AHEAD)
            done = c.token_major(j, c.xT, 4 * half, 4, 384, [ps[:, 2 * b + t, 0:384] for t in range(NT)],
                                 half == 0, half == 1)
        wait(c.A, done)
        for t in range(NT):
            squared = c.act(c.A.activation(junk[:, 2 * b + t, 0:384], ps[:, 2 * b + t, 0:384], ACT.Square,
                                           accum_out=sq[:, t, b:b + 1]))
    wait(c.V, squared)
    r = c.dve(c.V.tensor_tensor(sq2[:, :, 0], sq[:, :, 0], sq[:, :, 1], ALU.add))
    wait(c.V, r)
    r = rsqrt(c, sq2[:, :, 0], c.rs[:, :], 1e-6, c.tmp, 1.0 / QL)
    wait(c.V, r)
    for b in range(2):
        for t in range(NT):
            qlat_in = c.dve(c.V.tensor_scalar(qlat[:, t, b * 384:(b + 1) * 384], ps[:, 2 * b + t, 0:384],
                                              c.rs[:, t:t + 1], None, ALU.mult))
    c.advance(4)

    DOWN = KVL + 2 * ROPE
    for j in range(4):
        c.load(j, d["kv_w_down"][0, j])
        c.split(j + AHEAD)
        wh, wl = (z[:, 0:2 * DOWN].rearrange("p (k n) -> p k n", k=2) for z in c.use(j))
        for k in range(2):
            first, last = j == 0 and k == 0, j == 3 and k == 1
            for t in range(NT):
                x = tuple(z[:, 2 * j + k, t * P:(t + 1) * P] for z in c.xT)
                c.mm3(ps[:, 4 + t, :], x, (wh[:, k, 0:KVL], wl[:, k, 0:KVL]), first, last)
            x = tuple(z[:, 2 * j + k, :] for z in c.xT)
            m = c.mm3(ps[:, 6, 0:S], (wh[:, k, KVL:DOWN], wl[:, k, KVL:DOWN]), x, first, last)
        m.then_inc(c.w_used, 1)
    done = c.used(3)
    c.advance(4)
    transposed = transpose_in(c, lambda t, k: qlat[:, t, k * P:(k + 1) * P], QL // P, whole(qlatT[0]), whole(qlatT[1]),
                              (qlat_in,), banks=(0, 1, 2), weight=qnorm)
    wait(c.A, done)
    for t in range(NT):
        squared = c.act(c.A.activation(junk[:, t, :], ps[:, 4 + t, :], ACT.Square, accum_out=sq[:, t, 0:1]))
    wait(c.V, squared)
    r = rsqrt(c, sq[:, :, 0], c.rs[:, :], 1e-6, c.tmp, 1.0 / KVL)
    wait(c.V, r)
    for t in range(NT):
        lat_in = c.dve(c.V.tensor_scalar(lat[:, t, :], ps[:, 4 + t, :], c.rs[:, t:t + 1], None, ALU.mult))
    xr_in = c.dve(c.V.tensor_copy(xr[:, :], ps[:, 6, 0:S]))
    wait(c.T, xr_in)
    rotated = c.pe(c.T.matmul(ps[:, 7, 0:S], rot[:, :], xr[:, :], start=True, stop=True))
    wait(c.V, xr_in)
    a = c.dve(c.V.tensor_tensor(xc[:, :], xr[:, :], rope[:, 0, :], ALU.mult))
    wait(c.V, rotated, zero, a)
    a = c.dve(c.V.tensor_tensor(xs[:, :], ps[:, 7, 0:S], rope[:, 1, :], ALU.mult))
    wait(c.V, a)
    for n in range(2):
        rows = slice(n * ROPE, (n + 1) * ROPE)
        kr_in = c.dve(c.V.tensor_tensor(kr[rows, n, :], xc[rows, :], xs[rows, :], ALU.add))
    transposed2 = transpose_in(c, lambda t, k: lat[:, t, k * P:(k + 1) * P], KVL // P, whole(latT[0]), whole(latT[1]),
                               (lat_in,), banks=(3, 4), weight=kvnorm)
    wait(c.T, transposed, transposed2, kr_in)

    w_gate, w_uq, w_kv = d["b_w_gate"], d["b_w_uq"], d["kv_w_up"]
    QC, KC = NOPE + ROPE, NOPE + VH

    class Free:

        def __init__(self, *issued):
            self.ready = self.scores_free = self.pT_bank_free = self.o_free = self.og_free = issued
            self.gate_free = self.uq_free = self.kv_free = self.q_free = self.xr_free = self.xs_free = issued
            self.p_free, self.pT_free = [issued] * 2, [issued] * 2

    def attend_scores(pr, par, h):
        wait(c.T, *pr.ready, *pr.scores_free)
        for q, cols in enumerate((slice(0, P), slice(P, 3 * P))):
            out, qs, keys = ps[:, 5, cols], slice(q * P, (q + 1) * P), slice(0, (q + 1) * P)
            c.T.matmul(out, qn[:, par, h, qs], kn[:, par, h, keys], start=q == 0, stop=False, skip_group_check=True)
            m = c.T.matmul(out, qr[:, par, qs], kr[:, h, keys], start=False, stop=True, skip_group_check=True)
        scored = c.pe(m)
        wait(c.V, scored, *pr.p_free[h])
        c.V.memset(nmax[:, h, :], 0.0)
        for q, cols in enumerate((slice(0, P), slice(P, 3 * P))):
            a = c.dve(c.V.tensor_tensor_reduce(out=p[:, h, cols], in0=ps[:, 5, cols], in1=mask[:, cols],
                                               scale=SCALE_B, scalar=-3.0e38, op0=ALU.add, op1=ALU.max,
                                               accum_out=sums[:, h, q:q + 1]))
        pr.scores_free = (a,)
        wait(c.V, a)
        negated = c.dve(c.V.tensor_scalar(nmax[:, h, :], sums[:, h, :], -1.0, None, ALU.mult))
        wait(c.A, negated)
        for q, cols in enumerate((slice(0, P), slice(P, 3 * P))):
            a = c.act(c.A.activation(p[:, h, cols], p[:, h, cols], ACT.Exp, bias=nmax[:, h, q:q + 1],
                                     accum_out=rsum[:, h, q:q + 1]))
        wait(c.V, a)
        a = c.dve(c.V.reciprocal(rsum[:, h, :], rsum[:, h, :]))
        wait(c.V, a)
        for q, cols in enumerate((slice(0, P), slice(P, 3 * P))):
            a = c.dve(c.V.tensor_scalar(p[:, h, cols], p[:, h, cols], rsum[:, h, q:q + 1], None, ALU.mult))
        pr.p_in = a

    def attend_turn(pr, par, h):
        wait(c.T, pr.p_in, *pr.pT_bank_free)
        for n in range(3):
            m = c.T.transpose(ps[:, 6, n * P:(n + 1) * P], p[:, h, n * P:(n + 1) * P], c.ident[:, :])
        turned = c.pe(m)
        pr.p_free[h] = (turned,)
        wait(c.A, turned, *pr.pT_free[h])
        pr.pT_in = c.act(c.A.activation(pT[:, h, :], ps[:, 6, 0:3 * P], ACT.Copy))
        pr.pT_bank_free = (pr.pT_in,)

    def attend_values(pr, par, h):
        wait(c.T, pr.pT_in, *pr.o_free)
        out = ps[:, 7, h * S:(h + 1) * S]
        cols = slice(h * VH, (h + 1) * VH)
        c.T.matmul(out, v[:, par, 0, cols], pT[:, h, 0:2 * P], start=h == 0, stop=False, skip_group_check=True)
        done = c.pe(c.T.matmul(out[:, P:2 * P], v[:, par, 1, cols], pT[:, h, 2 * P:3 * P], start=False, stop=True,
                               skip_group_check=True))
        pr.pT_free[h] = (done,)
        return done

    def attend_out(pr, par, pair, done):
        wait(c.V, done, *pr.og_free)
        o = c.dve(c.V.tensor_tensor(og[:, :, :], ps[:, 7, :].rearrange("p (h s) -> p h s", h=2), gate[:, par, :, :], ALU.mult))
        pr.o_free = (o,)
        at = bass.ds(pair * 2, 2)
        wait(c.A, o)
        r = c.act(c.A.activation(oT[0][:, at, :], og[:, :, :], ACT.Copy))
        wait(c.G, r)
        g_ = c.pool(c.G.tensor_tensor(oT[1][:, at, :], og[:, :, :], oT[0][:, at, :].bitcast(F32), ALU.subtract))
        pr.og_free = (g_,)

    def step(pr, j0, pair, par, other):
        if pair is not None:
            at = bass.ds(pair, 1)
            c.load(j0, w_gate[at])
            for n in range(2):
                c.load(j0 + 1 + n, w_uq[at, n])
            c.load(j0 + 3, w_kv[at])
            c.split(j0 + AHEAD)
            wait(c.T, *pr.gate_free)
            done = c.feature_major(j0, c.xT, 0, KD, 2 * VH, HALVES(ps[:, 0, :]), True, True)
            wait(c.A, done, *pr.o_free)
            gate_in = c.act(c.A.activation(gate[:, par, :, :], ps[:, 0, :].rearrange("p (h s) -> p h s", h=2), ACT.Silu))
            pr.gate_free = (gate_in,)
        if other is not None:
            attend_scores(pr, 1 - par, 0)
        if pair is not None:
            wait(c.T, *pr.uq_free)
            for n in range(2):
                c.split(j0 + 1 + n + AHEAD)
                wh, wl = (z[:, 0:6 * QC].rearrange("p (k n) -> p k n", k=3) for z in c.use(j0 + 1 + n))
                for q, out in enumerate((ps[:, 1, 0:S], ps[:, 1, S:2 * S], ps[:, 2, 0:S])):
                    for k in range(3):
                        m = c.mm3(out, tuple(z[:, k, q * P:(q + 1) * P] for z in (wh, wl)),
                                  tuple(z[:, 3 * n + k, :] for z in qlatT), n == 0 and k == 0 and q != 1, n == 1 and k == 2)
                m.then_inc(c.w_used, 1)
                if n == 0 and other is not None:
                    attend_turn(pr, 1 - par, 0)
                    attend_scores(pr, 1 - par, 1)
            done = c.used(j0 + 2)
            wait(c.A, done, *pr.q_free)
            qn_in = c.act(c.A.activation(qn[:, par, :, :], ps[:, 1, :].rearrange("p (h s) -> p h s", h=2), ACT.Copy))
            wait(c.V, done, *pr.xr_free)
            xr_in = c.dve(c.V.tensor_copy(xr[:, :], ps[:, 2, 0:S]))
        elif other is not None:
            attend_turn(pr, 1 - par, 0)
            attend_scores(pr, 1 - par, 1)
        if other is not None:
            attend_values(pr, 1 - par, 0)
            attend_turn(pr, 1 - par, 1)
        if pair is not None:
            c.split(j0 + 3 + AHEAD)
            wait(c.T, *pr.kv_free)
            wh, wl = (z[:, 0:4 * 2 * KC].rearrange("p (k n) -> p k n", k=4) for z in c.use(j0 + 3))
            for h in range(2):
                for k in range(4):
                    c.mm3(ps[:, 3, h * S:(h + 1) * S], tuple(z[:, k, h * P:(h + 1) * P] for z in (wh, wl)),
                          tuple(z[:, k, :] for z in latT), h == 0 and k == 0, k == 3)
            for t in range(NT):
                for k in range(4):
                    m = c.mm3(ps[:, 4, t * S:(t + 1) * S], tuple(z[:, k, t * P:(t + 1) * P] for z in latT),
                              tuple(z[:, k, 2 * NOPE:2 * KC] for z in (wh, wl)),
                              t == 0 and k == 0, k == 3)
            m.then_inc(c.w_used, 1)
            done = c.used(j0 + 3)
            wait(c.T, xr_in)
            rotated = c.pe(c.T.matmul(ps[:, 2, S:2 * S], rot[:, :], xr[:, :], start=True, stop=True))
        if other is not None:
            o_done = attend_values(pr, 1 - par, 1)
            attend_out(pr, 1 - par, other, o_done)
        if pair is not None:
            wait(c.G, xr_in, *pr.xs_free)
            cosines = c.pool(c.G.tensor_tensor(xc[:, :], xr[:, :], rope[:, 0, :], ALU.mult))
            pr.xr_free = (cosines, rotated)
            wait(c.V, rotated, *pr.xs_free)
            sines = c.dve(c.V.tensor_tensor(xs[:, :], ps[:, 2, S:2 * S], rope[:, 1, :], ALU.mult))
            pr.uq_free = (sines, qn_in)
            wait(c.G, sines, cosines, *pr.q_free)
            qr_in = c.pool(c.G.tensor_tensor(qr[:, par, :], xc[:, :], xs[:, :], ALU.add))
            pr.xs_free = (qr_in,)
            wait(c.A, done)
            kn_in = c.act(c.A.activation(kn[:, par, :, :], ps[:, 3, :].rearrange("p (h s) -> p h s", h=2), ACT.Copy))
            wait(c.V, done, *pr.q_free)
            v_in = c.dve(c.V.tensor_copy(v[:, par, :, :], ps[:, 4, :].rearrange("p (t n) -> p t n", t=2)))
            pr.kv_free = (kn_in, v_in)
            pr.ready = (kn_in, v_in, qn_in, qr_in)
            pr.q_free = ()
        if other is not None:
            pr.q_free = (o_done,)

    def fresh():
        return Free(c.pe.now(), c.dve.now(), c.act.now(), c.pool.now())

    pr = fresh()
    step(pr, 0, 0, 0, None)
    c.advance(4)
    with c.loop("attention", 3, 8) as i:
        pr = fresh()
        step(pr, 0, i * 2 + 1, 1, i * 2)
        step(pr, 4, i * 2 + 2, 0, i * 2 + 1)
    pr = fresh()
    step(pr, 0, HB // 2 - 1, 1, HB // 2 - 2)
    c.advance(4)
    step(pr, 0, None, 0, HB // 2 - 1)
    return oT


def feature_stage(c, name, count, source, xT, banks, drain, signal, per_unit=1):
    wait(c.T, c.dve.now(), c.act.now(), c.pool.now())

    def body(i):
        for j in range(4):
            n = i * 4 + j
            c.load(j, source(n))
            c.split(j + AHEAD)
            wait(c.T, signal.now(3 * per_unit))
            done = c.feature_major(j, xT, 0, KD, S, HALVES(c.ps[:, banks[j], :]), True, True)
            drain(n, c.ps[:, banks[j], :].rearrange("p (k s) -> p k s", k=2), done, j)

    if count == 1:
        body(0)
        c.advance(4)
    else:
        with c.loop(name, count, 4) as i:
            body(i)


def softplus8(c, lam, out, neg, tmp):
    t, e, q = tmp
    v, one = c.V, lambda ins: wait(c.V, c.dve(ins))
    one(v.tensor_scalar(t, lam, -1.0, None, ALU.mult))
    one(v.tensor_tensor(e, t, lam, ALU.min))
    wait(c.A, c.dve.now())
    wait(v, c.act(c.A.activation(e, e, ACT.Exp)))
    one(v.tensor_scalar(t, e, 2.0, None, ALU.add))
    one(v.reciprocal(q, t))
    one(v.tensor_tensor(e, e, q, ALU.mult))
    one(v.tensor_tensor(t, e, e, ALU.mult))
    one(v.tensor_scalar(q, t, 1.0 / 17.0, None, ALU.mult))
    for n in (15.0, 13.0, 11.0, 9.0, 7.0, 5.0, 3.0):
        one(v.scalar_tensor_tensor(q, q, 1.0 / n, t, ALU.add, ALU.mult))
    one(v.scalar_tensor_tensor(q, q, 1.0, e, ALU.add, ALU.mult))
    one(v.tensor_scalar(t, lam, -1.0, 0.0, ALU.mult, ALU.max))
    one(v.scalar_tensor_tensor(t, q, 2.0, t, ALU.mult, ALU.add))
    one(v.tensor_scalar(out, t, 8.0, None, ALU.mult))
    one(v.tensor_scalar(neg, t, -8.0, None, ALU.mult))


def rms_input(c, h, junk, norm, weight, after):
    wait(c.A, *after)
    for t in range(NT):
        squared = c.act(c.A.activation(junk[:, t, :], c.res[:, t, :], ACT.Square, accum_out=norm[:, t:t + 1]))
    wait(c.V, squared)
    r = rsqrt(c, norm[:, :], c.rs[:, :], 1e-6, c.tmp, 1.0 / D)
    wait(c.V, r, *after)
    for t in range(NT):
        h_in = c.dve(c.V.tensor_scalar(h[:, t, :], c.res[:, t, :], c.rs[:, t:t + 1], None, ALU.mult))
    return transpose_in(c, lambda t, k: h[:, t, k * P:(k + 1) * P], KD, whole(c.xT[0]), whole(c.xT[1]), (h_in,),
                        weight=weight)


def hybrid_layer(c, d, out, normed):
    ps, V, A, G, T = c.ps, c.V, c.A, c.G, c.T
    dve, act, pool, pe = c.dve, c.act, c.pool, c.pe
    everything = lambda: (pe.now(), dve.now(), act.now(), pool.now())
    pair = lambda b: b.rearrange("p (k s) -> p k s", k=2)
    QCOLS = (slice(0, P), slice(P, 3 * P))

    c.top = c.phase
    qk = c.place("c_qk", [P, NT, D + 256])
    v = c.place("c_v", [P, NT, 256])
    iq = c.place("c_iq", [P, NT, IH * ID])
    qT = c.place("c_qT", [P, KD, S])
    kz = c.place("c_kz", [P, HKV, S])
    iqT = c.place("c_iqT", [P, IH // 2, S])
    ikz = c.place("c_ikz", [P, 2, S])
    isc = c.place("c_isc", [P, NT, S])
    xc = c.place("c_xc", [P, KD, S])
    ig = c.place("c_ig", [P, KD, S])
    aa = c.place("c_aa", [P, KD, S])
    gel = c.place("c_gel", [P, KD, S])
    rgw = c.place("c_rgw", [P, 2, KD, P])
    g0 = c.place("c_g0", [P, KD, S])
    ikw = c.place("c_ikw", [P, NT, 2 * ID + IH])
    small = c.top
    rr = c.place("c_rr", [P, KD, S], at=c.at["c_qk"])
    ya = c.place("c_ya", [P, NT, D], at=c.at["c_qk"])
    rl = c.place("c_rl", [P, 2, 3 * P], at=c.at["c_iq"])
    wk = c.place("c_wk", [P, NT, S], at=c.at["c_iq"])
    eqs = c.place("c_eqs", [P, NT, S])
    ones = c.place("c_ones", [P, S], at=c.at["c_iqT"])
    cum = c.place("c_cum", [P, NT, S])
    pT = c.place("c_pT", [P, 4, 3 * P], at=c.at["c_iqT"])
    h = c.place("c_h", [P, NT, D], at=c.at["c_xc"])
    kw_raw = c.place("c_kw_raw", [P, KD, 2 * ID + IH], at=c.at["c_ig"])
    kw = [c.place("c_kw_hi", [P, KD, 2 * ID + IH], F32R), c.place("c_kw_lo", [P, KD, 2 * ID + IH], F32R)]
    junk = c.place("c_junk", [P, NT, D], at=c.at["c_gel"])
    yT = [c.place("c_yT_hi", [P, KD, S], F32R, at=c.at["c_xc"]), c.place("c_yT_lo", [P, KD, S], F32R)]
    zT = yT
    p = c.place("c_p", [P, 4, 3 * P], at=c.at["c_aa"])
    g1 = c.place("c_g1", [P, KD, S], at=c.at["c_rgw"])
    fT = [c.place("c_fT_hi", [P, DFF // P, S], F32R, at=c.phase), c.place("c_fT_lo", [P, DFF // P, S], F32R)]
    fr = c.place("c_fr", [P, 4, 2, S])
    h2 = c.place("c_h2", [P, NT, D], at=c.phase)
    junk2 = c.place("c_junk2", [P, NT, D])
    c.top = small
    wait(A, *everything())
    vec = {}
    for name, n in (("norm1_w_2", 8), ("norm2_w_2", 8), ("rg_ba_2", 8), ("rg_bx_2", 8), ("rg_lambda_2", 8),
                    ("conv_b_2", 8), ("conv_w_2", 32), ("gate_b_2", 16), ("head_norms", 3)):
        vec[name], arrived = table(c, A, "c_" + name, d[name], [P, n])
        wait(V, arrived)
        wait(A, arrived)
    s_kw, s_rgw = c.nc.alloc_semaphore("s_kw"), c.nc.alloc_semaphore("s_rgw")
    A.dma_start(kw_raw[:, :, :].rearrange("p k n -> p (k n)"), d["w_ikw"]).then_inc(s_kw, 16)
    A.dma_start(rgw[:, :, :, :].rearrange("p a k n -> p (a k n)"), d["rg_w"]).then_inc(s_rgw, 16)
    lam8, nlam8 = c.place("c_lam8", [P, 8]), c.place("c_nlam8", [P, 8])
    ltmp = [c.place(f"c_ltmp{n}", [P, 8]) for n in range(3)]
    n2 = c.place("c_n2", [P, NT])
    NH = HC + HKV + 1
    hs, hr, ht0, ht1 = (c.place(n, [P, NT, NH]) for n in ("c_hs", "c_hr", "c_ht0", "c_ht1"))
    m8 = c.place("c_m8", [P, NT, 8])
    cnt = c.place("c_cnt", [P, NT])
    smx, ssum = (c.place(n, [P, 2, 4]) for n in ("c_smx", "c_ssum"))

    transposed = rms_input(c, h, junk, n2, vec["norm1_w_2"], normed)
    wait(T, transposed)
    softplus8(c, vec["rg_lambda_2"][:, :], lam8[:, :], nlam8[:, :], [t[:, :] for t in ltmp])

    wait(A, (s_kw, 16))
    kw_hi = act(A.activation(kw[0][:, :, :], kw_raw[:, :, :], ACT.Copy))
    wait(V, kw_hi)
    kw_in = dve(V.tensor_tensor(kw[1][:, :, :], kw_raw[:, :, :], kw[0][:, :, :].bitcast(F32), ALU.subtract))
    wait(T, *everything())
    drained = {}
    for b, name in enumerate(("q", "q", "kv", "iq")):
        block = [ps[:, 2 * (b % 2) + t, :] for t in range(NT)]
        if b >= 2:
            wait(T, *drained[b - 2])
        for half in range(2):
            j = 2 * b + half
            c.load(j, d["w_qkvi"][b, half])
            c.split(j + AHEAD)
            done = c.token_major(j, c.xT, 4 * half, 4, 512, block, half == 0, half == 1)
        wait(A, done)
        wait(V, done)
        for t in range(NT):
            copy = (lambda o, i: act(A.activation(o, i, ACT.Copy))) if t == 0 else (lambda o, i: dve(V.tensor_copy(o, i)))
            if name == "q":
                copy(qk[:, t, b * 512:(b + 1) * 512], block[t])
            elif name == "kv":
                copy(qk[:, t, D:D + 256], block[t][:, 0:256])
                copy(v[:, t, :], block[t][:, 256:512])
            else:
                copy(iq[:, t, :], block[t])
        drained[b] = (act.now(), dve.now())
    c.advance(8)
    for k in range(KD):
        for t in range(NT):
            x = tuple(z[:, k, t * P:(t + 1) * P] for z in c.xT)
            m = c.mm3(ps[:, 4 + t, 0:2 * ID + IH], x, tuple(z[:, k, :] for z in kw), k == 0, k == KD - 1)
    done = pe(m)
    wait(A, done)
    for t in range(NT):
        ikw_in = act(A.activation(ikw[:, t, :], ps[:, 4 + t, 0:2 * ID + IH], ACT.Copy))

    wait(A, *drained[3], ikw_in)
    for t in range(NT):
        A.activation(junk[:, t, :], qk[:, t, 0:D], ACT.Square)
    A.activation(h[:, :, 0:256], qk[:, :, D:D + 256], ACT.Square)
    squared = act(A.activation(h[:, :, 256:256 + ID], ikw[:, :, 0:ID], ACT.Square))
    wait(V, squared)
    for t in range(NT):
        V.reduce_sum(hs[:, t, 0:HC], junk[:, t, :].rearrange("p (h n) -> p h n", n=DC), AX.X)
        a = dve(V.reduce_sum(hs[:, t, HC:NH], h[:, t, 0:256 + ID].rearrange("p (h n) -> p h n", n=DC), AX.X))
    flat = lambda t: t[:, :, :].rearrange("p t n -> p (t n)")
    wait(V, a)
    r = rsqrt(c, flat(hs), flat(hr), 1e-6, (flat(ht0), flat(ht1)), 1.0 / DC)
    wait(V, r)
    wait(G, r)
    for t, (eng, sig) in enumerate(((V, dve), (G, pool))):
        x = qk[:, t, :].rearrange("p (h n) -> p h n", n=DC)
        sig(eng.tensor_tensor(x, x, hr[:, t, 0:HC + HKV].unsqueeze(2).broadcast_to([P, HC + HKV, DC]), ALU.mult))
    for t in range(NT):
        V.tensor_scalar(ikw[:, t, 0:2 * ID], ikw[:, t, 0:2 * ID], hr[:, t, NH - 1:NH], None, ALU.mult)
    V.memset(kz[:, :, :], 0.0)
    dve(V.memset(ikz[:, :, :], 0.0))
    heads = everything()

    cw, cb = vec["conv_w_2"], vec["conv_b_2"]

    def conv(n, bank, done, j):
        wait(A, done)
        for k in range(2):
            tile = 2 * n + k
            first = act(A.activation(xc[:, tile, :], bank[:, k, :], ACT.Identity, bias=cb[:, tile:tile + 1],
                                     scale=cw[:, 24 + tile:25 + tile]))
        wait(V, first)
        for s in (1, 2, 3):
            for k in range(2):
                tile = 2 * n + k
                a = dve(V.scalar_tensor_tensor(xc[:, tile, s:S], bank[:, k, 0:S - s], cw[:, (3 - s) * 8 + tile:(3 - s) * 8 + tile + 1],
                                               xc[:, tile, s:S], ALU.mult, ALU.add))
            if s < 3:
                wait(V, a)

    wait(A, *heads)
    feature_stage(c, None, 1, lambda n: d["w_rnn"][n], c.xT, (0, 1, 2, 3), conv, dve, 6)
    conv_in = dve.now()

    hn = vec["head_norms"]
    wait(T, *heads)
    jobs = [("iq", 0), ("iq", 2), ("ik", 0), ("k", 0)] + [("q", n) for n in range(0, KD, 2)]
    free = {}
    for n, (name, t0) in enumerate(jobs):
        b = ps[:, 4 + n % 4, :]
        if n >= 4:
            wait(T, free[n - 4])
        for k in range(1 if name == "ik" else 2):
            for t in range(NT):
                src = {"q": lambda: qk[:, t, (t0 + k) * P:(t0 + k + 1) * P], "k": lambda: qk[:, t, D + k * P:D + (k + 1) * P],
                       "iq": lambda: iq[:, t, (t0 + k) * P:(t0 + k + 1) * P], "ik": lambda: ikw[:, t, 0:P]}[name]()
                m = T.transpose(b[:, (2 * k + t) * P:(2 * k + t + 1) * P], src, c.ident[:, :])
        turned = pe(m)
        wait(A, turned)
        if name == "q":
            free[n] = act(A.activation(qT[:, t0:t0 + 2, :], pair(b), ACT.Copy, scale=hn[:, 0:1]))
        elif name == "iq":
            free[n] = act(A.activation(iqT[:, t0:t0 + 2, :], pair(b), ACT.Copy))
        elif name == "k":
            for g in range(HKV):
                rows = slice(64 * (g % 2), 64 * (g % 2) + 64)
                free[n] = act(A.activation(kz[rows, g, :], b[rows, (g // 2) * S:(g // 2 + 1) * S], ACT.Copy, scale=hn[rows, 1:2]))
        else:
            for g in range(2):
                rows = slice(64 * g, 64 * g + 64)
                free[n] = act(A.activation(ikz[rows, g, :], b[rows, 0:S], ACT.Copy, scale=hn[rows, 2:3]))
    turned_in = act.now()

    wait(T, turned_in)
    wait(A, pe.now())
    read, acc = {}, {}
    for hd in range(IH):
        b = ps[:, 4 + hd % 4, :]
        if hd >= 4:
            wait(T, read[hd - 4])
        for q, cols in enumerate(QCOLS):
            m = T.matmul(b[:, cols], iqT[:, hd // 2, q * P:(q + 1) * P], ikz[:, hd % 2, 0:(q + 1) * P], start=q == 0,
                         stop=True, skip_group_check=True)
        scored = pe(m)
        wait(A, scored)
        if hd >= 2:
            wait(A, acc[hd - 2])
        read[hd] = act(A.activation(rl[:, hd % 2, :], b[:, 0:3 * P], ACT.Relu))
        wait(V, read[hd])
        if hd:
            wait(V, acc[hd - 1])
        for q, cols in enumerate(QCOLS):
            o, w = isc[:, q, 0:(q + 1) * P], ikw[:, q, 2 * ID + hd:2 * ID + hd + 1]
            if hd == 0:
                acc[hd] = dve(V.tensor_scalar(o, rl[:, 0, cols], w, None, ALU.mult))
            else:
                acc[hd] = dve(V.scalar_tensor_tensor(o, rl[:, hd % 2, cols], w, o, ALU.mult, ALU.add))

    wait(T, conv_in, act.now(), (s_rgw, 16))
    wait(A, turned_in, pe.now())
    gate_read = {}
    for n in range(KD):
        b = ps[:, n % 4, :]
        if n >= 4:
            wait(T, gate_read[n - 4])
        T.matmul(b[:, 0:S], rgw[:, 0, n, :], xc[:, n, :], start=True, stop=True, skip_group_check=True)
        gated = pe(T.matmul(b[:, S:2 * S], rgw[:, 1, n, :], xc[:, n, :], start=False, stop=True, skip_group_check=True))
        wait(A, gated)
        A.activation(rr[:, n, :], b[:, 0:S], ACT.Sigmoid, bias=vec["rg_ba_2"][:, n:n + 1])
        gate_read[n] = act(A.activation(ig[:, n, :], b[:, S:2 * S], ACT.Sigmoid, bias=vec["rg_bx_2"][:, n:n + 1]))

    done_ = {}

    def selection():
        widths = [(q, (q + 1) * P) for q in range(NT)]
        wait(V, acc[IH - 1])
        for q, n in widths:
            a = dve(V.tensor_scalar(isc[:, q, 0:n], isc[:, q, 0:n], IDX_SCALE, None, ALU.mult))
        wait(V, a)
        for q, n in widths:
            V.memset(isc[0:CH, q, n - CH:n], -1.0e30)
        a = dve(V.memset(ones[:, :], 1.0))
        for step in range(TOPK // 8):
            src = isc if step == 0 else wk
            wait(V, a)
            for q, n in widths:
                a = dve(V.max(m8[:, q, :], src[:, q, 0:n]))
            yield
            if step < TOPK // 8 - 1:
                wait(V, a)
                for q, n in widths:
                    a = dve(V.match_replace(out=wk[:, q, 0:n], in_to_replace=m8[:, q, :], in_values=src[:, q, 0:n],
                                            imm_value=-3.0e38))
                yield
        wait(V, a)
        for q, n in widths:
            V.tensor_scalar(eqs[:, q, 0:n], isc[:, q, 0:n], m8[:, q, 7:8], None, ALU.is_equal)
            a = dve(V.tensor_scalar(wk[:, q, 0:n], isc[:, q, 0:n], m8[:, q, 7:8], None, ALU.is_gt, ALU.add,
                                    accum_out=cnt[:, q:q + 1]))
        wait(V, a)
        dve(V.tensor_scalar(cnt[:, :], cnt[:, :], -1.0, float(TOPK), ALU.mult, ALU.add))
        for q, n in widths:
            a = dve(V.tensor_tensor_scan(cum[:, q, 0:n], ones[:, 0:n], eqs[:, q, 0:n], 0.0, ALU.mult, ALU.add))
        yield
        wait(V, a)
        for q, n in widths:
            a = dve(V.scalar_tensor_tensor(eqs[:, q, 0:n], cum[:, q, 0:n], cnt[:, q:q + 1], eqs[:, q, 0:n],
                                           ALU.is_le, ALU.mult))
        wait(V, a)
        for q, n in widths:
            a = dve(V.tensor_tensor(wk[:, q, 0:n], wk[:, q, 0:n], eqs[:, q, 0:n], ALU.add))
        wait(V, a)
        for q, n in widths:
            done_["selected"] = dve(V.tensor_scalar(isc[:, q, 0:n], wk[:, q, 0:n], 1.0e30, -1.0e30, ALU.mult, ALU.add))
        yield

    def recurrence():
        wait(A, gate_read[KD - 1])
        for n in range(KD):
            exps = act(A.activation(aa[:, n, :], rr[:, n, :], ACT.Exp, scale=nlam8[:, n:n + 1]))
        wait(A, exps)
        for n in range(KD):
            tanhs = act(A.activation(rr[:, n, :], rr[:, n, :], ACT.Tanh, scale=lam8[:, n:n + 1]))
        wait(G, gate_read[KD - 1], conv_in)
        ix = pool(G.tensor_tensor(ig[:, :, :], ig[:, :, :], xc[:, :, :], ALU.mult))
        gates_done = pe.now()
        yield
        for half in range(2):
            tiles = slice(4 * half, 4 * half + 4)
            wait(V, tanhs, ix, gates_done)
            a = dve(V.tensor_scalar(xc[:, tiles, :], rr[:, tiles, :], 1.0, None, ALU.add))
            wait(V, a)
            a = dve(V.reciprocal(xc[:, tiles, :], xc[:, tiles, :]))
            wait(V, a)
            a = dve(V.tensor_tensor(rr[:, tiles, :], rr[:, tiles, :], xc[:, tiles, :], ALU.mult))
            wait(A, a)
            root = act(A.activation(rr[:, tiles, :], rr[:, tiles, :], ACT.Sqrt, scale=2.0))
            wait(G, root)
            u = pool(G.tensor_tensor(ig[:, tiles, :], ig[:, tiles, :], rr[:, tiles, :], ALU.mult))
            yield
        wait(V, u, exps)
        for n in range(KD):
            scanned = dve(V.tensor_tensor_scan(rr[:, n, :], aa[:, n, :], ig[:, n, :], 0.0, ALU.mult, ALU.add))
            if n % 2:
                yield
        done_["scanned"] = scanned
        wait(G, scanned, done_["gelu"])
        y = pool(G.tensor_tensor(gel[:, :, :], rr[:, :, :], gel[:, :, :], ALU.mult))
        yield
        wait(A, y, scanned)
        rounded = act(A.activation(yT[0][:, :, :], gel[:, :, :], ACT.Copy))
        yield
        wait(V, rounded)
        done_["y"] = dve(V.tensor_tensor(yT[1][:, :, :], gel[:, :, :], yT[0][:, :, :].bitcast(F32), ALU.subtract))
        yield

    def scores(g):
        wait(T, *done_.get("scores_free", ()), *done_.get("pT_banks_free", ()))
        for r in range(4):
            tile = 4 * (g // 2) + r
            T.matmul(ps[:, 4, r * P:(r + 1) * P], qT[:, tile, 0:P], kz[:, g, 0:P], start=r == 0, stop=True,
                     skip_group_check=True)
            m = T.matmul(ps[:, 5 + r // 2, (r % 2) * S:(r % 2 + 1) * S], qT[:, tile, P:2 * P], kz[:, g, :], start=r % 2 == 0,
                         stop=True, skip_group_check=True)
        scored = pe(m)
        wait(V, scored, done_["selected"], *done_.get("p_free", ()))
        q0, q1 = p[:, :, 0:P], p[:, :, P:3 * P]
        bias = lambda q, n, heads: isc[:, q:q + 1, 0:n].broadcast_to([P, heads, n])
        dve(V.scalar_tensor_tensor(q0, ps[:, 4, :].rearrange("p (r n) -> p r n", r=4), SCALE_C, bias(0, P, 4),
                                   ALU.mult, ALU.add))
        for half in range(2):
            a = dve(V.scalar_tensor_tensor(q1[:, 2 * half:2 * half + 2, :], pair(ps[:, 5 + half, :]), SCALE_C,
                                           bias(1, S, 2), ALU.mult, ALU.add))
        done_["scores_free"] = (a,)
        wait(V, a)
        V.tensor_reduce(smx[:, 0, :], q0, AX.X, ALU.max)
        a = dve(V.tensor_reduce(smx[:, 1, :], q1, AX.X, ALU.max))
        wait(V, a)
        a = dve(V.tensor_scalar(smx[:, :, :], smx[:, :, :], -1.0, None, ALU.mult))
        wait(A, a, *done_.get("ssum_free", ()))
        for r in range(4):
            for q, cols in enumerate(QCOLS):
                a = act(A.activation(p[:, r, cols], p[:, r, cols], ACT.Exp, bias=smx[:, q, r:r + 1],
                                     accum_out=ssum[:, q, r:r + 1]))
        done_["p"] = a

    def turn(g):
        for r in range(4):
            b = ps[:, 4 + r % 3, :]
            wait(T, done_["p"], *done_["scores_free"])
            if r == 3:
                wait(T, *done_["first_pT"])
            for n in range(3):
                m = T.transpose(b[:, n * P:(n + 1) * P], p[:, r, n * P:(n + 1) * P], c.ident[:, :])
            turned = pe(m)
            wait(A, turned, *done_.get("pT_free", ()))
            a = act(A.activation(pT[:, r, :], b[:, 0:3 * P], ACT.Copy))
            if r == 0:
                done_["first_pT"] = (a,)
        done_["p_free"] = (turned,)
        done_["pT_banks_free"] = done_["pT"] = (a,)

    def values(g):
        wait(T, *done_["pT"], *done_.get("o_free", ()))
        for q in range(NT):
            for r in range(4):
                o = ps[:, 7, (4 * q + r) * DC:(4 * q + r + 1) * DC]
                for k in range(q + 1):
                    m = T.matmul(o, pT[:, r, (q + k) * P:(q + k + 1) * P], v[:, k, g * DC:(g + 1) * DC],
                                 start=q == 0 and r == 0, stop=k == q, skip_group_check=True)
        done = pe(m)
        done_["pT_free"] = (done,)
        wait(V, done_["p"])
        a = dve(V.reciprocal(smx[:, :, :], ssum[:, :, :]))
        wait(V, a, done)
        done_["ssum_free"] = (a,)
        for q in range(NT):
            a = dve(V.tensor_tensor(ya[:, q, g * 4 * DC:(g + 1) * 4 * DC].rearrange("p (r n) -> p r n", r=4),
                                    ps[:, 7, 4 * q * DC:4 * (q + 1) * DC].rearrange("p (r n) -> p r n", r=4),
                                    smx[:, q, :].unsqueeze(2).broadcast_to([P, 4, DC]), ALU.mult))
        done_["o_free"] = (a,)

    background = [selection(), recurrence()]

    def steps(n):
        while n and background:
            if next(background[0], "end") == "end":
                background.pop(0)
            n -= 1

    def finish(n):
        while len(background) > n:
            steps(1)

    gb = vec["gate_b_2"]
    wait(T, *everything())
    wait(A, conv_in)
    bank_free = {}
    for n in range(16):
        kind, t0 = n // 4, 2 * (n % 4)
        c.load(n, (d["w_rnn"][4 + n] if kind == 0 else d["w_gates"][n - 4] if kind < 3 else d["w_o_rnn"][n - 12]))
        c.split(n + AHEAD)
        steps(4)
        if n == 7:
            finish(0)
        if kind == 3:
            wait(T, done_["y"])
        bank = ps[:, n % 4, :]
        if n >= 4:
            wait(T, *bank_free[n - 4])
        done = c.feature_major(n, yT if kind == 3 else c.xT, 0, KD, S, HALVES(bank), True, True)
        if kind == 0:
            wait(A, done)
            a = act(A.activation(gel[:, t0:t0 + 2, :], pair(bank), ACT.Gelu_apprx_tanh))
            done_["gelu"] = a
        elif kind < 3:
            wait(A, done)
            for k in range(2):
                a = act(A.activation((g0, g1)[kind - 1][:, t0 + k, :], bank[:, k * S:(k + 1) * S], ACT.Sigmoid,
                                     bias=gb[:, 8 * (kind - 1) + t0 + k:8 * (kind - 1) + t0 + k + 1]))
        else:
            wait(V, done, act.now())
            a = dve(V.tensor_tensor(g0[:, t0:t0 + 2, :], pair(bank), g0[:, t0:t0 + 2, :], ALU.mult))
        bank_free[n] = (a,)
        if n >= 9 and n % 2:
            values((n - 9) // 2)
        if 7 <= n < 15 and n % 2:
            scores((n - 7) // 2)
        if n >= 8 and n % 2 == 0:
            turn((n - 8) // 2)
    c.advance(16)

    wait(A, c.w_used_now())
    wait(V, c.w_used_now())
    turned = transpose_in(c, lambda t, k: ya[:, t, k * P:(k + 1) * P], KD, whole(zT[0]), whole(zT[1]), everything())
    wait(T, turned)

    def mix(n, bank, done, j):
        t = slice(2 * n, 2 * n + 2)
        wait(V, done)
        a = dve(V.tensor_tensor(g1[:, t, :], bank, g1[:, t, :], ALU.mult))
        wait(G, a)
        a = pool(G.tensor_tensor(g0[:, t, :], g0[:, t, :], g1[:, t, :], ALU.add))
        wait(A, a)
        a = act(A.activation(c.xT[0][:, t, :], g0[:, t, :], ACT.Copy))
        wait(G, a)
        pool(G.tensor_tensor(c.xT[1][:, t, :], g0[:, t, :], c.xT[0][:, t, :].bitcast(F32), ALU.subtract))

    feature_stage(c, None, 1, lambda n: d["w_o_attn"][n], zT, (0, 1, 2, 3), mix, dve)

    wait(T, *everything())
    for b in range(2):
        block = [ps[:, 4 + 2 * b + t, :] for t in range(NT)]
        for half in range(2):
            j = 2 * b + half
            c.load(j, d["w_out"][b, half])
            c.split(j + AHEAD)
            done = c.token_major(j, c.xT, 4 * half, 4, 512, block, half == 0, half == 1)
        wait(V, done)
        for t in range(NT):
            r = c.res[:, t, b * 512:(b + 1) * 512]
            a = dve(V.tensor_tensor(r, r, block[t], ALU.add))
    c.advance(4)

    wait(V, *everything())
    transposed = rms_input(c, h2, junk2, n2, vec["norm2_w_2"], everything())
    wait(T, transposed)
    wait(A, pe.now(), dve.now())

    def relu2(n, bank, done, j):
        at = bass.ds(n * 2, 2)
        wait(A, done, pool.now(3))
        relu = act(A.activation(fr[:, j, :, :], bank, ACT.Relu))
        wait(V, relu)
        square = dve(V.tensor_tensor(fr[:, j, :, :], fr[:, j, :, :], fr[:, j, :, :], ALU.mult))
        wait(A, square)
        hi = act(A.activation(fT[0][:, at, :], fr[:, j, :, :], ACT.Copy))
        wait(G, hi)
        pool(G.tensor_tensor(fT[1][:, at, :], fr[:, j, :, :], fT[0][:, at, :].bitcast(F32), ALU.subtract))

    feature_stage(c, "feed_forward", 4, lambda n: d["w_ff_in"][bass.ds(n, 1)], c.xT, (0, 1, 2, 3), relu2, act, 2)

    wait(T, *everything())
    c.last_unit = 16
    for b in range(2):
        block = [ps[:, 4 + 2 * b + t, :] for t in range(NT)]
        for q in range(8):
            j = 8 * b + q
            c.load(j, d["w_ff_out"][b, q])
            c.split(j + AHEAD)
            done = c.token_major(j, fT, 4 * q, 4, 512, block, q == 0, q == 7)
        wait(V, done)
        for t in range(NT):
            r = c.res[:, t, b * 512:(b + 1) * 512]
            a = dve(V.tensor_tensor(r, r, block[t], ALU.add))
        wait(c.G, a)
        c.G.dma_start(out[0].rearrange("(t p) n -> p t n", p=P)[:, :, b * 512:(b + 1) * 512],
                       c.res[:, :, b * 512:(b + 1) * 512]).then_inc(c.s_out, 16)
    c.G.wait_ge(c.s_out, 32)


LOOPS = {
    "retention": dict(pe=8, dve=38, act=16, pool=4),
        "feed_forward": dict(pe=0, dve=4, act=8, pool=4),
    "attention": dict(pe=14, dve=32, act=20, pool=6),
}


def build(nc, d, out, stop=None):
    c = Core(nc)
    c.ps = nc.alloc_psum_tensor("ps", [P, 8, 512], F32)
    c.raw = [c.place(f"w_raw{r}", [P, SLOT]) for r in range(RING)]
    c.hi = c.place("w_hi_ring", [P, RING, SLOT], F32R)
    c.lo = c.place("w_lo_ring", [P, RING, SLOT], F32R)
    c.res = c.place("res", [P, NT, D])
    c.xT = [c.place("xT_hi", [P, KD, S], F32R), c.place("xT_lo", [P, KD, S], F32R)]
    c.st = c.place("st", [P, NT, 2, 6])
    c.mv = c.place("mv", [P, NT, 2])
    norms = c.place("norms", [P, 3, NT])
    c.rs, c.tmp = norms[:, 0, :], [norms[:, 1 + n, :] for n in range(2)]
    c.s_x, c.s_out = (nc.alloc_semaphore(n) for n in ("s_x", "s_out"))

    c.A.dma_start(c.res[:, :, :], d["x"][0].rearrange("(t p) n -> p t n", p=P)).then_inc(c.s_x, 16)
    c.ident, t_ident = table(c, c.A, "ident", d["k_ident"], [P, P])
    wait(c.T, (c.s_x, 16), t_ident)
    wait(c.V, (c.s_x, 16))
    c.phase = c.top
    transposed = transpose_in(c, lambda t, k: c.res[:, t, k * P:(k + 1) * P], KD, whole(c.xT[0]), whole(c.xT[1]), ())
    for j in range(AHEAD):
        c.split(j)
    wait(c.T, transposed)
    oT = retention_layer(c, d)
    lnw = load_ln(c, 0, d, c.top, ())
    c.last_unit = 8 if stop == 1 else None
    added = out_projection(c, d["a_w_out"], oT, ALPHA, "a")
    normed = layer_norm(c, 0, d, lnw, (added,))
    if stop == 1:
        return store(c, out, normed)
    transposed = transpose_in(c, lambda t, k: c.res[:, t, k * P:(k + 1) * P], KD, whole(c.xT[0]), whole(c.xT[1]), normed)
    wait(c.T, transposed)
    oT = latent_attention_layer(c, d)
    lnw = load_ln(c, 1, d, c.ln_at, (c.pe.now(),))
    c.last_unit = 8 if stop == 2 else None
    added = out_projection(c, d["b_w_out"], oT, ALPHA, "b")
    normed = layer_norm(c, 1, d, lnw, (added,))
    if stop == 2:
        return store(c, out, normed)
    hybrid_layer(c, d, out, normed)


def store(c, out, after):
    wait(c.SP, *after)
    c.SP.dma_start(out[0].rearrange("(t p) n -> p t n", p=P), c.res[:, :, :]).then_inc(c.s_out, 16)
    c.SP.wait_ge(c.s_out, 16)


COLUMNS = ("b_q_norm", "kv_norm", "norm1_w_2", "rg_ba_2", "rg_bx_2", "rg_lambda_2", "conv_b_2", "gate_b_2", "norm2_w_2")


def units(w, k, n):
    K, N = w.shape
    w = w.reshape(K // (P * k), k, P, N // n, n).transpose(3, 0, 2, 1, 4)
    return np.ascontiguousarray(w).reshape(N // n, K // (P * k), P, k * n)


def layout(inputs):
    out = {name: np.asarray(a) for name, a in inputs.items()}
    for name in COLUMNS:
        out[name] = np.ascontiguousarray(out[name].reshape(-1, P).T)
    w = out["a_w_in"][0]
    at = np.cumsum([HA * DKA, HA * DKA, WA])
    q, k, v, g = np.split(w, at, 1)
    out["a_w_in"] = np.concatenate([units(q, KD, DKA), units(k, KD, DKA), units(v, 4, DVA), units(g, 4, DVA)], 1)
    out["a_w_out"] = units(out["a_w_out"][0], 4, 512)
    w = out.pop("b_w_in")[0]
    out["b_w_qlat"] = units(w[:, :QL], 4, 384)
    out["b_w_gate"] = units(w[:, QL:], KD, 2 * VH)[:, 0]
    w = out["kv_w_down"]
    out["kv_w_down"] = units(np.concatenate([w, w[:, KVL:]], 1), 2, KVL + 2 * ROPE)
    w = out["b_w_uq"][0].reshape(QL, HB // 2, 2, NOPE + ROPE)
    w = np.concatenate([w[..., :NOPE].reshape(QL, HB // 2, -1), w[..., NOPE:].reshape(QL, HB // 2, -1)], 2)
    out["b_w_uq"] = units(w.reshape(QL, -1), 3, 2 * (NOPE + ROPE))
    w = out["kv_w_up"].reshape(KVL, HB // 2, 2, NOPE + VH)
    w = np.concatenate([w[..., :NOPE].reshape(KVL, HB // 2, -1), w[..., NOPE:].reshape(KVL, HB // 2, -1)], 2)
    out["kv_w_up"] = units(w.reshape(KVL, -1), 4, 512)[:, 0]
    out["b_w_out"] = units(out["b_w_out"][0], 4, 512)

    w = out.pop("w_in_2")[0]
    rnn_x, rnn_g, q, k, v, iq, ik, iw, gates = np.split(w, np.cumsum([DR, DR, D, 256, 256, IH * ID, ID, IH]), 1)
    group = HC // HKV
    order = [(t // group * 2 + half) * group + t % group for t in range(HC // 2) for half in range(2)]
    q = q.reshape(D, HC, DC)[:, order].reshape(D, D)
    out["w_qkvi"] = units(np.concatenate([q, k, v, iq], 1), 4, 512)
    out["w_ikw"] = units(np.concatenate([ik, ik, iw], 1), KD, 2 * ID + IH)[0, 0]
    out["w_rnn"] = units(np.concatenate([rnn_x, rnn_g], 1), KD, S)[:, 0]
    out["w_gates"] = units(gates, KD, S)[:, 0]
    for name in ("w_o_rnn", "w_o_attn"):
        out[name] = units(out.pop(name + "_2")[0], KD, S)[:, 0]
    out["w_out"] = units(out.pop("w_out_2")[0], 4, 512)
    out["w_ff_in"] = units(out.pop("w_ff_in_2")[0], KD, S)[:, 0]
    out["w_ff_out"] = units(out.pop("w_ff_out_2")[0], 4, 512)
    out["conv_w_2"] = np.ascontiguousarray(out["conv_w_2"][0].reshape(4, KD, P).transpose(2, 0, 1)).reshape(P, 4 * KD)
    norms = [np.tile(out.pop(n)[0], 2) for n in ("q_norm_w_2", "k_norm_w_2", "idx_k_norm_w_2")]
    out["head_norms"] = np.ascontiguousarray(np.stack(norms, 1))
    wa, wx = out.pop("rg_wa_2")[0], out.pop("rg_wx_2")[0]
    rg = np.zeros((P, 2, KD, P), wa.dtype)
    for n, w in enumerate((wa, wx)):
        for half in range(2):
            rows = slice(64 * half, 64 * half + 64)
            rg[rows, n, :, rows] = w[half::2].transpose(1, 0, 2)
    out["rg_w"] = rg.reshape(P, -1)
    return out


def rope_angles(dim):
    f = np.float32
    inv = (f(10000.0) ** (-np.arange(dim // 2, dtype=f) / f(dim // 2))).astype(f)
    return np.arange(S, dtype=f)[None, :] * inv[:, None]


def constants():
    f = np.float32
    ang = rope_angles(DKA)
    out = {"k_ident": np.eye(P, dtype=f), "k_ropeA": np.stack([np.cos(ang), np.sin(ang)], 1).astype(f)}
    lg = np.log1p(-np.exp2(-5.0 - np.arange(HA)))
    e, n = np.arange(P)[:, None], np.arange(S)[None, :]
    m = np.where(n >= e, np.exp(np.maximum(n - e, 0)[None] * lg[:, None, None]), 0.0) / np.sqrt(DKA)
    m = np.concatenate([m, m[:, :, 0:P]], 2)
    out["k_decay"] = np.ascontiguousarray(m.transpose(1, 0, 2)).astype(f)
    ang = np.tile(rope_angles(ROPE), (2 * P // ROPE, 1))
    out["k_ropeB"] = np.stack([np.cos(ang), np.sin(ang)], 1).astype(f)
    rot = np.zeros((P, P), f)
    for r in range(P):
        half = ROPE // 2
        if r % ROPE < half:
            rot[r + half, r] = -1.0
        else:
            rot[r - half, r] = 1.0
    out["k_rotB"] = rot
    causal = np.where(np.arange(P)[None, :] <= np.arange(P)[:, None], 0.0, -1.0e30).astype(f)
    out["k_maskB"] = np.concatenate([causal, np.zeros((P, P), f), causal], 1)
    return out


def kernel(**inputs):
    import concourse.bacc as bacc
    from concourse.bass_utils import run_bass_kernel_spmd

    arrays = {**layout(inputs), **constants()}
    nc = bacc.Bacc("TRN2", target_bir_lowering=False, num_devices=1)
    d = {n: nc.dram_tensor("in_" + n, a.shape, mybir.dt.from_np(a.dtype), kind="ExternalInput").ap()
         for n, a in arrays.items()}
    out = nc.dram_tensor("out", (1, S, D), F32, kind="ExternalOutput").ap()
    build(nc, d, out)
    r = run_bass_kernel_spmd(nc, [{"in_" + n: a for n, a in arrays.items()}], core_ids=[0])
    return r.results[0]["out"]
```

```python
import numpy as np
import concourse.bass as bass
from concourse import mybir

F32 = mybir.dt.float32
F32R = mybir.dt.float32r
ACT = mybir.ActivationFunctionType
ALU = mybir.AluOpType
AX = mybir.AxisListType

P = 128
D = 1024
S = 256
NT = S // P
KD = D // P

HA, DKA, DVA = 4, 256, 512
WA = HA * DVA
HB, NOPE, ROPE, VH = 16, 128, 64, 128
QL, KVL = 768, 512
WB = HB * VH
SCALE_B = float(NOPE + ROPE) ** -0.5
ALPHA = 4.0 ** 0.25
DR, HC, HKV, DC = 1024, 16, 4, 64
IH, ID = 8, 64
TOPK = 64
CH = 64
DFF = 4096
SCALE_C = float(DC) ** -0.5
IDX_SCALE = (float(ID) ** -0.5) * (float(IH) ** -0.5)

RING = 4
SLOT = 2048
AHEAD = 3


class Signal:

    FIRST = 64

    def __init__(self, nc, name, engine):
        self.sem = nc.alloc_semaphore(name)
        engine.sem_inc(self.sem, self.FIRST)
        self.base, self.i, self.per, self.k, self.serial = self.FIRST, 0, 0, 0, 0

    def __call__(self, instruction):
        instruction.then_inc(self.sem, 1)
        self.k += 1
        self.serial += 1
        return self.now()

    def now(self, back=0):
        return (self.sem, self.base + self.i * self.per + (self.k - back), self, self.serial - back)

    def enter(self, i, per):
        self.base, self.k = self.base + self.k, 0
        self.i, self.per = i, per

    def leave(self, count):
        if self.k != self.per:
            raise ValueError(f"a loop's body signals {self.k}, {self.per} were declared")
        self.base, self.i, self.per, self.k = self.base + count * self.per, 0, 0, 0


def wait(engine, *tokens):
    for token in tokens:
        engine.wait_ge(token[0], token[1])


class Core:

    def __init__(self, nc):
        self.nc = nc
        self.T, self.V, self.A, self.G, self.SP = nc.tensor, nc.vector, nc.scalar, nc.gpsimd, nc.sync
        self.pe, self.dve, self.act, self.pool = (
            Signal(nc, n, e) for n, e in (("pe", self.T), ("dve", self.V), ("act", self.A), ("pool", self.G)))
        self.landed = [nc.alloc_semaphore(f"w_landed{r}") for r in range(RING)]
        self.w_hi, self.w_lo, self.w_used = (nc.alloc_semaphore(n) for n in ("w_hi", "w_lo", "w_used"))
        self.unit0, self.it, self.upi = 0, 0, 0
        self.V.sem_inc(self.w_lo, RING)
        self.T.sem_inc(self.w_used, RING)
        self.last_unit = None
        self.top = (nc.sbuf_base + 31) // 32 * 32
        self.at = {}

    def place(self, name, shape, dtype=F32, at=None):
        at = self.top if at is None else at
        size = int(np.prod(shape[1:])) * 4
        t = self.nc.alloc_sbuf_tensor_at(name, shape, dtype, offset=at)
        self.top = at + (size + 31) // 32 * 32
        if self.top > self.nc.sbuf_usable_end:
            raise ValueError(f"{name} ends {self.top - self.nc.sbuf_usable_end} bytes after the SBUF")
        self.at[name] = at
        return t

    def loop(self, name, count, upi):
        return _Loop(self, name, count, upi)

    def unit(self, j):
        return self.unit0 + self.it * self.upi + j

    def load(self, j, src):
        slot = j % RING
        if len(src.shape) == 3:
            src = src.rearrange("a p n -> (a p) n")
        self.SP.wait_ge(self.w_lo, self.unit(j) + 1)
        self.SP.dma_start(self.raw[slot][:, 0:src.shape[-1]], src).then_inc(self.landed[slot], 16)

    def split(self, j):
        if self.last_unit is not None and j >= self.last_unit:
            return
        slot = j % RING
        u = self.unit(j)
        self.A.wait_ge(self.landed[slot], 16 * (self.unit0 // RING + 1 + j // RING) + self.it * (16 * (self.upi // RING)))
        self.A.wait_ge(self.w_used, u + 1)
        self.A.activation(self.hi[:, slot, :], self.raw[slot][:, :], ACT.Copy).then_inc(self.w_hi, 1)
        self.V.wait_ge(self.w_hi, u + 1)
        self.V.tensor_tensor(self.lo[:, slot, :], self.raw[slot][:, :], self.hi[:, slot, :].bitcast(F32),
                             ALU.subtract).then_inc(self.w_lo, 1)

    def advance(self, units):
        self.unit0 += units

    def used(self, j):
        return (self.w_used, RING + self.unit(j) + 1)

    def w_used_now(self):
        return (self.w_used, RING + self.unit(0))

    def use(self, j):
        self.T.wait_ge(self.w_lo, RING + self.unit(j) + 1)
        return self.hi[:, j % RING, :], self.lo[:, j % RING, :]

    def mm3(self, out, lhs, rhs, start, stop, used=False):
        (lh, ll), (rh, rl) = lhs, rhs
        self.T.matmul(out, lh, rh, start=start, stop=False, skip_group_check=True)
        self.T.matmul(out, lh, rl, start=False, stop=False, skip_group_check=True)
        m = self.T.matmul(out, ll, rh, start=False, stop=stop, skip_group_check=True)
        return m

    def token_major(self, j, xT, k0, nk, cols, outs, first, last, ready=()):
        wh, wl = (w.rearrange("p (k n) -> p k n", k=nk) if nk * cols == SLOT
                  else w[:, 0:nk * cols].rearrange("p (k n) -> p k n", k=nk) for w in self.use(j))
        for k in range(nk):
            if ready and k % 2 == 0:
                wait(self.T, ready[(k0 + k) // 2])
            for t in range(NT):
                x = tuple(z[:, k0 + k, t * P:(t + 1) * P] for z in xT)
                m = self.mm3(outs[t], x, (wh[:, k, :], wl[:, k, :]), first and k == 0, last and k == nk - 1)
        m.then_inc(self.w_used, 1)
        return self.used(j)

    def feature_major(self, j, xT, k0, nk, cols, outs, first, last, ready=()):
        wh, wl = (w[:, 0:nk * cols].rearrange("p (k n) -> p k n", k=nk) for w in self.use(j))
        for part in (range(0, nk // 2), range(nk // 2, nk)):
            for c, out in enumerate(outs):
                for k in part:
                    if ready and c == 0 and k % 2 == 0:
                        wait(self.T, ready[(k0 + k) // 2])
                    w = tuple(z[:, k, c * P:(c + 1) * P] for z in (wh, wl))
                    x = tuple(z[:, k0 + k, :] for z in xT)
                    m = self.mm3(out, w, x, first and k == 0 and c % 2 == 0, last and k == nk - 1)
        m.then_inc(self.w_used, 1)
        return self.used(j)


class _Loop:
    def __init__(self, core, name, count, upi):
        self.c, self.name, self.count, self.upi, self.per = core, name, count, upi, LOOPS[name]
        nc = core.nc
        engines = [e.engine for e in (nc.sync, nc.scalar, nc.vector, nc.tensor, nc.gpsimd)]
        self.fori = nc.Fori(0, count, engines=engines)

    def __enter__(self):
        c = self.c
        i = self.fori.__enter__()
        for n, k in self.per.items():
            {"pe": c.pe, "dve": c.dve, "act": c.act, "pool": c.pool}[n].enter(i, k)
        c.it, c.upi = i, self.upi
        return i

    def __exit__(self, *e):
        c = self.c
        self.fori.__exit__(*e)
        if e[0] is not None:
            return False
        got = {n: s.k for n, s in (("pe", c.pe), ("dve", c.dve), ("act", c.act), ("pool", c.pool))}
        if got != self.per:
            raise ValueError(f"LOOPS[{self.name!r}] = {got}")
        for s in (c.pe, c.dve, c.act, c.pool):
            s.leave(self.count)
        c.unit0, c.it, c.upi = c.unit0 + self.count * self.upi, 0, 0
        c.ended = self.name


def table(c, queue, name, src, shape):
    t = c.place(name, shape)
    sem = c.nc.alloc_semaphore("s_" + name)
    queue.dma_start(t[tuple(slice(None) for _ in shape)], src).then_inc(sem, 16)
    return t, (sem, 16)


def transpose_in(c, src, nk, hi, lo, after, banks=(4, 5, 6, 7), weight=None):
    tokens = []
    for n in range(0, nk, 2):
        b = c.ps[:, banks[n // 2 % len(banks)], :]
        if isinstance(after, list):
            wait(c.T, *after[n // 2])
        elif n == 0:
            wait(c.T, *after)
        if n // 2 >= len(banks):
            wait(c.T, tokens[n // 2 - len(banks)])
        for k in range(2):
            for t in range(NT):
                m = c.T.transpose(b[:, (2 * k + t) * P:(2 * k + t + 1) * P], src(t, n + k), c.ident[:, :])
        turned = c.pe(m)
        wait(c.A, turned)
        if weight is None:
            rounded = c.act(c.A.activation(hi(n, 2), b.rearrange("p (k s) -> p k s", k=2), ACT.Copy))
            wait(c.V, rounded)
            tokens.append(c.dve(c.V.tensor_tensor(lo(n, 2), b.rearrange("p (k s) -> p k s", k=2),
                                                  hi(n, 2).bitcast(F32), ALU.subtract)))
        else:
            for k in range(2):
                part = b[:, k * S:(k + 1) * S]
                rounded = c.act(c.A.activation(hi(n + k, 1)[:, 0, :], part, ACT.Copy, scale=weight[:, n + k:n + k + 1]))
            wait(c.V, rounded)
            for k in range(2):
                part = b[:, k * S:(k + 1) * S]
                last = c.V.scalar_tensor_tensor(lo(n + k, 1)[:, 0, :], part, weight[:, n + k:n + k + 1],
                                                hi(n + k, 1)[:, 0, :].bitcast(F32), ALU.mult, ALU.subtract)
            tokens.append(c.dve(last))
    return tokens


def whole(t):
    return lambda n, k: t[:, n:n + k, :]


def rsqrt(c, var, out, eps, tmp, scale=1.0, meanwhile=None):
    a = c.dve(c.V.tensor_scalar(tmp[0], var, scale, eps, ALU.mult, ALU.add))
    wait(c.A, a)
    r = c.act(c.A.activation(tmp[1], tmp[0], ACT.Sqrt))
    if meanwhile:
        meanwhile()
    wait(c.V, r)
    a = c.dve(c.V.reciprocal(out, tmp[1]))
    wait(c.V, a)
    a = c.dve(c.V.tensor_tensor(tmp[1], out, out, ALU.mult))
    wait(c.V, a)
    a = c.dve(c.V.tensor_tensor(tmp[1], tmp[1], tmp[0], ALU.mult))
    wait(c.V, a)
    a = c.dve(c.V.tensor_scalar(tmp[1], tmp[1], -0.5, 1.5, ALU.mult, ALU.add))
    wait(c.V, a)
    return c.dve(c.V.tensor_tensor(out, out, tmp[1], ALU.mult))


def retention_layer(c, d, ready):
    oT = [c.place("a_oT_hi", [P, WA // P, S], F32R, at=c.phase), c.place("a_oT_lo", [P, WA // P, S], F32R)]
    raw = c.place("a_qk_raw", [P, 4, S])
    tcos = c.place("a_tcos", [P, 4, S])
    tsin = c.place("a_tsin", [P, 4, S])
    qk = c.place("a_qk", [P, 4, S])
    sm = c.place("a_scores", [P, 3 * P])
    v = c.place("a_v", [P, NT, DVA])
    g = c.place("a_gate", [P, NT, DVA])
    o = c.place("a_o", [P, NT, DVA])
    st = c.place("a_stats", [P, NT, 6])
    mv = c.place("a_mv", [P, NT, 2])
    rs = c.place("a_rs", [P, NT])
    tmp = [c.place(f"a_tmp{n}", [P, NT]) for n in range(2)]
    ropeA, t_rope = table(c, c.A, "ropeA", d["k_ropeA"], [P, 2, S])
    decay, t_decay = table(c, c.A, "decay", d["k_decay"], [P, HA, 3 * P])
    wait(c.V, t_rope, t_decay)
    wait(c.G, t_rope)
    w = d["a_w_in"]
    cos, sin = (ropeA[:, n:n + 1, :].broadcast_to([P, 4, S]) for n in range(2))
    ps = c.ps
    RAW_BACK, SCORES_BACK = 4, 14
    c.pool(c.G.memset(o[:, :, :], 0.0))

    def turn(head, after, banks=(2, 3)):
        wait(c.T, *after)
        for n in range(2):
            b = ps[:, banks[n], :]
            for k in range(2):
                for t in range(NT):
                    m = c.T.transpose(b[:, (2 * k + t) * P:(2 * k + t + 1) * P],
                                      o[:, t, (2 * n + k) * P:(2 * n + k + 1) * P], c.ident[:, :])
            turned = c.pe(m)
            at = bass.ds(head * 4 + 2 * n, 2)
            b = b.rearrange("p (k s) -> p k s", k=2)
            wait(c.A, turned)
            rounded = c.act(c.A.activation(oT[0][:, at, :], b, ACT.Copy))
            wait(c.V, rounded)
            read = c.dve(c.V.tensor_tensor(oT[1][:, at, :], b, oT[0][:, at, :].bitcast(F32), ALU.subtract))
        return turned, read

    with c.loop("retention", 2, 12) as i:
        t0, v0, a0, g0 = c.pe.now(), c.dve.now(), c.act.now(), c.pool.now()
        raw_read, scores_read = c.act.now(RAW_BACK), c.dve.now(SCORES_BACK)
        wait(c.T, raw_read)
        roped = o_in = turned_read = v0
        gate_in, gated, turned = a0, g0, t0
        v_in0, v_in1 = a0, v0
        for a in range(2):
            u = 6 * a
            for n in range(6):
                c.load(u + n, w[bass.ds(i * 2 + a, 1), n])

            wait(c.T, scores_read)
            for half in range(2):
                c.split(u + half + AHEAD)
                done = c.feature_major(u + half, c.xT, 0, KD, DKA, HALVES(ps[:, half, :]), True, True, ready)
                ready = ()
            wait(c.A, done, roped, gated)
            for n in range(2):
                raw_in = c.act(c.A.activation(raw[:, 2 * n:2 * n + 2, :], ps[:, n, :].rearrange("p (k s) -> p k s", k=2),
                                              ACT.Copy))
            if a == 0:
                turned, turned_read = turn(i * -2 + 3, (v0, a0, g0))
            else:
                turned, turned_read = turn(*todo)
            wait(c.G, raw_in, roped)
            sines = c.pool(c.G.tensor_tensor(tsin[:, :, :], raw[:, :, :], sin, ALU.mult))
            wait(c.V, raw_in)
            cosines = c.dve(c.V.tensor_tensor(tcos[:, :, :], raw[:, :, :], cos, ALU.mult))
            wait(c.V, sines, cosines)
            c.V.tensor_tensor(qk[:, 0::2, :], tcos[:, 0::2, :], tsin[:, 1::2, :], ALU.subtract)
            roped = c.dve(c.V.tensor_tensor(qk[:, 1::2, :], tcos[:, 1::2, :], tsin[:, 0::2, :], ALU.add))

            v_out = [ps[:, 4 + t, :] for t in range(NT)]
            wait(c.T, v_in0, v_in1)
            c.split(u + 2 + AHEAD)
            c.token_major(u + 2, c.xT, 0, 4, 512, v_out, True, False)
            wait(c.T, roped)
            for e, cols in enumerate((slice(0, 2 * P), slice(2 * P, 3 * P))):
                for k in range(2):
                    m = c.T.matmul(ps[:, 0, cols], qk[:, 2 + k, e * P:(e + 1) * P], qk[:, k, e * P:2 * P],
                                   start=e == 0 and k == 0, stop=k == 1, skip_group_check=True)
            scored = c.pe(m)
            c.split(u + 3 + AHEAD)
            wait(c.V, scored)
            scores_read = c.dve(c.V.tensor_tensor(sm[:, :], ps[:, 0, 0:3 * P],
                                                  decay[:, bass.ds(i * 2 + a, 1), :].rearrange("p a n -> p (a n)"), ALU.mult))
            done = c.token_major(u + 3, c.xT, 4, 4, 512, v_out, False, True)
            wait(c.A, done)
            v_in0 = c.act(c.A.activation(v[:, 0, :], v_out[0], ACT.Copy))
            wait(c.V, done)
            v_in1 = c.dve(c.V.tensor_copy(v[:, 1, :], v_out[1]))

            g_out = [ps[:, 2 + t, :] for t in range(NT)]
            c.split(u + 4 + AHEAD)
            wait(c.T, gate_in, turned_read)
            c.token_major(u + 4, c.xT, 0, 4, 512, g_out, True, False)
            wait(c.T, scores_read, v_in0, v_in1, o_in)
            c.T.matmul(ps[:, 6, :], sm[:, 0:P], v[:, 0, :], start=True, stop=True)
            c.T.matmul(ps[:, 7, :], sm[:, P:2 * P], v[:, 0, :], start=True, stop=False)
            inner = c.pe(c.T.matmul(ps[:, 7, :], sm[:, 2 * P:3 * P], v[:, 1, :], start=False, stop=True))
            c.split(u + 5 + AHEAD)
            done = c.token_major(u + 5, c.xT, 4, 4, 512, g_out, False, True)
            wait(c.V, inner)
            for t in range(NT):
                s_ = c.dve(c.V.bn_stats(st[:, t, :], ps[:, 6 + t, :]))
            wait(c.V, s_)
            c.V.memset(tmp[0][:, :], 0.0)
            for t in range(NT):
                s_ = c.dve(c.V.bn_aggr(mv[:, t, :], st[:, t, :]))
            wait(c.V, s_)
            r = rsqrt(c, mv[:, :, 1], rs[:, :], 1e-5, [t[:, :] for t in tmp])
            wait(c.V, r, turned)
            for t in range(NT):
                o_in = c.dve(c.V.tensor_scalar(o[:, t, :], ps[:, 6 + t, :], mv[:, t, 0:1], rs[:, t:t + 1],
                                               ALU.subtract, ALU.mult))
            wait(c.A, done, gated)
            for t in range(NT):
                gate_in = c.act(c.A.activation(g[:, t, :], g_out[t], ACT.Silu))
            wait(c.G, gate_in, o_in)
            gated = c.pool(c.G.tensor_tensor(o[:, 0, :], o[:, 0, :], g[:, 0, :], ALU.mult))
            wait(c.V, gate_in, o_in)
            gated1 = c.dve(c.V.tensor_tensor(o[:, 1, :], o[:, 1, :], g[:, 1, :], ALU.mult))
            todo = (i * 2 + a, (gated, gated1))
            roped = gated1
        if raw_in[3] > c.act.serial - RAW_BACK or scores_read[3] > c.dve.serial - SCORES_BACK:
            raise ValueError("banks 0 and 1 are read later than is waited for")
        last = [(token[2], token[2].serial - token[3]) for token in (raw_in, scores_read, turned_read)]
    after = [signal.now(back) for signal, back in last]
    everything = (c.dve.now(), c.act.now(), c.pool.now())

    def last_head():
        return turn(HA - 1, everything, (4, 5))[1]

    def gates_read():
        wait(c.T, *everything)

    return oT, after, {3: [gates_read], 5: [last_head], 6: [lambda: wait(c.T, c.dve.now())]}


def layer_norm(c, lnw, after):
    lnw, arrived = lnw
    gain, bias = lnw[:, 0, :], lnw[:, 1, :]
    wait(c.V, *after, arrived)
    for t in range(NT):
        aggregated = c.dve(c.V.bn_aggr(c.mv[:, t, :], c.st[:, t, :, :].rearrange("p a b -> p (a b)")))
    wait(c.V, aggregated)
    wait(c.G, aggregated, arrived)
    blocks = [(0, 0, c.V, c.dve), (1, 1, c.G, c.pool), (1, 0, c.V, c.dve), (0, 1, c.V, c.dve)]
    centred = {}

    def centre():
        for t, b, engine, signal in blocks:
            r, cols = c.res[:, t, b * 512:(b + 1) * 512], slice(b * 512, (b + 1) * 512)
            if engine is c.G:
                less = signal(engine.tensor_scalar(r, r, c.mv[:, t, 0:1], None, ALU.subtract))
                wait(engine, less)
                centred[t, b] = signal(engine.tensor_tensor(r, r, gain[:, cols], ALU.mult))
            else:
                centred[t, b] = signal(engine.scalar_tensor_tensor(r, r, c.mv[:, t, 0:1], gain[:, cols],
                                                                   ALU.subtract, ALU.mult))

    root = rsqrt(c, c.mv[:, :, 1], c.rs[:, :], 1e-5, c.tmp, meanwhile=centre)
    wait(c.V, root)
    wait(c.G, root)
    normed = [[], []]
    for t, b, engine, signal in blocks:
        r, cols = c.res[:, t, b * 512:(b + 1) * 512], slice(b * 512, (b + 1) * 512)
        if engine is c.G:
            wait(engine, centred[t, b])
            scaled = signal(engine.tensor_scalar(r, r, c.rs[:, t:t + 1], None, ALU.mult))
            wait(engine, scaled)
            normed[b].append(signal(engine.tensor_tensor(r, r, bias[:, cols], ALU.add)))
        else:
            normed[b].append(signal(engine.scalar_tensor_tensor(r, r, c.rs[:, t:t + 1], bias[:, cols],
                                                                ALU.mult, ALU.add)))
    return normed


def load_ln(c, layer, d, at, after):
    lnw = c.place(f"lnw{layer}", [P, 2, D], at=at)
    sem = c.nc.alloc_semaphore(f"s_lnw{layer}")
    wait(c.A, *after)
    for n, name in enumerate(("ln_g", "ln_b")):
        c.A.dma_start(lnw[:, n, :], d[name][layer:layer + 1, :].broadcast_to([P, D])).then_inc(sem, 16)
    return lnw, (sem, 32)


def out_projection(c, w, oT, alpha, after, hooks):
    order = [(b, q) for b in range(2) for q in range(3)] + [(0, 3), (1, 3)]
    for n, (b, q) in enumerate(order):
        out = [c.ps[:, 2 * b + t, :] for t in range(NT)]
        c.load(n, w[b, q])
        c.split(n + AHEAD)
        if n == 0:
            wait(c.T, *after)
        for hook in hooks.get(n, ()):
            hook()
        done = c.token_major(n, oT, 4 * q, 4, 512, out, q == 0, q == 3)
        if q == 3:
            wait(c.V, done)
            for t in range(NT):
                r = c.res[:, t, b * 512:(b + 1) * 512]
                added = c.dve(c.V.scalar_tensor_tensor(r, r, alpha, out[t], ALU.mult, ALU.add))
                wait(c.V, added)
                stats = c.dve(c.V.bn_stats(c.st[:, t, b, :], r))
    c.advance(8)
    return stats


def HALVES(*banks):
    return [b[:, n * S:(n + 1) * S] for b in banks for n in range(2)]


def latent_tables(c, d):
    c.top = c.phase + 2 * 4 * HB * S
    wait(c.A, c.pe.now(), c.dve.now(), c.act.now(), c.pool.now())
    named = (("ropeB", "k_ropeB", [P, 2, S]), ("rotB", "k_rotB", [P, P]), ("maskB", "k_maskB", [P, 3 * P]),
             ("qnorm", "b_q_norm", [P, QL // P]), ("kvnorm", "kv_norm", [P, KVL // P]))
    loaded = [table(c, c.A, name, d[source], shape) for name, source, shape in named]
    return [t for t, _ in loaded], [arrived for _, arrived in loaded], c.top


def latent_attention_layer(c, d, ready, tables):
    ps = c.ps
    (rope, rot, mask, qnorm, kvnorm), arrived, end = tables
    oT = [c.place("b_oT_hi", [P, HB, S], F32R, at=c.phase), c.place("b_oT_lo", [P, HB, S], F32R)]
    c.top = end
    lat = c.place("b_lat", [P, NT, KVL], at=c.phase)
    qlat = c.place("b_qlat", [P, NT, QL])
    junk = c.place("b_junk", [P, 4, 512])
    c.top = end
    qlatT = [c.place("b_qlatT_hi", [P, QL // P, S], F32R), c.place("b_qlatT_lo", [P, QL // P, S], F32R)]
    latT = [c.place("b_latT_hi", [P, KVL // P, S], F32R), c.place("b_latT_lo", [P, KVL // P, S], F32R)]
    kr = c.place("b_kr", [P, 2, S])
    both = lambda name, *shape: c.place(name, [P, 2, *shape])
    qn, kn, v, gate = both("b_qn", 2, S), both("b_kn", 2, S), both("b_v", NT, 2 * VH), both("b_gate", 2, S)
    qr, p, pT = both("b_qr", S), both("b_p", 3 * P), both("b_pT", 3 * P)
    xr, xc, xs = (c.place(n, [P, S]) for n in ("b_xr", "b_xc", "b_xs"))
    og = c.place("b_og", [P, 2, S])
    few = c.place("b_few", [P, 5, 2, 2])
    sq, sq2, nmax, sums, rsum = (few[:, n, :, :] for n in range(5))
    wait(c.V, *arrived)
    wait(c.G, *arrived)
    wait(c.A, *arrived)
    wait(c.T, *arrived)
    zero = c.dve(c.V.memset(kr[:, :, :], 0.0))

    w = d["b_w_qlat"]
    for b in range(2):
        for half in range(2):
            j = 2 * b + half
            c.load(j, w[b, half])
            c.split(j + AHEAD)
            done = c.token_major(j, c.xT, 4 * half, 4, 384, [ps[:, 2 * b + t, 0:384] for t in range(NT)],
                                 half == 0, half == 1, ready if b == 0 else ())
        wait(c.A, done)
        for t in range(NT):
            squared = c.act(c.A.activation(junk[:, 2 * b + t, 0:384], ps[:, 2 * b + t, 0:384], ACT.Square,
                                           accum_out=sq[:, t, b:b + 1]))
    wait(c.V, squared)
    r = c.dve(c.V.tensor_tensor(sq2[:, :, 0], sq[:, :, 0], sq[:, :, 1], ALU.add))
    wait(c.V, r)
    r = rsqrt(c, sq2[:, :, 0], c.rs[:, :], 1e-6, c.tmp, 1.0 / QL)
    wait(c.V, r)
    for b in range(2):
        for t in range(NT):
            qlat_in = c.dve(c.V.tensor_scalar(qlat[:, t, b * 384:(b + 1) * 384], ps[:, 2 * b + t, 0:384],
                                              c.rs[:, t:t + 1], None, ALU.mult))
    c.advance(4)

    DOWN = KVL + 2 * ROPE
    for j in range(4):
        c.load(j, d["kv_w_down"][0, j])
        c.split(j + AHEAD)
        wh, wl = (z[:, 0:2 * DOWN].rearrange("p (k n) -> p k n", k=2) for z in c.use(j))
        for k in range(2):
            first, last = j == 0 and k == 0, j == 3 and k == 1
            for t in range(NT):
                x = tuple(z[:, 2 * j + k, t * P:(t + 1) * P] for z in c.xT)
                c.mm3(ps[:, 4 + t, :], x, (wh[:, k, 0:KVL], wl[:, k, 0:KVL]), first, last)
            x = tuple(z[:, 2 * j + k, :] for z in c.xT)
            m = c.mm3(ps[:, 6, 0:S], (wh[:, k, KVL:DOWN], wl[:, k, KVL:DOWN]), x, first, last)
        m.then_inc(c.w_used, 1)
    done = c.used(3)
    c.advance(4)
    queries = transpose_in(c, lambda t, k: qlat[:, t, k * P:(k + 1) * P], QL // P, whole(qlatT[0]), whole(qlatT[1]),
                              (qlat_in,), banks=(0, 1, 2), weight=qnorm)
    wait(c.A, done)
    for t in range(NT):
        squared = c.act(c.A.activation(junk[:, t, :], ps[:, 4 + t, :], ACT.Square, accum_out=sq[:, t, 0:1]))
    wait(c.V, squared)
    r = rsqrt(c, sq[:, :, 0], c.rs[:, :], 1e-6, c.tmp, 1.0 / KVL)
    wait(c.V, r)
    for t in range(NT):
        lat_in = c.dve(c.V.tensor_scalar(lat[:, t, :], ps[:, 4 + t, :], c.rs[:, t:t + 1], None, ALU.mult))
    xr_in = c.dve(c.V.tensor_copy(xr[:, :], ps[:, 6, 0:S]))

    def latents_to_features():
        wait(c.T, xr_in)
        rotated = c.pe(c.T.matmul(ps[:, 7, 0:S], rot[:, :], xr[:, :], start=True, stop=True))
        wait(c.V, xr_in)
        a = c.dve(c.V.tensor_tensor(xc[:, :], xr[:, :], rope[:, 0, :], ALU.mult))
        wait(c.V, rotated, zero, a)
        a = c.dve(c.V.tensor_tensor(xs[:, :], ps[:, 7, 0:S], rope[:, 1, :], ALU.mult))
        wait(c.V, a)
        for n in range(2):
            rows = slice(n * ROPE, (n + 1) * ROPE)
            kr_in = c.dve(c.V.tensor_tensor(kr[rows, n, :], xc[rows, :], xs[rows, :], ALU.add))
        latents = transpose_in(c, lambda t, k: lat[:, t, k * P:(k + 1) * P], KVL // P, whole(latT[0]),
                               whole(latT[1]), (lat_in,), banks=(4, 5), weight=kvnorm)
        pr["ready"] = (kr_in,)
        pr["kv"] += (latents[-1],)
        wait(c.T, queries[-1])

    w_gate, w_uq, w_kv = d["b_w_gate"], d["b_w_uq"], d["kv_w_up"]
    QC, KC = NOPE + ROPE, NOPE + VH

    class Free(dict):

        NAMES = ("ready", "scores", "pT_bank", "o", "og", "gate", "uq", "kv", "q", "xr", "xs", "p0", "p1", "pT0", "pT1")

        def __init__(self, *issued):
            super().__init__((name, issued) for name in self.NAMES)

        def distances(self):
            return {name: [(t[2], t[2].serial - t[3]) for t in tokens] for name, tokens in self.items()}

        def carry(self, distances):
            self.update((name, tuple(signal.now(back) for signal, back in d)) for name, d in distances.items())

    def attend_scores(pr, par, h):
        wait(c.T, *pr["ready"], *pr["scores"])
        for q, cols in enumerate((slice(0, P), slice(P, 3 * P))):
            out, qs, keys = ps[:, 5, cols], slice(q * P, (q + 1) * P), slice(0, (q + 1) * P)
            c.T.matmul(out, qn[:, par, h, qs], kn[:, par, h, keys], start=q == 0, stop=False, skip_group_check=True)
            m = c.T.matmul(out, qr[:, par, qs], kr[:, h, keys], start=False, stop=True, skip_group_check=True)
        scored = c.pe(m)
        wait(c.V, scored, *pr[f"p{h}"])
        c.V.memset(nmax[:, h, :], 0.0)
        for q, cols in enumerate((slice(0, P), slice(P, 3 * P))):
            a = c.dve(c.V.tensor_tensor_reduce(out=p[:, h, cols], in0=ps[:, 5, cols], in1=mask[:, cols],
                                               scale=SCALE_B, scalar=-3.0e38, op0=ALU.add, op1=ALU.max,
                                               accum_out=sums[:, h, q:q + 1]))
        pr["scores"] = (a,)
        wait(c.V, a)
        negated = c.dve(c.V.tensor_scalar(nmax[:, h, :], sums[:, h, :], -1.0, None, ALU.mult))
        wait(c.A, negated)
        for q, cols in enumerate((slice(0, P), slice(P, 3 * P))):
            a = c.act(c.A.activation(p[:, h, cols], p[:, h, cols], ACT.Exp, bias=nmax[:, h, q:q + 1],
                                     accum_out=rsum[:, h, q:q + 1]))
        wait(c.V, a)
        a = c.dve(c.V.reciprocal(rsum[:, h, :], rsum[:, h, :]))
        wait(c.V, a)
        for q, cols in enumerate((slice(0, P), slice(P, 3 * P))):
            a = c.dve(c.V.tensor_scalar(p[:, h, cols], p[:, h, cols], rsum[:, h, q:q + 1], None, ALU.mult))
        pr.p_in = a

    def attend_turn(pr, par, h):
        wait(c.T, pr.p_in, *pr["pT_bank"])
        for n in range(3):
            m = c.T.transpose(ps[:, 6, n * P:(n + 1) * P], p[:, h, n * P:(n + 1) * P], c.ident[:, :])
        turned = c.pe(m)
        pr[f"p{h}"] = (turned,)
        wait(c.A, turned, *pr[f"pT{h}"])
        pr.pT_in = c.act(c.A.activation(pT[:, h, :], ps[:, 6, 0:3 * P], ACT.Copy))
        pr["pT_bank"] = (pr.pT_in,)

    def attend_values(pr, par, h):
        wait(c.T, pr.pT_in, *pr["o"])
        out = ps[:, 7, h * S:(h + 1) * S]
        cols = slice(h * VH, (h + 1) * VH)
        c.T.matmul(out, v[:, par, 0, cols], pT[:, h, 0:2 * P], start=h == 0, stop=False, skip_group_check=True)
        done = c.pe(c.T.matmul(out[:, P:2 * P], v[:, par, 1, cols], pT[:, h, 2 * P:3 * P], start=False, stop=True,
                               skip_group_check=True))
        pr[f"pT{h}"] = (done,)
        return done

    def attend_out(pr, par, pair, done):
        wait(c.V, done, *pr["og"])
        o = c.dve(c.V.tensor_tensor(og[:, :, :], ps[:, 7, :].rearrange("p (h s) -> p h s", h=2), gate[:, par, :, :], ALU.mult))
        pr["o"] = (o,)
        at = bass.ds(pair * 2, 2)
        wait(c.A, o)
        r = c.act(c.A.activation(oT[0][:, at, :], og[:, :, :], ACT.Copy))
        wait(c.G, r)
        g_ = c.pool(c.G.tensor_tensor(oT[1][:, at, :], og[:, :, :], oT[0][:, at, :].bitcast(F32), ALU.subtract))
        pr["og"] = (g_,)

    def step(pr, j0, pair, par, other, between=None):
        if pair is not None:
            at = bass.ds(pair, 1)
            c.load(j0, w_gate[at])
            for n in range(2):
                c.load(j0 + 1 + n, w_uq[at, n])
            c.load(j0 + 3, w_kv[at])
            c.split(j0 + AHEAD)
            wait(c.T, *pr["gate"])
            done = c.feature_major(j0, c.xT, 0, KD, 2 * VH, HALVES(ps[:, 0, :]), True, True)
            wait(c.A, done, *pr["o"])
            gate_in = c.act(c.A.activation(gate[:, par, :, :], ps[:, 0, :].rearrange("p (h s) -> p h s", h=2), ACT.Silu))
            pr["gate"] = (gate_in,)
        if between:
            between()
        if other is not None:
            attend_scores(pr, 1 - par, 0)
        if pair is not None:
            wait(c.T, *pr["uq"])
            for n in range(2):
                c.split(j0 + 1 + n + AHEAD)
                wh, wl = (z[:, 0:6 * QC].rearrange("p (k n) -> p k n", k=3) for z in c.use(j0 + 1 + n))
                for q, out in enumerate((ps[:, 1, 0:S], ps[:, 1, S:2 * S], ps[:, 2, 0:S])):
                    for k in range(3):
                        m = c.mm3(out, tuple(z[:, k, q * P:(q + 1) * P] for z in (wh, wl)),
                                  tuple(z[:, 3 * n + k, :] for z in qlatT), n == 0 and k == 0 and q != 1, n == 1 and k == 2)
                m.then_inc(c.w_used, 1)
                if n == 0 and other is not None:
                    attend_turn(pr, 1 - par, 0)
                    attend_scores(pr, 1 - par, 1)
            done = c.used(j0 + 2)
            wait(c.A, done, *pr["q"])
            qn_in = c.act(c.A.activation(qn[:, par, :, :], ps[:, 1, :].rearrange("p (h s) -> p h s", h=2), ACT.Copy))
            wait(c.V, done, *pr["xr"])
            xr_in = c.dve(c.V.tensor_copy(xr[:, :], ps[:, 2, 0:S]))
        elif other is not None:
            attend_turn(pr, 1 - par, 0)
            attend_scores(pr, 1 - par, 1)
        if other is not None:
            attend_values(pr, 1 - par, 0)
            attend_turn(pr, 1 - par, 1)
        if pair is not None:
            c.split(j0 + 3 + AHEAD)
            wait(c.T, *pr["kv"])
            wh, wl = (z[:, 0:4 * 2 * KC].rearrange("p (k n) -> p k n", k=4) for z in c.use(j0 + 3))
            for h in range(2):
                for k in range(4):
                    c.mm3(ps[:, 3, h * S:(h + 1) * S], tuple(z[:, k, h * P:(h + 1) * P] for z in (wh, wl)),
                          tuple(z[:, k, :] for z in latT), h == 0 and k == 0, k == 3)
            for t in range(NT):
                for k in range(4):
                    m = c.mm3(ps[:, 4, t * S:(t + 1) * S], tuple(z[:, k, t * P:(t + 1) * P] for z in latT),
                              tuple(z[:, k, 2 * NOPE:2 * KC] for z in (wh, wl)),
                              t == 0 and k == 0, k == 3)
            m.then_inc(c.w_used, 1)
            done = c.used(j0 + 3)
            wait(c.T, xr_in)
            rotated = c.pe(c.T.matmul(ps[:, 2, S:2 * S], rot[:, :], xr[:, :], start=True, stop=True))
        if other is not None:
            o_done = attend_values(pr, 1 - par, 1)
            attend_out(pr, 1 - par, other, o_done)
        if pair is not None:
            wait(c.G, xr_in, *pr["xs"])
            cosines = c.pool(c.G.tensor_tensor(xc[:, :], xr[:, :], rope[:, 0, :], ALU.mult))
            pr["xr"] = (cosines, rotated)
            wait(c.V, rotated, *pr["xs"])
            sines = c.dve(c.V.tensor_tensor(xs[:, :], ps[:, 2, S:2 * S], rope[:, 1, :], ALU.mult))
            pr["uq"] = (sines, qn_in)
            wait(c.G, sines, cosines, *pr["q"])
            qr_in = c.pool(c.G.tensor_tensor(qr[:, par, :], xc[:, :], xs[:, :], ALU.add))
            pr["xs"] = (qr_in,)
            wait(c.A, done)
            kn_in = c.act(c.A.activation(kn[:, par, :, :], ps[:, 3, :].rearrange("p (h s) -> p h s", h=2), ACT.Copy))
            wait(c.V, done, *pr["q"])
            v_in = c.dve(c.V.tensor_copy(v[:, par, :, :], ps[:, 4, :].rearrange("p (t n) -> p t n", t=2)))
            pr["kv"] = (kn_in, v_in)
            pr["ready"] = (kn_in, v_in, qn_in, qr_in)
            pr["q"] = ()
        if other is not None:
            pr["q"] = (o_done,)

    pr = Free(c.pe.now(), c.dve.now(), c.act.now(), c.pool.now())
    pr["gate"] = (queries[-1],)
    step(pr, 0, 0, 0, None, latents_to_features)
    c.advance(4)
    step(pr, 0, 1, 1, 0)
    c.advance(4)
    back = pr.distances()
    with c.loop("attention", 3, 8) as i:
        pr.carry(back)
        step(pr, 0, i * 2 + 2, 0, i * 2 + 1)
        step(pr, 4, i * 2 + 3, 1, i * 2 + 2)
        if pr.distances() != back:
            raise ValueError("the loop's body ends in another order than the step before it")
    pr.carry(back)

    last = HB // 2 - 1
    done = []

    def first_scores():
        attend_scores(pr, last % 2, 0)

    def second_scores():
        attend_turn(pr, last % 2, 0)
        attend_scores(pr, last % 2, 1)

    def first_values():
        attend_values(pr, last % 2, 0)
        attend_turn(pr, last % 2, 1)
        wait(c.T, *pr["kv"])

    def last_values():
        done.append(attend_values(pr, last % 2, 1))
        attend_out(pr, last % 2, last, done[0])

    after = (*pr["gate"], *pr["uq"], *pr["kv"], *pr["og"])
    hooks = {1: [first_scores], 2: [second_scores], 3: [first_values], 4: [last_values],
             6: [lambda: wait(c.T, *pr["og"])]}
    return oT, after, hooks


def feature_stage(c, name, count, source, xT, drain, signal, after, per_unit=1, ready=(), hooks={}):
    wait(c.T, *after)

    def body(i):
        for j in range(4):
            n = i * 4 + j
            c.load(j, source(n))
            c.split(j + AHEAD)
            for hook in hooks.get(j, ()):
                hook()
            if count > 1:
                wait(c.T, signal.now(3 * per_unit))
            done = c.feature_major(j, xT, 0, KD, S, HALVES(c.ps[:, j, :]), True, True, ready if j == 0 else ())
            drain(n, c.ps[:, j, :].rearrange("p (k s) -> p k s", k=2), done, j)

    if count == 1:
        body(0)
        c.advance(4)
    else:
        with c.loop(name, count, 4) as i:
            body(i)


def softplus8(c, lam, out, neg, tmp):
    t, e, q = tmp
    v, one = c.V, lambda ins: wait(c.V, c.dve(ins))
    one(v.tensor_scalar(t, lam, -1.0, None, ALU.mult))
    one(v.tensor_tensor(e, t, lam, ALU.min))
    wait(c.A, c.dve.now())
    wait(v, c.act(c.A.activation(e, e, ACT.Exp)))
    one(v.tensor_scalar(t, e, 2.0, None, ALU.add))
    one(v.reciprocal(q, t))
    one(v.tensor_tensor(e, e, q, ALU.mult))
    one(v.tensor_tensor(t, e, e, ALU.mult))
    one(v.tensor_scalar(q, t, 1.0 / 17.0, None, ALU.mult))
    for n in (15.0, 13.0, 11.0, 9.0, 7.0, 5.0, 3.0):
        one(v.scalar_tensor_tensor(q, q, 1.0 / n, t, ALU.add, ALU.mult))
    one(v.scalar_tensor_tensor(q, q, 1.0, e, ALU.add, ALU.mult))
    one(v.tensor_scalar(t, lam, -1.0, 0.0, ALU.mult, ALU.max))
    one(v.scalar_tensor_tensor(t, q, 2.0, t, ALU.mult, ALU.add))
    one(v.tensor_scalar(out, t, 4.0, None, ALU.mult))
    one(v.tensor_scalar(neg, t, -8.0, None, ALU.mult))


def rms_input(c, h, junk, squares, weight, normed):
    for b in range(2):
        cols = slice(b * 512, (b + 1) * 512)
        wait(c.A, *normed[b])
        for t in range(NT):
            squared = c.act(c.A.activation(junk[:, t, cols], c.res[:, t, cols], ACT.Square,
                                           accum_out=squares[:, b, t:t + 1]))
    wait(c.V, squared)
    total = c.dve(c.V.tensor_tensor(squares[:, 0, :], squares[:, 0, :], squares[:, 1, :], ALU.add))
    wait(c.V, total)
    r = rsqrt(c, squares[:, 0, :], c.rs[:, :], 1e-6, c.tmp, 1.0 / D)
    wait(c.V, r, *normed[0], *normed[1])
    wait(c.A, r)
    scaled = []
    for b in range(2):
        cols = slice(b * 512, (b + 1) * 512)
        scaled.append((c.dve(c.V.tensor_scalar(h[:, 0, cols], c.res[:, 0, cols], c.rs[:, 0:1], None, ALU.mult)),
                       c.act(c.A.activation(h[:, 1, cols], c.res[:, 1, cols], ACT.Copy, scale=c.rs[:, 1:2]))))
    return transpose_in(c, lambda t, k: h[:, t, k * P:(k + 1) * P], KD, whole(c.xT[0]), whole(c.xT[1]),
                        [scaled[n // 2] for n in range(4)], weight=weight)


def hybrid_layer(c, d, out):
    ps, V, A, G, T = c.ps, c.V, c.A, c.G, c.T
    dve, act, pool, pe = c.dve, c.act, c.pool, c.pe
    everything = lambda: (pe.now(), dve.now(), act.now(), pool.now())
    pair = lambda b: b.rearrange("p (k s) -> p k s", k=2)
    QCOLS = (slice(0, P), slice(P, 3 * P))

    c.top = c.phase
    qk = c.place("c_qk", [P, NT, D + 256])
    v = c.place("c_v", [P, NT, 256])
    iq = c.place("c_iq", [P, NT, IH * ID])
    qT = c.place("c_qT", [P, KD, S])
    kz = c.place("c_kz", [P, HKV, S])
    iqT = c.place("c_iqT", [P, IH // 2, S])
    ikz = c.place("c_ikz", [P, 2, S])
    isc = c.place("c_isc", [P, NT, S])
    xc = c.place("c_xc", [P, KD, S])
    ig = c.place("c_ig", [P, KD, S])
    aa = c.place("c_aa", [P, KD, S])
    gel = c.place("c_gel", [P, KD, S])
    rgw = c.place("c_rgw", [P, 2, KD, P])
    g0 = c.place("c_g0", [P, KD, S])
    ikw = c.place("c_ikw", [P, NT, 2 * ID + IH])
    small = c.top
    rr = c.place("c_rr", [P, KD, S], at=c.at["c_qk"])
    ya = c.place("c_ya", [P, NT, D], at=c.at["c_qk"])
    rl = c.place("c_rl", [P, 2, 3 * P], at=c.at["c_iq"])
    wk = c.place("c_wk", [P, NT, S], at=c.at["c_iq"])
    eqs = c.place("c_eqs", [P, NT, S])
    ones = c.place("c_ones", [P, S], at=c.at["c_iqT"])
    cum = c.place("c_cum", [P, NT, S])
    pT = c.place("c_pT", [P, 4, 3 * P], at=c.at["c_iqT"])
    h = c.place("c_h", [P, NT, D], at=c.at["c_xc"])
    kw_raw = c.place("c_kw_raw", [P, KD, 2 * ID + IH], at=c.at["c_ig"])
    kw = [c.place("c_kw_hi", [P, KD, 2 * ID + IH], F32R), c.place("c_kw_lo", [P, KD, 2 * ID + IH], F32R)]
    junk = c.place("c_junk", [P, NT, D], at=c.at["c_gel"])
    yT = [c.place("c_yT_hi", [P, KD, S], F32R, at=c.at["c_xc"]), c.place("c_yT_lo", [P, KD, S], F32R)]
    zT = yT
    p = c.place("c_p", [P, 4, 3 * P], at=c.at["c_aa"])
    g1 = c.place("c_g1", [P, KD, S], at=c.at["c_rgw"])
    fT = [c.place("c_fT_hi", [P, DFF // P, S], F32R, at=c.phase), c.place("c_fT_lo", [P, DFF // P, S], F32R)]
    fr = c.place("c_fr", [P, 4, 2, S])
    h2 = c.place("c_h2", [P, NT, D], at=c.phase)
    junk2 = c.place("c_junk2", [P, NT, D])
    c.top = small
    s_kw, s_rgw, s_columns, s_out0 = (c.nc.alloc_semaphore(n) for n in ("s_kw", "s_rgw", "s_columns", "s_out0"))
    columns = c.place("c_columns", [P, sum(n for _, n in COLUMNS_C)])
    vec, at = {}, 0
    for name, n in COLUMNS_C:
        vec[name], at = columns[:, at:at + n], at + n
    lam = c.place("c_lam", [P, 6, 8])
    hlam8, nlam8 = lam[:, 0, :], lam[:, 1, :]
    NH = HC + HKV + 1
    hs, hr, ht0, ht1 = (c.place(n, [P, NT, NH]) for n in ("c_hs", "c_hr", "c_ht0", "c_ht1"))
    few = c.place("c_few", [P, 2 * NT + 8 * NT + NT + 16])
    squares = few[:, 0:4].rearrange("p (b t) -> p b t", b=2)
    m8 = few[:, 4:20].rearrange("p (t n) -> p t n", t=NT)
    cnt = few[:, 20:22]
    smx, ssum = (few[:, n:n + 8].rearrange("p (q r) -> p q r", q=2) for n in (22, 30))

    wait(A, *everything())
    A.dma_start(columns[:, :], d["columns"]).then_inc(s_columns, 16)
    A.dma_start(kw_raw[:, :, :].rearrange("p k n -> p (k n)"), d["w_ikw"]).then_inc(s_kw, 16)
    A.dma_start(rgw[:, :, :, :].rearrange("p a k n -> p (a k n)"), d["rg_w"]).then_inc(s_rgw, 16)
    yield

    wait(A, (s_kw, 16))
    kw_hi = act(A.activation(kw[0][:, :, :], kw_raw[:, :, :], ACT.Copy))
    wait(V, (s_columns, 16))
    softplus8(c, vec["rg_lambda_2"], hlam8, nlam8, [lam[:, 3 + n, :] for n in range(3)])
    wait(V, kw_hi)
    kw_in = dve(V.tensor_tensor(kw[1][:, :, :], kw_raw[:, :, :], kw[0][:, :, :].bitcast(F32), ALU.subtract))
    normed = yield

    wait(A, (s_columns, 16))
    transposed = rms_input(c, h, junk, squares, vec["norm1_w_2"], normed)

    drained = {}
    for b, name in enumerate(("q", "q", "kv", "iq")):
        block = [ps[:, 2 * (b % 2) + t, :] for t in range(NT)]
        if b >= 2:
            wait(T, *drained[b - 2])
        for half in range(2):
            j = 2 * b + half
            c.load(j, d["w_qkvi"][b, half])
            c.split(j + AHEAD)
            done = c.token_major(j, c.xT, 4 * half, 4, 512, block, half == 0, half == 1,
                                 transposed if b == 0 else ())
        wait(A, done)
        wait(V, done)
        for t in range(NT):
            copy = (lambda o, i: act(A.activation(o, i, ACT.Copy))) if t == 0 else (lambda o, i: dve(V.tensor_copy(o, i)))
            if name == "q":
                copy(qk[:, t, b * 512:(b + 1) * 512], block[t])
            elif name == "kv":
                copy(qk[:, t, D:D + 256], block[t][:, 0:256])
                copy(v[:, t, :], block[t][:, 256:512])
            else:
                copy(iq[:, t, :], block[t])
        drained[b] = (act.now(), dve.now())
    c.advance(8)
    wait(T, kw_in)
    for k in range(KD):
        for t in range(NT):
            x = tuple(z[:, k, t * P:(t + 1) * P] for z in c.xT)
            m = c.mm3(ps[:, 4 + t, 0:2 * ID + IH], x, tuple(z[:, k, :] for z in kw), k == 0, k == KD - 1)
    done = pe(m)
    wait(A, done)
    for t in range(NT):
        ikw_in = act(A.activation(ikw[:, t, :], ps[:, 4 + t, 0:2 * ID + IH], ACT.Copy))

    wait(A, *drained[3], ikw_in)
    for t in range(NT):
        A.activation(junk[:, t, :], qk[:, t, 0:D], ACT.Square)
    A.activation(h[:, :, 0:256], qk[:, :, D:D + 256], ACT.Square)
    squared = act(A.activation(h[:, :, 256:256 + ID], ikw[:, :, 0:ID], ACT.Square))
    wait(V, squared)
    for t in range(NT):
        V.reduce_sum(hs[:, t, 0:HC], junk[:, t, :].rearrange("p (h n) -> p h n", n=DC), AX.X)
        a = dve(V.reduce_sum(hs[:, t, HC:NH], h[:, t, 0:256 + ID].rearrange("p (h n) -> p h n", n=DC), AX.X))
    flat = lambda t: t[:, :, :].rearrange("p t n -> p (t n)")
    wait(V, a)
    r = rsqrt(c, flat(hs), flat(hr), 1e-6, (flat(ht0), flat(ht1)), 1.0 / DC)
    wait(V, r)
    wait(G, r)
    for t, (eng, sig) in enumerate(((V, dve), (G, pool))):
        x = qk[:, t, :].rearrange("p (h n) -> p h n", n=DC)
        sig(eng.tensor_tensor(x, x, hr[:, t, 0:HC + HKV].unsqueeze(2).broadcast_to([P, HC + HKV, DC]), ALU.mult))
    for t in range(NT):
        V.tensor_scalar(ikw[:, t, 0:2 * ID], ikw[:, t, 0:2 * ID], hr[:, t, NH - 1:NH], None, ALU.mult)
    V.memset(kz[:, :, :], 0.0)
    dve(V.memset(ikz[:, :, :], 0.0))
    heads = everything()

    cw, cb = vec["conv_w_2"], vec["conv_b_2"]

    def conv(n, bank, done, j):
        wait(A, done)
        for k in range(2):
            tile = 2 * n + k
            first = act(A.activation(xc[:, tile, :], bank[:, k, :], ACT.Identity, bias=cb[:, tile:tile + 1],
                                     scale=cw[:, 24 + tile:25 + tile]))
        wait(V, first)
        for s in (1, 2, 3):
            for k in range(2):
                tile = 2 * n + k
                a = dve(V.scalar_tensor_tensor(xc[:, tile, s:S], bank[:, k, 0:S - s], cw[:, (3 - s) * 8 + tile:(3 - s) * 8 + tile + 1],
                                               xc[:, tile, s:S], ALU.mult, ALU.add))
            if s < 3:
                wait(V, a)

    hn = vec["head_norms"]
    small_banks = [4, 5, 6, 7]
    bank_read = {b: (ikw_in,) for b in small_banks}

    def small_bank():
        b = small_banks.pop(0)
        small_banks.append(b)
        wait(T, *bank_read[b])
        return b, ps[:, b, :]

    def to_features(name, t0):
        b, bank = small_bank()
        for k in range(1 if name == "ik" else 2):
            for t in range(NT):
                src = {"q": lambda: qk[:, t, (t0 + k) * P:(t0 + k + 1) * P], "k": lambda: qk[:, t, D + k * P:D + (k + 1) * P],
                       "iq": lambda: iq[:, t, (t0 + k) * P:(t0 + k + 1) * P], "ik": lambda: ikw[:, t, 0:P]}[name]()
                m = T.transpose(bank[:, (2 * k + t) * P:(2 * k + t + 1) * P], src, c.ident[:, :])
        turned = pe(m)
        wait(A, turned)
        if name == "q":
            a = act(A.activation(qT[:, t0:t0 + 2, :], pair(bank), ACT.Copy, scale=hn[:, 0:1]))
        elif name == "iq":
            a = act(A.activation(iqT[:, t0:t0 + 2, :], pair(bank), ACT.Copy))
        elif name == "k":
            for g in range(HKV):
                rows = slice(64 * (g % 2), 64 * (g % 2) + 64)
                a = act(A.activation(kz[rows, g, :], bank[rows, (g // 2) * S:(g // 2 + 1) * S], ACT.Copy, scale=hn[rows, 1:2]))
        else:
            for g in range(2):
                rows = slice(64 * g, 64 * g + 64)
                a = act(A.activation(ikz[rows, g, :], bank[rows, 0:S], ACT.Copy, scale=hn[rows, 2:3]))
        bank_read[b] = (a,)

    def queries_of_index():
        to_features("iq", 0)
        to_features("iq", 2)

    def keys_to_features():
        wait(T, *heads)
        wait(A, *heads)
        to_features("ik", 0)
        to_features("k", 0)

    feature_stage(c, None, 1, lambda n: d["w_rnn"][n], c.xT, conv, dve, drained[2] + drained[3], 6,
                  hooks={1: [queries_of_index], 3: [keys_to_features]})
    conv_in = dve.now()

    acc = {}

    def index_scores(heads_of_index):
        if 0 in heads_of_index:
            wait(T, act.now())
        for hd in heads_of_index:
            b, bank = small_bank()
            for q, cols in enumerate(QCOLS):
                m = T.matmul(bank[:, cols], iqT[:, hd // 2, q * P:(q + 1) * P], ikz[:, hd % 2, 0:(q + 1) * P],
                             start=q == 0, stop=True, skip_group_check=True)
            scored = pe(m)
            wait(A, scored)
            if hd >= 2:
                wait(A, acc[hd - 2])
            a = act(A.activation(rl[:, hd % 2, :], bank[:, 0:3 * P], ACT.Relu))
            bank_read[b] = (a,)
            wait(V, a)
            if hd:
                wait(V, acc[hd - 1])
            for q, cols in enumerate(QCOLS):
                o, w = isc[:, q, 0:(q + 1) * P], ikw[:, q, 2 * ID + hd:2 * ID + hd + 1]
                if hd == 0:
                    acc[hd] = dve(V.tensor_scalar(o, rl[:, 0, cols], w, None, ALU.mult))
                else:
                    acc[hd] = dve(V.scalar_tensor_tensor(o, rl[:, hd % 2, cols], w, o, ALU.mult, ALU.add))

    gates = {}

    def recurrence_gates(tiles):
        wait(T, conv_in, (s_rgw, 16))
        for n in tiles:
            b, bank = small_bank()
            T.matmul(bank[:, 0:S], rgw[:, 0, n, :], xc[:, n, :], start=True, stop=True, skip_group_check=True)
            gated = pe(T.matmul(bank[:, S:2 * S], rgw[:, 1, n, :], xc[:, n, :], start=False, stop=True, skip_group_check=True))
            wait(A, gated)
            A.activation(rr[:, n, :], bank[:, 0:S], ACT.Sigmoid, bias=vec["rg_ba_2"][:, n:n + 1])
            a = act(A.activation(ig[:, n, :], bank[:, S:2 * S], ACT.Sigmoid, bias=vec["rg_bx_2"][:, n:n + 1]))
            bank_read[b] = (a,)
        gates["in"], gates["made"] = a, gated

    done_ = {}

    def selection():
        widths = [(q, (q + 1) * P) for q in range(NT)]
        wait(V, acc[IH - 1])
        for q, n in widths:
            a = dve(V.tensor_scalar(isc[:, q, 0:n], isc[:, q, 0:n], IDX_SCALE, None, ALU.mult))
        wait(V, a)
        for q, n in widths:
            V.memset(isc[0:CH, q, n - CH:n], -1.0e30)
        a = dve(V.memset(ones[:, :], 1.0))
        for step in range(TOPK // 8):
            src = isc if step == 0 else wk
            wait(V, a)
            for q, n in widths:
                a = dve(V.max(m8[:, q, :], src[:, q, 0:n]))
            yield
            if step < TOPK // 8 - 1:
                wait(V, a)
                for q, n in widths:
                    a = dve(V.match_replace(out=wk[:, q, 0:n], in_to_replace=m8[:, q, :], in_values=src[:, q, 0:n],
                                            imm_value=-3.0e38))
                yield
        wait(V, a)
        for q, n in widths:
            V.tensor_scalar(eqs[:, q, 0:n], isc[:, q, 0:n], m8[:, q, 7:8], None, ALU.is_equal)
            a = dve(V.tensor_scalar(wk[:, q, 0:n], isc[:, q, 0:n], m8[:, q, 7:8], None, ALU.is_gt, ALU.add,
                                    accum_out=cnt[:, q:q + 1]))
        wait(V, a)
        dve(V.tensor_scalar(cnt[:, :], cnt[:, :], -1.0, float(TOPK), ALU.mult, ALU.add))
        for q, n in widths:
            a = dve(V.tensor_tensor_scan(cum[:, q, 0:n], ones[:, 0:n], eqs[:, q, 0:n], 0.0, ALU.mult, ALU.add))
        yield
        wait(V, a)
        for q, n in widths:
            a = dve(V.scalar_tensor_tensor(eqs[:, q, 0:n], cum[:, q, 0:n], cnt[:, q:q + 1], eqs[:, q, 0:n],
                                           ALU.is_le, ALU.mult))
        wait(V, a)
        for q, n in widths:
            a = dve(V.tensor_tensor(wk[:, q, 0:n], wk[:, q, 0:n], eqs[:, q, 0:n], ALU.add))
        wait(V, a)
        for q, n in widths:
            done_["selected"] = dve(V.tensor_scalar(isc[:, q, 0:n], wk[:, q, 0:n], 1.0e30, -1.0e30, ALU.mult, ALU.add))
        yield

    def recurrence():
        wait(G, gates["in"], conv_in)
        ix = pool(G.tensor_tensor(ig[:, :, :], ig[:, :, :], xc[:, :, :], ALU.mult))
        wait(A, gates["in"])
        for n in range(KD):
            exps = act(A.activation(aa[:, n, :], rr[:, n, :], ACT.Exp, scale=nlam8[:, n:n + 1]))
        yield
        wait(A, exps)
        for n in range(KD):
            tanhs = act(A.activation(rr[:, n, :], rr[:, n, :], ACT.Tanh, scale=hlam8[:, n:n + 1]))
        yield
        wait(A, tanhs)
        root = act(A.activation(rr[:, :, :], rr[:, :, :], ACT.Sqrt))
        wait(V, exps, ix)
        a = dve(V.scalar_tensor_tensor(ig[:, :, :], aa[:, :, :], 1.0, ig[:, :, :], ALU.add, ALU.mult))
        wait(G, root, a)
        u = pool(G.tensor_tensor(ig[:, :, :], ig[:, :, :], rr[:, :, :], ALU.mult))
        yield
        wait(V, u, exps)
        for n in range(KD):
            scanned = dve(V.tensor_tensor_scan(rr[:, n, :], aa[:, n, :], ig[:, n, :], 0.0, ALU.mult, ALU.add))
            if n % 2:
                yield
        done_["scanned"] = scanned
        wait(G, scanned, done_["gelu"])
        y = pool(G.tensor_tensor(gel[:, :, :], rr[:, :, :], gel[:, :, :], ALU.mult))
        yield
        wait(A, y, scanned)
        rounded = act(A.activation(yT[0][:, :, :], gel[:, :, :], ACT.Copy))
        wait(G, rounded)
        done_["y"] = pool(G.tensor_tensor(yT[1][:, :, :], gel[:, :, :], yT[0][:, :, :].bitcast(F32), ALU.subtract))
        yield

    def scores(g):
        wait(T, *(done_["scores_free"] + done_["pT_banks_free"] if g else everything()))
        for r in range(4):
            tile = 4 * (g // 2) + r
            T.matmul(ps[:, 4, r * P:(r + 1) * P], qT[:, tile, 0:P], kz[:, g, 0:P], start=r == 0, stop=True,
                     skip_group_check=True)
            m = T.matmul(ps[:, 5 + r // 2, (r % 2) * S:(r % 2 + 1) * S], qT[:, tile, P:2 * P], kz[:, g, :], start=r % 2 == 0,
                         stop=True, skip_group_check=True)
        scored = pe(m)
        wait(V, scored, done_["selected"], *done_.get("p_free", ()))
        q0, q1 = p[:, :, 0:P], p[:, :, P:3 * P]
        bias = lambda q, n, heads: isc[:, q:q + 1, 0:n].broadcast_to([P, heads, n])
        dve(V.scalar_tensor_tensor(q0, ps[:, 4, :].rearrange("p (r n) -> p r n", r=4), SCALE_C, bias(0, P, 4),
                                   ALU.mult, ALU.add))
        for half in range(2):
            a = dve(V.scalar_tensor_tensor(q1[:, 2 * half:2 * half + 2, :], pair(ps[:, 5 + half, :]), SCALE_C,
                                           bias(1, S, 2), ALU.mult, ALU.add))
        done_["scores_free"] = (a,)
        wait(V, a)
        V.tensor_reduce(smx[:, 0, :], q0, AX.X, ALU.max)
        a = dve(V.tensor_reduce(smx[:, 1, :], q1, AX.X, ALU.max))
        wait(V, a)
        a = dve(V.tensor_scalar(smx[:, :, :], smx[:, :, :], -1.0, None, ALU.mult))
        wait(A, a, *done_.get("ssum_free", ()))
        for r in range(4):
            for q, cols in enumerate(QCOLS):
                a = act(A.activation(p[:, r, cols], p[:, r, cols], ACT.Exp, bias=smx[:, q, r:r + 1],
                                     accum_out=ssum[:, q, r:r + 1]))
        done_["p"] = a

    def turn(g):
        for r in range(4):
            b = ps[:, 4 + r % 3, :]
            wait(T, done_["p"], *done_["scores_free"])
            if r == 3:
                wait(T, *done_["first_pT"])
            for n in range(3):
                m = T.transpose(b[:, n * P:(n + 1) * P], p[:, r, n * P:(n + 1) * P], c.ident[:, :])
            turned = pe(m)
            wait(A, turned, *done_.get("pT_free", ()))
            a = act(A.activation(pT[:, r, :], b[:, 0:3 * P], ACT.Copy))
            if r == 0:
                done_["first_pT"] = (a,)
        done_["p_free"] = (turned,)
        done_["pT_banks_free"] = done_["pT"] = (a,)

    def values(g):
        wait(T, *done_["pT"], *done_.get("o_free", ()))
        for q in range(NT):
            for r in range(4):
                o = ps[:, 7, (4 * q + r) * DC:(4 * q + r + 1) * DC]
                for k in range(q + 1):
                    m = T.matmul(o, pT[:, r, (q + k) * P:(q + k + 1) * P], v[:, k, g * DC:(g + 1) * DC],
                                 start=q == 0 and r == 0, stop=k == q, skip_group_check=True)
        done = pe(m)
        done_["pT_free"] = (done,)
        wait(V, done_["p"])
        a = dve(V.reciprocal(smx[:, :, :], ssum[:, :, :]))
        wait(V, a, done)
        done_["ssum_free"] = (a,)
        for q in range(NT):
            a = dve(V.tensor_tensor(ya[:, q, g * 4 * DC:(g + 1) * 4 * DC].rearrange("p (r n) -> p r n", r=4),
                                    ps[:, 7, 4 * q * DC:4 * (q + 1) * DC].rearrange("p (r n) -> p r n", r=4),
                                    smx[:, q, :].unsqueeze(2).broadcast_to([P, 4, DC]), ALU.mult))
        done_["o_free"] = (a,)

    chains = {"selection": selection(), "recurrence": recurrence()}

    def steps(name, n):
        for _ in range(n):
            next(chains[name], None)

    interludes = {0: [lambda t0=t0: to_features("q", t0) for t0 in range(0, KD, 2)]
                  + [lambda: recurrence_gates(range(KD))],
                  1: [lambda: index_scores(range(0, 4))], 2: [lambda: index_scores(range(4, IH))]}
    plan = {1: (0, 1), 2: (0, 1), 3: (4, 1), 4: (4, 2), 5: (4, 2), 6: (4, 3), 7: (4, 9)}
    gb = vec["gate_b_2"]
    bank_free = {}
    for n in range(16):
        kind, t0 = n // 4, 2 * (n % 4)
        c.load(n, (d["w_rnn"][4 + n] if kind == 0 else d["w_gates"][n - 4] if kind < 3 else d["w_o_rnn"][n - 12]))
        c.split(n + AHEAD)
        for interlude in interludes.get(n, ()):
            interlude()
        for name, count in zip(chains, plan.get(n, (0, 0))):
            steps(name, count)
        if kind == 3:
            wait(T, done_["y"])
        bank = ps[:, n % 4, :]
        wait(T, *(bank_free[n - 4] if n >= 4 else (conv_in,)))
        done = c.feature_major(n, yT if kind == 3 else c.xT, 0, KD, S, HALVES(bank), True, True)
        if kind == 0:
            wait(A, done)
            a = act(A.activation(gel[:, t0:t0 + 2, :], pair(bank), ACT.Gelu_apprx_tanh))
            done_["gelu"] = a
        elif kind < 3:
            wait(A, done)
            if kind == 2:
                wait(A, gates["made"])
            for k in range(2):
                a = act(A.activation((g0, g1)[kind - 1][:, t0 + k, :], bank[:, k * S:(k + 1) * S], ACT.Sigmoid,
                                     bias=gb[:, 8 * (kind - 1) + t0 + k:8 * (kind - 1) + t0 + k + 1]))
        else:
            wait(V, done, act.now())
            a = dve(V.tensor_tensor(g0[:, t0:t0 + 2, :], pair(bank), g0[:, t0:t0 + 2, :], ALU.mult))
        bank_free[n] = (a,)
        if n >= 9 and n % 2:
            values((n - 9) // 2)
        if 7 <= n < 15 and n % 2:
            scores((n - 7) // 2)
        if n >= 8 and n % 2 == 0:
            turn((n - 8) // 2)
    c.advance(16)

    wait(A, c.w_used_now())
    wait(V, c.w_used_now())
    turned = transpose_in(c, lambda t, k: ya[:, t, k * P:(k + 1) * P], KD, whole(zT[0]), whole(zT[1]), everything())
    mixed = {}

    def mix(n, bank, done, j):
        t = slice(2 * n, 2 * n + 2)
        wait(V, done)
        a = dve(V.tensor_tensor(g1[:, t, :], bank, g1[:, t, :], ALU.mult))
        wait(G, a)
        a = pool(G.tensor_tensor(g0[:, t, :], g0[:, t, :], g1[:, t, :], ALU.add))
        wait(A, a)
        a = act(A.activation(c.xT[0][:, t, :], g0[:, t, :], ACT.Copy))
        wait(G, a)
        mixed[n] = pool(G.tensor_tensor(c.xT[1][:, t, :], g0[:, t, :], c.xT[0][:, t, :].bitcast(F32), ALU.subtract))

    feature_stage(c, None, 1, lambda n: d["w_o_attn"][n], zT, mix, dve, bank_free[15], ready=turned)

    wait(T, *done_["o_free"])
    added = []
    for half in range(2):
        for b in range(2):
            j = 2 * half + b
            block = [ps[:, 4 + 2 * b + t, :] for t in range(NT)]
            c.load(j, d["w_out"][b, half])
            c.split(j + AHEAD)
            wait(T, mixed[2 * half], mixed[2 * half + 1])
            done = c.token_major(j, c.xT, 4 * half, 4, 512, block, half == 0, half == 1)
            if half == 1:
                wait(V, done)
                for t in range(NT):
                    r = c.res[:, t, b * 512:(b + 1) * 512]
                    a = dve(V.tensor_tensor(r, r, block[t], ALU.add))
                added.append((a,))
    c.advance(4)

    transposed = transpose_in(c, lambda t, k: c.res[:, t, k * P:(k + 1) * P], KD, whole(c.xT[0]), whole(c.xT[1]),
                              [added[k // 2] for k in range(4)], banks=(0, 1, 2, 3), weight=vec["norm2_w_2"])
    wait(A, *added[0], *added[1])
    for t in range(NT):
        squared = act(A.activation(junk2[:, t, :], c.res[:, t, :], ACT.Square, accum_out=squares[:, 0, t:t + 1]))
    wait(V, squared)
    a = dve(V.tensor_scalar(squares[:, 1, :], squares[:, 0, :], 1.0 / D, 1e-6, ALU.mult, ALU.add))
    wait(V, a)
    a = dve(V.reciprocal(c.rs[:, :], squares[:, 1, :]))

    def relu2(n, bank, done, j):
        at = bass.ds(n * 2, 2)
        wait(A, done, pool.now(3))
        relu = act(A.activation(fr[:, j, :, :], bank, ACT.Relu))
        wait(V, relu)
        square = dve(V.tensor_tensor(fr[:, j, :, :], fr[:, j, :, :], fr[:, j, :, :], ALU.mult))
        wait(A, square)
        hi = act(A.activation(fT[0][:, at, :], fr[:, j, :, :], ACT.Copy))
        wait(G, hi)
        pool(G.tensor_tensor(fT[1][:, at, :], fr[:, j, :, :], fT[0][:, at, :].bitcast(F32), ALU.subtract))

    wait(A, a)
    feature_stage(c, "feed_forward", 4, lambda n: d["w_ff_in"][bass.ds(n, 1)], c.xT, relu2, act, (), 2, ready=transposed)

    last_tiles = (dve.now(), act.now(), pool.now())
    c.last_unit = 16
    for b in range(2):
        block = [ps[:, 4 + 2 * b + t, :] for t in range(NT)]
        for q in range(8):
            j = 8 * b + q
            c.load(j, d["w_ff_out"][b, q])
            c.split(j + AHEAD)
            wait(T, *(last_tiles if j == 6 else (pool.now(2),)))
            done = c.token_major(j, fT, 4 * q, 4, 512, block, q == 0, q == 7)
        wait(V, done)
        for t in range(NT):
            r = c.res[:, t, b * 512:(b + 1) * 512]
            a = dve(V.scalar_tensor_tensor(r, block[t], c.rs[:, t:t + 1], r, ALU.mult, ALU.add))
            queue = c.SP if b else c.G
            wait(queue, a)
            queue.dma_start(out[0, t * P:(t + 1) * P, b * 512:(b + 1) * 512], r).then_inc(c.s_out if b else s_out0, 16)
    c.SP.wait_ge(c.s_out, 32)
    G.wait_ge(s_out0, 32)
    yield


LOOPS = {
    "retention": dict(pe=8, dve=38, act=16, pool=4),
        "feed_forward": dict(pe=0, dve=4, act=8, pool=4),
    "attention": dict(pe=14, dve=32, act=20, pool=6),
}


def build(nc, d, out, stop=None):
    c = Core(nc)
    c.ps = nc.alloc_psum_tensor("ps", [P, 8, 512], F32)
    c.raw = [c.place(f"w_raw{r}", [P, SLOT]) for r in range(RING)]
    c.hi = c.place("w_hi_ring", [P, RING, SLOT], F32R)
    c.lo = c.place("w_lo_ring", [P, RING, SLOT], F32R)
    c.res = c.place("res", [P, NT, D])
    c.xT = [c.place("xT_hi", [P, KD, S], F32R), c.place("xT_lo", [P, KD, S], F32R)]
    c.st = c.place("st", [P, NT, 2, 6])
    c.mv = c.place("mv", [P, NT, 2])
    norms = c.place("norms", [P, 3, NT])
    c.rs, c.tmp = norms[:, 0, :], [norms[:, 1 + n, :] for n in range(2)]
    c.s_x, c.s_out = (nc.alloc_semaphore(n) for n in ("s_x", "s_out"))

    c.A.dma_start(c.res[:, :, :], d["x"][0].rearrange("(t p) n -> p t n", p=P)).then_inc(c.s_x, 16)
    c.ident, t_ident = table(c, c.A, "ident", d["k_ident"], [P, P])
    wait(c.T, (c.s_x, 16), t_ident)
    wait(c.V, (c.s_x, 16))
    c.phase = c.top
    transposed = transpose_in(c, lambda t, k: c.res[:, t, k * P:(k + 1) * P], KD, whole(c.xT[0]), whole(c.xT[1]), ())
    for j in range(AHEAD):
        c.split(j)
    oT, after, hooks = retention_layer(c, d, transposed)
    lnw = load_ln(c, 0, d, c.top, ())
    c.last_unit = 8 if stop == 1 else None
    tables = []
    hooks[7] = [lambda: tables.append(latent_tables(c, d))]
    stats = out_projection(c, d["a_w_out"], oT, ALPHA, after, hooks)
    normed = layer_norm(c, lnw, (stats,))
    if stop == 1:
        return store(c, out, normed)
    transposed = transpose_in(c, lambda t, k: c.res[:, t, k * P:(k + 1) * P], KD, whole(c.xT[0]), whole(c.xT[1]),
                              [normed[k // 2] for k in range(4)])
    oT, after, hooks = latent_attention_layer(c, d, transposed, tables[0])
    c.last_unit = 8 if stop == 2 else None
    hybrid = hybrid_layer(c, d, out)
    lnw = []
    hooks[5] = [lambda: lnw.append(load_ln(c, 1, d, c.phase + 2 * 4 * HB * S, (c.pe.now(), c.dve.now()))),
                lambda: next(hybrid)]
    hooks[6].append(lambda: next(hybrid))
    stats = out_projection(c, d["b_w_out"], oT, ALPHA, after, hooks)
    normed = layer_norm(c, lnw[0], (stats,))
    if stop == 2:
        return store(c, out, normed)
    hybrid.send(normed)


def store(c, out, after):
    wait(c.SP, *after[0], *after[1])
    c.SP.dma_start(out[0].rearrange("(t p) n -> p t n", p=P), c.res[:, :, :]).then_inc(c.s_out, 16)
    c.SP.wait_ge(c.s_out, 16)


COLUMNS = ("b_q_norm", "kv_norm", "norm1_w_2", "rg_ba_2", "rg_bx_2", "rg_lambda_2", "conv_b_2", "gate_b_2", "norm2_w_2")
COLUMNS_C = (("norm1_w_2", 8), ("norm2_w_2", 8), ("rg_ba_2", 8), ("rg_bx_2", 8), ("rg_lambda_2", 8), ("conv_b_2", 8),
             ("conv_w_2", 32), ("gate_b_2", 16), ("head_norms", 3))


def units(w, k, n):
    K, N = w.shape
    w = w.reshape(K // (P * k), k, P, N // n, n).transpose(3, 0, 2, 1, 4)
    return np.ascontiguousarray(w).reshape(N // n, K // (P * k), P, k * n)


def layout(inputs):
    out = {name: np.asarray(a) for name, a in inputs.items()}
    for name in COLUMNS:
        out[name] = np.ascontiguousarray(out[name].reshape(-1, P).T)
    w = out["a_w_in"][0]
    at = np.cumsum([HA * DKA, HA * DKA, WA])
    q, k, v, g = np.split(w, at, 1)
    out["a_w_in"] = np.concatenate([units(q, KD, DKA), units(k, KD, DKA), units(v, 4, DVA), units(g, 4, DVA)], 1)
    out["a_w_out"] = units(out["a_w_out"][0], 4, 512)
    w = out.pop("b_w_in")[0]
    out["b_w_qlat"] = units(w[:, :QL], 4, 384)
    out["b_w_gate"] = units(w[:, QL:], KD, 2 * VH)[:, 0]
    w = out["kv_w_down"]
    out["kv_w_down"] = units(np.concatenate([w, w[:, KVL:]], 1), 2, KVL + 2 * ROPE)
    w = out["b_w_uq"][0].reshape(QL, HB // 2, 2, NOPE + ROPE)
    w = np.concatenate([w[..., :NOPE].reshape(QL, HB // 2, -1), w[..., NOPE:].reshape(QL, HB // 2, -1)], 2)
    out["b_w_uq"] = units(w.reshape(QL, -1), 3, 2 * (NOPE + ROPE))
    w = out["kv_w_up"].reshape(KVL, HB // 2, 2, NOPE + VH)
    w = np.concatenate([w[..., :NOPE].reshape(KVL, HB // 2, -1), w[..., NOPE:].reshape(KVL, HB // 2, -1)], 2)
    out["kv_w_up"] = units(w.reshape(KVL, -1), 4, 512)[:, 0]
    out["b_w_out"] = units(out["b_w_out"][0], 4, 512)

    w = out.pop("w_in_2")[0]
    rnn_x, rnn_g, q, k, v, iq, ik, iw, gates = np.split(w, np.cumsum([DR, DR, D, 256, 256, IH * ID, ID, IH]), 1)
    group = HC // HKV
    order = [(t // group * 2 + half) * group + t % group for t in range(HC // 2) for half in range(2)]
    q = q.reshape(D, HC, DC)[:, order].reshape(D, D)
    out["w_qkvi"] = units(np.concatenate([q, k, v, iq], 1), 4, 512)
    out["w_ikw"] = units(np.concatenate([ik, ik, iw], 1), KD, 2 * ID + IH)[0, 0]
    out["w_rnn"] = units(np.concatenate([rnn_x, rnn_g], 1), KD, S)[:, 0]
    out["w_gates"] = units(gates, KD, S)[:, 0]
    for name in ("w_o_rnn", "w_o_attn"):
        out[name] = units(out.pop(name + "_2")[0], KD, S)[:, 0]
    out["w_out"] = units(out.pop("w_out_2")[0], 4, 512)
    out["w_ff_in"] = units(out.pop("w_ff_in_2")[0], KD, S)[:, 0]
    out["w_ff_out"] = units(out.pop("w_ff_out_2")[0], 4, 512)
    out["conv_w_2"] = np.ascontiguousarray(out["conv_w_2"][0].reshape(4, KD, P).transpose(2, 0, 1)).reshape(P, 4 * KD)
    norms = [np.tile(out.pop(n)[0], 2) for n in ("q_norm_w_2", "k_norm_w_2", "idx_k_norm_w_2")]
    out["head_norms"] = np.ascontiguousarray(np.stack(norms, 1))
    out["columns"] = np.ascontiguousarray(np.concatenate([out.pop(name) for name, _ in COLUMNS_C], 1))
    wa, wx = out.pop("rg_wa_2")[0], out.pop("rg_wx_2")[0]
    rg = np.zeros((P, 2, KD, P), wa.dtype)
    for n, w in enumerate((wa, wx)):
        for half in range(2):
            rows = slice(64 * half, 64 * half + 64)
            rg[rows, n, :, rows] = w[half::2].transpose(1, 0, 2)
    out["rg_w"] = rg.reshape(P, -1)
    return out


def rope_angles(dim):
    f = np.float32
    inv = (f(10000.0) ** (-np.arange(dim // 2, dtype=f) / f(dim // 2))).astype(f)
    return np.arange(S, dtype=f)[None, :] * inv[:, None]


def constants():
    f = np.float32
    ang = rope_angles(DKA)
    out = {"k_ident": np.eye(P, dtype=f), "k_ropeA": np.stack([np.cos(ang), np.sin(ang)], 1).astype(f)}
    lg = np.log1p(-np.exp2(-5.0 - np.arange(HA)))
    e, n = np.arange(P)[:, None], np.arange(S)[None, :]
    m = np.where(n >= e, np.exp(np.maximum(n - e, 0)[None] * lg[:, None, None]), 0.0) / np.sqrt(DKA)
    m = np.concatenate([m, m[:, :, 0:P]], 2)
    out["k_decay"] = np.ascontiguousarray(m.transpose(1, 0, 2)).astype(f)
    ang = np.tile(rope_angles(ROPE), (2 * P // ROPE, 1))
    out["k_ropeB"] = np.stack([np.cos(ang), np.sin(ang)], 1).astype(f)
    rot = np.zeros((P, P), f)
    for r in range(P):
        half = ROPE // 2
        if r % ROPE < half:
            rot[r + half, r] = -1.0
        else:
            rot[r - half, r] = 1.0
    out["k_rotB"] = rot
    causal = np.where(np.arange(P)[None, :] <= np.arange(P)[:, None], 0.0, -1.0e30).astype(f)
    out["k_maskB"] = np.concatenate([causal, np.zeros((P, P), f), causal], 1)
    return out


def kernel(**inputs):
    import concourse.bacc as bacc
    from concourse.bass_utils import run_bass_kernel_spmd

    arrays = {**layout(inputs), **constants()}
    nc = bacc.Bacc("TRN2", target_bir_lowering=False, num_devices=1)
    d = {n: nc.dram_tensor("in_" + n, a.shape, mybir.dt.from_np(a.dtype), kind="ExternalInput").ap()
         for n, a in arrays.items()}
    out = nc.dram_tensor("out", (1, S, D), F32, kind="ExternalOutput").ap()
    build(nc, d, out)
    r = run_bass_kernel_spmd(nc, [{"in_" + n: a for n, a in arrays.items()}], core_ids=[0])
    return r.results[0]["out"]
```

```python
import numpy as np
import concourse.bass as bass
from concourse import mybir

F32 = mybir.dt.float32
F32R = mybir.dt.float32r
ACT = mybir.ActivationFunctionType
ALU = mybir.AluOpType
AX = mybir.AxisListType

P = 128
D = 1024
S = 256
NT = S // P
KD = D // P

HA, DKA, DVA = 4, 256, 512
WA = HA * DVA
HB, NOPE, ROPE, VH = 16, 128, 64, 128
QL, KVL = 768, 512
SCALE_B = float(NOPE + ROPE) ** -0.5
ALPHA = 4.0 ** 0.25
DR, HC, HKV, DC = 1024, 16, 4, 64
IH, ID = 8, 64
TOPK = 64
CH = 64
DFF = 4096
SCALE_C = float(DC) ** -0.5
IDX_SCALE = (float(ID) ** -0.5) * (float(IH) ** -0.5)

RING = 4
SLOT = 2048
WARM = (20, 36)
AHEAD = 3


class Signal:

    FIRST = 64

    def __init__(self, nc, name, engine):
        self.sem = nc.alloc_semaphore(name)
        engine.sem_inc(self.sem, self.FIRST)
        self.base, self.i, self.per, self.k, self.serial = self.FIRST, 0, 0, 0, 0

    def __call__(self, instruction):
        instruction.then_inc(self.sem, 1)
        self.k += 1
        self.serial += 1
        return self.now()

    def now(self, back=0):
        return (self.sem, self.base + self.i * self.per + (self.k - back), self, self.serial - back)

    def enter(self, i, per):
        self.base, self.k = self.base + self.k, 0
        self.i, self.per = i, per

    def leave(self, count):
        if self.k != self.per:
            raise ValueError(f"a loop's body signals {self.k}, {self.per} were declared")
        self.base, self.i, self.per, self.k = self.base + count * self.per, 0, 0, 0


def wait(engine, *tokens):
    for token in tokens:
        engine.wait_ge(token[0], token[1])


class Core:

    def __init__(self, nc):
        self.nc = nc
        self.T, self.V, self.A, self.G, self.SP = nc.tensor, nc.vector, nc.scalar, nc.gpsimd, nc.sync
        self.pe, self.dve, self.act, self.pool = (
            Signal(nc, n, e) for n, e in (("pe", self.T), ("dve", self.V), ("act", self.A), ("pool", self.G)))
        self.landed = [nc.alloc_semaphore(f"w_landed{r}") for r in range(RING)]
        self.w_hi, self.w_lo, self.w_used = (nc.alloc_semaphore(n) for n in ("w_hi", "w_lo", "w_used"))
        self.unit0, self.it, self.upi = 0, 0, 0
        self.V.sem_inc(self.w_lo, RING)
        self.T.sem_inc(self.w_used, RING)
        self.last_unit = None
        self.on_pool = {}
        self.top = (nc.sbuf_base + 31) // 32 * 32
        self.at = {}

    def place(self, name, shape, dtype=F32, at=None):
        at = self.top if at is None else at
        size = int(np.prod(shape[1:])) * 4
        t = self.nc.alloc_sbuf_tensor_at(name, shape, dtype, offset=at)
        self.top = at + (size + 31) // 32 * 32
        if self.top > self.nc.sbuf_usable_end:
            raise ValueError(f"{name} ends {self.top - self.nc.sbuf_usable_end} bytes after the SBUF")
        self.at[name] = at
        return t

    def loop(self, name, count, upi):
        return _Loop(self, name, count, upi)

    def unit(self, j):
        return self.unit0 + self.it * self.upi + j

    def load(self, j, src):
        slot = j % RING
        if len(src.shape) == 3:
            src = src.rearrange("a p n -> (a p) n")
        self.SP.wait_ge(self.w_lo, self.unit(j) + 1)
        if self.upi == 0 and self.unit(j) - RING in self.on_pool:
            wait(self.SP, self.on_pool[self.unit(j) - RING])
        self.SP.dma_start(self.raw[slot][:, 0:src.shape[-1]], src).then_inc(self.landed[slot], 16)

    def split(self, j, on_pool=False):
        if self.last_unit is not None and j >= self.last_unit:
            return
        slot = j % RING
        u = self.unit(j)
        self.A.wait_ge(self.landed[slot], 16 * (self.unit0 // RING + 1 + j // RING) + self.it * (16 * (self.upi // RING)))
        self.A.wait_ge(self.w_used, u + 1)
        self.A.activation(self.hi[:, slot, :], self.raw[slot][:, :], ACT.Copy).then_inc(self.w_hi, 1)
        engine = self.G if on_pool else self.V
        engine.wait_ge(self.w_hi, u + 1)
        m = engine.tensor_tensor(self.lo[:, slot, :], self.raw[slot][:, :], self.hi[:, slot, :].bitcast(F32),
                                 ALU.subtract)
        if on_pool:
            self.on_pool[u] = self.pool(m)
            self.V.sem_inc(self.w_lo, 1)
        else:
            m.then_inc(self.w_lo, 1)

    def advance(self, units):
        self.unit0 += units

    def used(self, j):
        return (self.w_used, RING + self.unit(j) + 1)

    def w_used_now(self):
        return (self.w_used, RING + self.unit(0))

    def use(self, j):
        self.T.wait_ge(self.w_lo, RING + self.unit(j) + 1)
        if self.upi == 0 and self.unit(j) in self.on_pool:
            wait(self.T, self.on_pool[self.unit(j)])
        return self.hi[:, j % RING, :], self.lo[:, j % RING, :]

    def mm3(self, out, lhs, rhs, start, stop):
        (lh, ll), (rh, rl) = lhs, rhs
        self.T.matmul(out, lh, rh, start=start, stop=False, skip_group_check=True)
        self.T.matmul(out, lh, rl, start=False, stop=False, skip_group_check=True)
        m = self.T.matmul(out, ll, rh, start=False, stop=stop, skip_group_check=True)
        return m

    def token_major(self, j, xT, k0, nk, cols, outs, first, last, ready=()):
        wh, wl = (w.rearrange("p (k n) -> p k n", k=nk) if nk * cols == SLOT
                  else w[:, 0:nk * cols].rearrange("p (k n) -> p k n", k=nk) for w in self.use(j))
        for k in range(nk):
            if ready and k % 2 == 0:
                wait(self.T, ready[(k0 + k) // 2])
            for t in range(NT):
                x = tuple(z[:, k0 + k, t * P:(t + 1) * P] for z in xT)
                m = self.mm3(outs[t], x, (wh[:, k, :], wl[:, k, :]), first and k == 0, last and k == nk - 1)
        m.then_inc(self.w_used, 1)
        return self.used(j)

    def feature_major(self, j, xT, k0, nk, cols, outs, first, last, ready=()):
        wh, wl = (w[:, 0:nk * cols].rearrange("p (k n) -> p k n", k=nk) for w in self.use(j))
        for part in (range(0, nk // 2), range(nk // 2, nk)):
            for c, out in enumerate(outs):
                for k in part:
                    if ready and c == 0 and k % 2 == 0:
                        wait(self.T, ready[(k0 + k) // 2])
                    w = tuple(z[:, k, c * P:(c + 1) * P] for z in (wh, wl))
                    x = tuple(z[:, k0 + k, :] for z in xT)
                    m = self.mm3(out, w, x, first and k == 0 and c % 2 == 0, last and k == nk - 1)
        m.then_inc(self.w_used, 1)
        return self.used(j)


def keep_warm(c, products, bank=7):
    for _ in range(products):
        c.T.matmul(c.ps[:, bank, :], c.xT[0][:, 0, 0:P], c.xT[0][:, 0:2, :].rearrange("p k s -> p (k s)"),
                   start=True, stop=True, skip_group_check=True)


class _Loop:
    def __init__(self, core, name, count, upi):
        self.c, self.name, self.count, self.upi, self.per = core, name, count, upi, LOOPS[name]
        nc = core.nc
        engines = [e.engine for e in (nc.sync, nc.scalar, nc.vector, nc.tensor, nc.gpsimd)]
        self.fori = nc.Fori(0, count, engines=engines)

    def __enter__(self):
        c = self.c
        i = self.fori.__enter__()
        for n, k in self.per.items():
            {"pe": c.pe, "dve": c.dve, "act": c.act, "pool": c.pool}[n].enter(i, k)
        c.it, c.upi = i, self.upi
        return i

    def __exit__(self, *e):
        c = self.c
        self.fori.__exit__(*e)
        if e[0] is not None:
            return False
        got = {n: s.k for n, s in (("pe", c.pe), ("dve", c.dve), ("act", c.act), ("pool", c.pool))}
        if got != self.per:
            raise ValueError(f"LOOPS[{self.name!r}] = {got}")
        for s in (c.pe, c.dve, c.act, c.pool):
            s.leave(self.count)
        c.unit0, c.it, c.upi = c.unit0 + self.count * self.upi, 0, 0


def table(c, queue, name, src, shape):
    t = c.place(name, shape)
    sem = c.nc.alloc_semaphore("s_" + name)
    queue.dma_start(t[tuple(slice(None) for _ in shape)], src).then_inc(sem, 16)
    return t, (sem, 16)


def transpose_in(c, src, nk, hi, lo, after, banks=(4, 5, 6, 7), weight=None):
    tokens = []
    for n in range(0, nk, 2):
        b = c.ps[:, banks[n // 2 % len(banks)], :]
        if isinstance(after, list):
            wait(c.T, *after[n // 2])
        elif n == 0:
            wait(c.T, *after)
        if n // 2 >= len(banks):
            wait(c.T, tokens[n // 2 - len(banks)])
        for k in range(2):
            for t in range(NT):
                m = c.T.transpose(b[:, (2 * k + t) * P:(2 * k + t + 1) * P], src(t, n + k), c.ident[:, :])
        turned = c.pe(m)
        wait(c.A, turned)
        if weight is None:
            rounded = c.act(c.A.activation(hi(n, 2), b.rearrange("p (k s) -> p k s", k=2), ACT.Copy))
            wait(c.V, rounded)
            tokens.append(c.dve(c.V.tensor_tensor(lo(n, 2), b.rearrange("p (k s) -> p k s", k=2),
                                                  hi(n, 2).bitcast(F32), ALU.subtract)))
        else:
            for k in range(2):
                part = b[:, k * S:(k + 1) * S]
                rounded = c.act(c.A.activation(hi(n + k, 1)[:, 0, :], part, ACT.Copy, scale=weight[:, n + k:n + k + 1]))
            wait(c.V, rounded)
            for k in range(2):
                part = b[:, k * S:(k + 1) * S]
                last = c.V.scalar_tensor_tensor(lo(n + k, 1)[:, 0, :], part, weight[:, n + k:n + k + 1],
                                                hi(n + k, 1)[:, 0, :].bitcast(F32), ALU.mult, ALU.subtract)
            tokens.append(c.dve(last))
    return tokens


def whole(t):
    return lambda n, k: t[:, n:n + k, :]


def rsqrt(c, var, out, eps, tmp, scale=1.0, meanwhile=None):
    a = c.dve(c.V.tensor_scalar(tmp[0], var, scale, eps, ALU.mult, ALU.add))
    wait(c.A, a)
    r = c.act(c.A.activation(tmp[1], tmp[0], ACT.Sqrt))
    if meanwhile:
        meanwhile()
    wait(c.V, r)
    a = c.dve(c.V.reciprocal(out, tmp[1]))
    wait(c.V, a)
    a = c.dve(c.V.tensor_tensor(tmp[1], out, out, ALU.mult))
    wait(c.V, a)
    a = c.dve(c.V.tensor_tensor(tmp[1], tmp[1], tmp[0], ALU.mult))
    wait(c.V, a)
    a = c.dve(c.V.tensor_scalar(tmp[1], tmp[1], -0.5, 1.5, ALU.mult, ALU.add))
    wait(c.V, a)
    return c.dve(c.V.tensor_tensor(out, out, tmp[1], ALU.mult))


def retention_layer(c, d, ready):
    oT = [c.place("a_oT_hi", [P, WA // P, S], F32R, at=c.phase), c.place("a_oT_lo", [P, WA // P, S], F32R)]
    raw = c.place("a_qk_raw", [P, 4, S])
    tcos = c.place("a_tcos", [P, 4, S])
    tsin = c.place("a_tsin", [P, 4, S])
    qk = c.place("a_qk", [P, 4, S])
    sm = c.place("a_scores", [P, 3 * P])
    v = c.place("a_v", [P, NT, DVA])
    g = c.place("a_gate", [P, NT, DVA])
    o = c.place("a_o", [P, NT, DVA])
    st = c.place("a_stats", [P, NT, 6])
    mv = c.place("a_mv", [P, NT, 2])
    rs = c.place("a_rs", [P, NT])
    tmp = [c.place(f"a_tmp{n}", [P, NT]) for n in range(2)]
    ropeA, t_rope = table(c, c.A, "ropeA", d["k_ropeA"], [P, 2, S])
    decay, t_decay = table(c, c.A, "decay", d["k_decay"], [P, HA, 3 * P])
    wait(c.V, t_rope, t_decay)
    wait(c.G, t_rope)
    w = d["a_w_in"]
    cos, sin = (ropeA[:, n:n + 1, :].broadcast_to([P, 4, S]) for n in range(2))
    ps = c.ps
    RAW_BACK, SCORES_BACK = 4, 14
    c.pool(c.G.memset(o[:, :, :], 0.0))

    def turn(head, after, banks=(2, 3)):
        wait(c.T, *after)
        for n in range(2):
            b = ps[:, banks[n], :]
            for k in range(2):
                for t in range(NT):
                    m = c.T.transpose(b[:, (2 * k + t) * P:(2 * k + t + 1) * P],
                                      o[:, t, (2 * n + k) * P:(2 * n + k + 1) * P], c.ident[:, :])
            turned = c.pe(m)
            at = bass.ds(head * 4 + 2 * n, 2)
            b = b.rearrange("p (k s) -> p k s", k=2)
            wait(c.A, turned)
            rounded = c.act(c.A.activation(oT[0][:, at, :], b, ACT.Copy))
            wait(c.V, rounded)
            read = c.dve(c.V.tensor_tensor(oT[1][:, at, :], b, oT[0][:, at, :].bitcast(F32), ALU.subtract))
        return turned, read

    with c.loop("retention", 2, 12) as i:
        t0, v0, a0, g0 = c.pe.now(), c.dve.now(), c.act.now(), c.pool.now()
        raw_read, scores_read = c.act.now(RAW_BACK), c.dve.now(SCORES_BACK)
        wait(c.T, raw_read)
        roped = o_in = turned_read = v0
        gate_in, gated, turned = a0, g0, t0
        v_in0, v_in1 = a0, v0
        for a in range(2):
            u = 6 * a
            for n in range(6):
                c.load(u + n, w[bass.ds(i * 2 + a, 1), n])

            wait(c.T, scores_read)
            for half in range(2):
                c.split(u + half + AHEAD)
                done = c.feature_major(u + half, c.xT, 0, KD, DKA, halves(ps[:, half, :]), True, True, ready)
                ready = ()
            wait(c.A, done, roped, gated)
            for n in range(2):
                raw_in = c.act(c.A.activation(raw[:, 2 * n:2 * n + 2, :], ps[:, n, :].rearrange("p (k s) -> p k s", k=2),
                                              ACT.Copy))
            if a == 0:
                turned, turned_read = turn(i * -2 + 3, (v0, a0, g0))
            else:
                turned, turned_read = turn(*todo)
            wait(c.G, raw_in, roped)
            sines = c.pool(c.G.tensor_tensor(tsin[:, :, :], raw[:, :, :], sin, ALU.mult))
            wait(c.V, raw_in)
            cosines = c.dve(c.V.tensor_tensor(tcos[:, :, :], raw[:, :, :], cos, ALU.mult))
            wait(c.V, sines, cosines)
            c.V.tensor_tensor(qk[:, 0::2, :], tcos[:, 0::2, :], tsin[:, 1::2, :], ALU.subtract)
            roped = c.dve(c.V.tensor_tensor(qk[:, 1::2, :], tcos[:, 1::2, :], tsin[:, 0::2, :], ALU.add))

            v_out = [ps[:, 4 + t, :] for t in range(NT)]
            wait(c.T, v_in0, v_in1)
            c.split(u + 2 + AHEAD)
            c.token_major(u + 2, c.xT, 0, 4, 512, v_out, True, False)
            wait(c.T, roped)
            for e, cols in enumerate((slice(0, 2 * P), slice(2 * P, 3 * P))):
                for k in range(2):
                    m = c.T.matmul(ps[:, 0, cols], qk[:, 2 + k, e * P:(e + 1) * P], qk[:, k, e * P:2 * P],
                                   start=e == 0 and k == 0, stop=k == 1, skip_group_check=True)
            scored = c.pe(m)
            c.split(u + 3 + AHEAD)
            wait(c.V, scored)
            scores_read = c.dve(c.V.tensor_tensor(sm[:, :], ps[:, 0, 0:3 * P],
                                                  decay[:, bass.ds(i * 2 + a, 1), :].rearrange("p a n -> p (a n)"), ALU.mult))
            done = c.token_major(u + 3, c.xT, 4, 4, 512, v_out, False, True)
            wait(c.A, done)
            v_in0 = c.act(c.A.activation(v[:, 0, :], v_out[0], ACT.Copy))
            wait(c.V, done)
            v_in1 = c.dve(c.V.tensor_copy(v[:, 1, :], v_out[1]))

            g_out = [ps[:, 2 + t, :] for t in range(NT)]
            c.split(u + 4 + AHEAD)
            wait(c.T, gate_in, turned_read)
            c.token_major(u + 4, c.xT, 0, 4, 512, g_out, True, False)
            wait(c.T, scores_read, v_in0, v_in1, o_in)
            c.T.matmul(ps[:, 6, :], sm[:, 0:P], v[:, 0, :], start=True, stop=True)
            c.T.matmul(ps[:, 7, :], sm[:, P:2 * P], v[:, 0, :], start=True, stop=False)
            inner = c.pe(c.T.matmul(ps[:, 7, :], sm[:, 2 * P:3 * P], v[:, 1, :], start=False, stop=True))
            c.split(u + 5 + AHEAD)
            done = c.token_major(u + 5, c.xT, 4, 4, 512, g_out, False, True)
            wait(c.V, inner)
            for t in range(NT):
                s_ = c.dve(c.V.bn_stats(st[:, t, :], ps[:, 6 + t, :]))
            wait(c.V, s_)
            c.V.memset(tmp[0][:, :], 0.0)
            for t in range(NT):
                s_ = c.dve(c.V.bn_aggr(mv[:, t, :], st[:, t, :]))
            wait(c.V, s_)
            r = rsqrt(c, mv[:, :, 1], rs[:, :], 1e-5, [t[:, :] for t in tmp])
            wait(c.V, r, turned)
            for t in range(NT):
                o_in = c.dve(c.V.tensor_scalar(o[:, t, :], ps[:, 6 + t, :], mv[:, t, 0:1], rs[:, t:t + 1],
                                               ALU.subtract, ALU.mult))
            wait(c.A, done, gated)
            for t in range(NT):
                gate_in = c.act(c.A.activation(g[:, t, :], g_out[t], ACT.Silu))
            wait(c.G, gate_in, o_in)
            gated = c.pool(c.G.tensor_tensor(o[:, 0, :], o[:, 0, :], g[:, 0, :], ALU.mult))
            wait(c.V, gate_in, o_in)
            gated1 = c.dve(c.V.tensor_tensor(o[:, 1, :], o[:, 1, :], g[:, 1, :], ALU.mult))
            todo = (i * 2 + a, (gated, gated1))
            roped = gated1
        if raw_in[3] > c.act.serial - RAW_BACK or scores_read[3] > c.dve.serial - SCORES_BACK:
            raise ValueError("banks 0 and 1 are read later than is waited for")
        last = [(token[2], token[2].serial - token[3]) for token in (raw_in, scores_read, turned_read)]
    after = [signal.now(back) for signal, back in last]
    everything = (c.dve.now(), c.act.now(), c.pool.now())

    def last_head():
        return turn(HA - 1, everything, (4, 5))[1]

    def gates_read():
        wait(c.T, *everything)

    return oT, after, {3: [gates_read], 5: [last_head], 6: [lambda: wait(c.T, c.dve.now())]}


def load_ln(c, layer, d, at, after):
    lnw = c.place(f"lnw{layer}", [P, 2, D], at=at)
    sem = c.nc.alloc_semaphore(f"s_lnw{layer}")
    wait(c.A, *after)
    for n, name in enumerate(("ln_g", "ln_b")):
        c.A.dma_start(lnw[:, n, :], d[name][layer:layer + 1, :].broadcast_to([P, D])).then_inc(sem, 16)
    return lnw, (sem, 32)


def output(c, w, oT, alpha, lnw, after, hooks):
    for n, (b, q) in enumerate([(b, q) for b in range(2) for q in range(3)]):
        c.load(n, w[b, q])
        c.split(n + AHEAD)
        if n == 0:
            wait(c.T, *after)
        for hook in hooks.get(n, ()):
            hook()
        c.token_major(n, oT, 4 * q, 4, 512, [c.ps[:, 2 * b + t, :] for t in range(NT)], q == 0, False)
    for b in range(2):
        c.load(6 + b, w[b, 3])
    c.split(6 + AHEAD)
    for hook in (*hooks.get(6, ()), *hooks.get(7, ())):
        hook()
    last = [[z.rearrange("p (k n) -> p k n", k=4) for z in c.use(6 + b)] for b in range(2)]
    product = {}
    for t in range(NT):
        for b in range(2):
            for k in range(4):
                x = tuple(z[:, 12 + k, t * P:(t + 1) * P] for z in oT)
                m = c.mm3(c.ps[:, 2 * b + t, :], x, tuple(z[:, k, :] for z in last[b]), False, k == 3)
            if t == 0:
                product[t, b] = c.pe(m)
            else:
                m.then_inc(c.w_used, 1)
                product[t, b] = c.used(6 + b)
    c.advance(8)

    (lnw, arrived), = lnw
    block = lambda t, b: (c.res[:, t, b * 512:(b + 1) * 512], slice(b * 512, (b + 1) * 512))
    normed = [[None] * NT for _ in range(2)]

    def add(t, b):
        r, _ = block(t, b)
        wait(c.V, product[t, b])
        added = c.dve(c.V.scalar_tensor_tensor(r, r, alpha, c.ps[:, 2 * b + t, :], ALU.mult, ALU.add))
        wait(c.V, added)
        return c.dve(c.V.bn_stats(c.st[:, t, b, :], r))

    def root(t, stats, meanwhile):
        wait(c.V, stats)
        a = c.dve(c.V.bn_aggr(c.mv[:, t, :], c.st[:, t, :, :].rearrange("p a b -> p (a b)")))
        wait(c.V, a)
        return rsqrt(c, c.mv[:, t, 1:2], c.rs[:, t:t + 1], 1e-5, [z[:, t:t + 1] for z in c.tmp], meanwhile=meanwhile)

    add(0, 0)
    r0 = root(0, add(0, 1), lambda: add(1, 0))
    wait(c.V, r0)
    shift = c.dve(c.V.scalar_tensor_tensor(c.shift[:, 0:1], c.mv[:, 0, 0:1], -1.0, c.rs[:, 0:1], ALU.mult, ALU.mult))
    wait(c.A, shift)
    wait(c.G, arrived)
    for b in range(2):
        r, cols = block(0, b)
        scaled = c.act(c.A.activation(r, r, ACT.Identity, bias=c.shift[:, 0:1], scale=c.rs[:, 0:1]))
        wait(c.G, scaled)
        gained = c.pool(c.G.tensor_tensor(r, r, lnw[:, 0, cols], ALU.mult))
        wait(c.G, gained)
        normed[b][0] = c.pool(c.G.tensor_tensor(r, r, lnw[:, 1, cols], ALU.add))

    def centre():
        wait(c.V, arrived)
        for b in range(2):
            r, cols = block(1, b)
            c.dve(c.V.scalar_tensor_tensor(r, r, c.mv[:, 1, 0:1], lnw[:, 0, cols], ALU.subtract, ALU.mult))

    wait(c.V, root(1, add(1, 1), centre))
    for b in range(2):
        r, cols = block(1, b)
        normed[b][1] = c.dve(c.V.scalar_tensor_tensor(r, r, c.rs[:, 1:2], lnw[:, 1, cols], ALU.mult, ALU.add))
    return normed


def halves(*banks):
    return [b[:, n * S:(n + 1) * S] for b in banks for n in range(2)]


def latent_tables(c, d):
    c.top = c.phase + 2 * 4 * HB * S
    wait(c.A, c.pe.now(), c.dve.now(), c.act.now(), c.pool.now())
    named = (("ropeB", "k_ropeB", [P, 2, S]), ("rotB", "k_rotB", [P, P]), ("maskB", "k_maskB", [P, 3 * P]),
             ("qnorm", "b_q_norm", [P, QL // P]), ("kvnorm", "kv_norm", [P, KVL // P]))
    loaded = [table(c, c.A, name, d[source], shape) for name, source, shape in named]
    return [t for t, _ in loaded], [arrived for _, arrived in loaded], c.top


def latent_attention_layer(c, d, ready, tables):
    ps = c.ps
    (rope, rot, mask, qnorm, kvnorm), arrived, end = tables
    oT = [c.place("b_oT_hi", [P, HB, S], F32R, at=c.phase), c.place("b_oT_lo", [P, HB, S], F32R)]
    c.top = end
    lat = c.place("b_lat", [P, NT, KVL], at=c.phase)
    qlat = c.place("b_qlat", [P, NT, QL])
    junk = c.place("b_junk", [P, 4, 512])
    c.top = end
    qlatT = [c.place("b_qlatT_hi", [P, QL // P, S], F32R), c.place("b_qlatT_lo", [P, QL // P, S], F32R)]
    latT = [c.place("b_latT_hi", [P, KVL // P, S], F32R), c.place("b_latT_lo", [P, KVL // P, S], F32R)]
    kr = c.place("b_kr", [P, 2, S])
    both = lambda name, *shape: c.place(name, [P, 2, *shape])
    qn, kn, v, gate = both("b_qn", 2, S), both("b_kn", 2, S), both("b_v", NT, 2 * VH), both("b_gate", 2, S)
    qr, p, pT = both("b_qr", S), both("b_p", 3 * P), both("b_pT", 3 * P)
    xr, xc, xs = (c.place(n, [P, S]) for n in ("b_xr", "b_xc", "b_xs"))
    og = c.place("b_og", [P, 2, S])
    few = c.place("b_few", [P, 5, 2, 2])
    sq, sq2, nmax, sums, rsum = (few[:, n, :, :] for n in range(5))
    wait(c.V, *arrived)
    wait(c.G, *arrived)
    wait(c.A, *arrived)
    wait(c.T, *arrived)
    zero = c.dve(c.V.memset(kr[:, :, :], 0.0))

    w = d["b_w_qlat"]
    for b in range(2):
        for half in range(2):
            j = 2 * b + half
            c.load(j, w[b, half])
            c.split(j + AHEAD)
            done = c.token_major(j, c.xT, 4 * half, 4, 384, [ps[:, 2 * b + t, 0:384] for t in range(NT)],
                                 half == 0, half == 1, ready if b == 0 else ())
        wait(c.A, done)
        for t in range(NT):
            squared = c.act(c.A.activation(junk[:, 2 * b + t, 0:384], ps[:, 2 * b + t, 0:384], ACT.Square,
                                           accum_out=sq[:, t, b:b + 1]))
    wait(c.V, squared)
    r = c.dve(c.V.tensor_tensor(sq2[:, :, 0], sq[:, :, 0], sq[:, :, 1], ALU.add))
    wait(c.V, r)
    r = rsqrt(c, sq2[:, :, 0], c.rs[:, :], 1e-6, c.tmp, 1.0 / QL)
    wait(c.V, r)
    for b in range(2):
        for t in range(NT):
            qlat_in = c.dve(c.V.tensor_scalar(qlat[:, t, b * 384:(b + 1) * 384], ps[:, 2 * b + t, 0:384],
                                              c.rs[:, t:t + 1], None, ALU.mult))
    c.advance(4)

    DOWN = KVL + 2 * ROPE
    for j in range(4):
        c.load(j, d["kv_w_down"][0, j])
        c.split(j + AHEAD)
        wh, wl = (z[:, 0:2 * DOWN].rearrange("p (k n) -> p k n", k=2) for z in c.use(j))
        for k in range(2):
            first, last = j == 0 and k == 0, j == 3 and k == 1
            for t in range(NT):
                x = tuple(z[:, 2 * j + k, t * P:(t + 1) * P] for z in c.xT)
                c.mm3(ps[:, 4 + t, :], x, (wh[:, k, 0:KVL], wl[:, k, 0:KVL]), first, last)
            x = tuple(z[:, 2 * j + k, :] for z in c.xT)
            m = c.mm3(ps[:, 6, 0:S], (wh[:, k, KVL:DOWN], wl[:, k, KVL:DOWN]), x, first, last)
        m.then_inc(c.w_used, 1)
    done = c.used(3)
    c.advance(4)
    queries = transpose_in(c, lambda t, k: qlat[:, t, k * P:(k + 1) * P], QL // P, whole(qlatT[0]), whole(qlatT[1]),
                              (qlat_in,), banks=(1, 2, 3), weight=qnorm)
    wait(c.A, done)
    for t in range(NT):
        squared = c.act(c.A.activation(junk[:, t, :], ps[:, 4 + t, :], ACT.Square, accum_out=sq[:, t, 0:1]))
    wait(c.V, squared)
    r = rsqrt(c, sq[:, :, 0], c.rs[:, :], 1e-6, c.tmp, 1.0 / KVL)
    wait(c.V, r)
    for t in range(NT):
        lat_in = c.dve(c.V.tensor_scalar(lat[:, t, :], ps[:, 4 + t, :], c.rs[:, t:t + 1], None, ALU.mult))
    xr_in = c.dve(c.V.tensor_copy(xr[:, :], ps[:, 6, 0:S]))

    def latents_to_features():
        wait(c.T, xr_in)
        rotated = c.pe(c.T.matmul(ps[:, 7, 0:S], rot[:, :], xr[:, :], start=True, stop=True))
        wait(c.V, xr_in)
        a = c.dve(c.V.tensor_tensor(xc[:, :], xr[:, :], rope[:, 0, :], ALU.mult))
        wait(c.V, rotated, zero, a)
        a = c.dve(c.V.tensor_tensor(xs[:, :], ps[:, 7, 0:S], rope[:, 1, :], ALU.mult))
        wait(c.V, a)
        for n in range(2):
            rows = slice(n * ROPE, (n + 1) * ROPE)
            kr_in = c.dve(c.V.tensor_tensor(kr[rows, n, :], xc[rows, :], xs[rows, :], ALU.add))
        latents = transpose_in(c, lambda t, k: lat[:, t, k * P:(k + 1) * P], KVL // P, whole(latT[0]),
                               whole(latT[1]), (lat_in,), banks=(4, 5), weight=kvnorm)
        pr["ready"] = (kr_in,)
        pr["k"] += (latents[-1],)
        wait(c.T, queries[-1])

    w_gate, w_uq, w_kv = d["b_w_gate"], d["b_w_uq"], d["kv_w_up"]
    QC, KC = NOPE + ROPE, NOPE + VH

    class Free(dict):

        NAMES = ("ready", "scores", "pT_bank", "o", "og", "gate", "uq", "rotary", "k", "v", "q", "xr", "xs", "p0", "p1", "pT0", "pT1")

        def __init__(self, *issued):
            super().__init__((name, issued) for name in self.NAMES)
            self.pT_in = {}

        def distances(self):
            return {name: [(t[2], t[2].serial - t[3]) for t in tokens] for name, tokens in self.items()}

        def carry(self, distances):
            self.update((name, tuple(signal.now(back) for signal, back in d)) for name, d in distances.items())

    def attend_scores(pr, par, h):
        wait(c.T, *pr["ready"], *pr["scores"])
        for q, cols in enumerate((slice(0, P), slice(P, 3 * P))):
            out, qs, keys = ps[:, 5, cols], slice(q * P, (q + 1) * P), slice(0, (q + 1) * P)
            c.T.matmul(out, qn[:, par, h, qs], kn[:, par, h, keys], start=q == 0, stop=False, skip_group_check=True)
            m = c.T.matmul(out, qr[:, par, qs], kr[:, h, keys], start=False, stop=True, skip_group_check=True)
        scored = c.pe(m)
        wait(c.V, scored, *pr[f"p{h}"])
        c.V.memset(nmax[:, h, :], 0.0)
        for q, cols in enumerate((slice(0, P), slice(P, 3 * P))):
            a = c.dve(c.V.tensor_tensor_reduce(out=p[:, h, cols], in0=ps[:, 5, cols], in1=mask[:, cols],
                                               scale=SCALE_B, scalar=-3.0e38, op0=ALU.add, op1=ALU.max,
                                               accum_out=sums[:, h, q:q + 1]))
        pr["scores"] = (a,)
        wait(c.V, a)
        negated = c.dve(c.V.tensor_scalar(nmax[:, h, :], sums[:, h, :], -1.0, None, ALU.mult))
        wait(c.A, negated)
        for q, cols in enumerate((slice(0, P), slice(P, 3 * P))):
            a = c.act(c.A.activation(p[:, h, cols], p[:, h, cols], ACT.Exp, bias=nmax[:, h, q:q + 1],
                                     accum_out=rsum[:, h, q:q + 1]))
        wait(c.V, a)
        a = c.dve(c.V.reciprocal(rsum[:, h, :], rsum[:, h, :]))
        wait(c.V, a)
        for q, cols in enumerate((slice(0, P), slice(P, 3 * P))):
            a = c.dve(c.V.tensor_scalar(p[:, h, cols], p[:, h, cols], rsum[:, h, q:q + 1], None, ALU.mult))
        pr.p_in = a

    def attend_turn(pr, h):
        wait(c.T, pr.p_in, *pr["pT_bank"])
        for n in range(3):
            m = c.T.transpose(ps[:, 6, n * P:(n + 1) * P], p[:, h, n * P:(n + 1) * P], c.ident[:, :])
        turned = c.pe(m)
        pr[f"p{h}"] = (turned,)
        wait(c.A, turned, *pr[f"pT{h}"])
        pr.pT_in[h] = c.act(c.A.activation(pT[:, h, :], ps[:, 6, 0:3 * P], ACT.Copy))
        pr["pT_bank"] = (pr.pT_in[h],)

    def attend_values(pr, par, h):
        wait(c.T, pr.pT_in[h], *pr["o"])
        out = ps[:, 7, h * S:(h + 1) * S]
        cols = slice(h * VH, (h + 1) * VH)
        c.T.matmul(out, v[:, par, 0, cols], pT[:, h, 0:2 * P], start=h == 0, stop=False, skip_group_check=True)
        done = c.pe(c.T.matmul(out[:, P:2 * P], v[:, par, 1, cols], pT[:, h, 2 * P:3 * P], start=False, stop=True,
                               skip_group_check=True))
        pr[f"pT{h}"] = (done,)
        return done

    def attend_out(pr, par, pair, done):
        wait(c.V, done, *pr["og"])
        o = c.dve(c.V.tensor_tensor(og[:, :, :], ps[:, 7, :].rearrange("p (h s) -> p h s", h=2), gate[:, par, :, :], ALU.mult))
        pr["o"] = (o,)
        at = bass.ds(pair * 2, 2)
        wait(c.A, o)
        r = c.act(c.A.activation(oT[0][:, at, :], og[:, :, :], ACT.Copy))
        wait(c.G, r)
        g_ = c.pool(c.G.tensor_tensor(oT[1][:, at, :], og[:, :, :], oT[0][:, at, :].bitcast(F32), ALU.subtract))
        pr["og"] = (g_,)

    def step(pr, j0, pair, par, other, between=None):
        at = bass.ds(pair, 1)
        c.load(j0, w_gate[at])
        for n in range(2):
            c.load(j0 + 1 + n, w_uq[at, n])
        c.load(j0 + 3, w_kv[at])
        c.split(j0 + AHEAD)
        wait(c.T, *pr["gate"])
        done = c.feature_major(j0, c.xT, 0, KD, 2 * VH, halves(ps[:, 0, :]), True, True)
        wait(c.A, done, *pr["o"])
        gate_in = c.act(c.A.activation(gate[:, par, :, :], ps[:, 0, :].rearrange("p (h s) -> p h s", h=2), ACT.Silu))
        pr["gate"] = (gate_in,)
        if between:
            between()
        if other is not None:
            attend_scores(pr, 1 - par, 0)
        wait(c.T, *pr["uq"])
        for n in range(2):
            c.split(j0 + 1 + n + AHEAD)
            wh, wl = (z[:, 0:6 * QC].rearrange("p (k n) -> p k n", k=3) for z in c.use(j0 + 1 + n))
            for q, out in enumerate((ps[:, 1, 0:S], ps[:, 1, S:2 * S], ps[:, 2, 0:S])):
                if q == 2 and n == 0:
                    wait(c.T, *pr["rotary"])
                for k in range(3):
                    m = c.mm3(out, tuple(z[:, k, q * P:(q + 1) * P] for z in (wh, wl)),
                              tuple(z[:, 3 * n + k, :] for z in qlatT), n == 0 and k == 0 and q != 1, n == 1 and k == 2)
            m.then_inc(c.w_used, 1)
        done = c.used(j0 + 2)
        wait(c.A, done, *pr["q"])
        qn_in = c.act(c.A.activation(qn[:, par, :, :], ps[:, 1, :].rearrange("p (h s) -> p h s", h=2), ACT.Copy))
        wait(c.V, done, *pr["xr"])
        xr_in = c.dve(c.V.tensor_copy(xr[:, :], ps[:, 2, 0:S]))
        if other is not None:
            attend_turn(pr, 0)
            attend_scores(pr, 1 - par, 1)
        c.split(j0 + 3 + AHEAD)
        wait(c.T, *pr["k"])
        wh, wl = (z[:, 0:4 * 2 * KC].rearrange("p (k n) -> p k n", k=4) for z in c.use(j0 + 3))
        for h in range(2):
            for k in range(4):
                c.mm3(ps[:, 3, h * S:(h + 1) * S], tuple(z[:, k, h * P:(h + 1) * P] for z in (wh, wl)),
                      tuple(z[:, k, :] for z in latT), h == 0 and k == 0, k == 3)
        wait(c.T, *pr["v"])
        for t in range(NT):
            for k in range(4):
                m = c.mm3(ps[:, 4, t * S:(t + 1) * S], tuple(z[:, k, t * P:(t + 1) * P] for z in latT),
                          tuple(z[:, k, 2 * NOPE:2 * KC] for z in (wh, wl)),
                          t == 0 and k == 0, k == 3)
        m.then_inc(c.w_used, 1)
        done = c.used(j0 + 3)
        wait(c.T, xr_in)
        rotated = c.pe(c.T.matmul(ps[:, 2, S:2 * S], rot[:, :], xr[:, :], start=True, stop=True))
        if other is not None:
            attend_turn(pr, 1)
            attend_values(pr, 1 - par, 0)
            o_done = attend_values(pr, 1 - par, 1)
            attend_out(pr, 1 - par, other, o_done)
        wait(c.G, xr_in, *pr["xs"])
        cosines = c.pool(c.G.tensor_tensor(xc[:, :], xr[:, :], rope[:, 0, :], ALU.mult))
        pr["xr"] = (cosines, rotated)
        wait(c.V, rotated, *pr["xs"])
        sines = c.dve(c.V.tensor_tensor(xs[:, :], ps[:, 2, S:2 * S], rope[:, 1, :], ALU.mult))
        pr["uq"], pr["rotary"] = (qn_in,), (sines,)
        wait(c.G, sines, cosines, *pr["q"])
        qr_in = c.pool(c.G.tensor_tensor(qr[:, par, :], xc[:, :], xs[:, :], ALU.add))
        pr["xs"] = (qr_in,)
        wait(c.A, done)
        kn_in = c.act(c.A.activation(kn[:, par, :, :], ps[:, 3, :].rearrange("p (h s) -> p h s", h=2), ACT.Copy))
        wait(c.V, done, *pr["q"])
        v_in = c.dve(c.V.tensor_copy(v[:, par, :, :], ps[:, 4, :].rearrange("p (t n) -> p t n", t=2)))
        pr["k"], pr["v"] = (kn_in,), (v_in,)
        pr["ready"] = (kn_in, v_in, qn_in, qr_in)
        pr["q"] = ()
        if other is not None:
            pr["q"] = (o_done,)

    pr = Free(c.pe.now(), c.dve.now(), c.act.now(), c.pool.now())
    pr["gate"] = (qlat_in,)
    step(pr, 0, 0, 0, None, latents_to_features)
    c.advance(4)
    step(pr, 0, 1, 1, 0)
    c.advance(4)
    back = pr.distances()
    with c.loop("attention", 3, 8) as i:
        pr.carry(back)
        step(pr, 0, i * 2 + 2, 0, i * 2 + 1)
        step(pr, 4, i * 2 + 3, 1, i * 2 + 2)
        if pr.distances() != back:
            raise ValueError("the loop's body ends in another order than the step before it")
    pr.carry(back)

    last = HB // 2 - 1
    done = []

    def first_scores():
        attend_scores(pr, last % 2, 0)

    def second_scores():
        attend_turn(pr, 0)
        attend_scores(pr, last % 2, 1)

    def first_values():
        attend_values(pr, last % 2, 0)
        attend_turn(pr, 1)
        wait(c.T, *pr["rotary"], *pr["k"])

    def last_values():
        done.append(attend_values(pr, last % 2, 1))
        attend_out(pr, last % 2, last, done[0])

    after, gated = (*pr["gate"], *pr["uq"]), pr["og"]
    hooks = {1: [first_scores], 2: [second_scores, lambda: wait(c.T, *gated)], 3: [first_values], 4: [last_values],
             6: [lambda: wait(c.T, *pr["og"])]}
    return oT, after, hooks


def feature_stage(c, name, count, source, xT, drain, signal, after, per_unit=1, ready=(), hooks={}, on_pool=()):
    wait(c.T, *after)

    def body(i):
        for j in range(4):
            n = i * 4 + j
            c.load(j, source(n))
            c.split(j + AHEAD, j in on_pool)
            for hook in hooks.get(j, ()):
                hook()
            if count > 1:
                wait(c.T, signal.now(3 * per_unit))
            done = c.feature_major(j, xT, 0, KD, S, halves(c.ps[:, j, :]), True, True, ready if j == 0 else ())
            drain(n, c.ps[:, j, :].rearrange("p (k s) -> p k s", k=2), done, j)

    if count == 1:
        body(0)
        c.advance(4)
    else:
        with c.loop(name, count, 4) as i:
            body(i)


def softplus8(c, lam, out, neg, tmp):
    t, e, q = tmp
    v, one = c.V, lambda ins: wait(c.V, c.dve(ins))
    one(v.tensor_scalar(t, lam, -1.0, None, ALU.mult))
    one(v.tensor_tensor(e, t, lam, ALU.min))
    wait(c.A, c.dve.now())
    wait(v, c.act(c.A.activation(e, e, ACT.Exp)))
    one(v.tensor_scalar(t, e, 2.0, None, ALU.add))
    one(v.reciprocal(q, t))
    one(v.tensor_tensor(e, e, q, ALU.mult))
    one(v.tensor_tensor(t, e, e, ALU.mult))
    one(v.tensor_scalar(q, t, 1.0 / 17.0, None, ALU.mult))
    for n in (15.0, 13.0, 11.0, 9.0, 7.0, 5.0, 3.0):
        one(v.scalar_tensor_tensor(q, q, 1.0 / n, t, ALU.add, ALU.mult))
    one(v.scalar_tensor_tensor(q, q, 1.0, e, ALU.add, ALU.mult))
    one(v.tensor_scalar(t, lam, -1.0, 0.0, ALU.mult, ALU.max))
    one(v.scalar_tensor_tensor(t, q, 2.0, t, ALU.mult, ALU.add))
    one(v.tensor_scalar(out, t, 4.0, None, ALU.mult))
    one(v.tensor_scalar(neg, t, -8.0, None, ALU.mult))


def rms_input(c, h, junk, squares, weight, normed):
    for t, b in ((0, 0), (1, 0), (1, 1), (0, 1)):
        cols = slice(b * 512, (b + 1) * 512)
        wait(c.A, normed[b][t])
        squared = c.act(c.A.activation(junk[:, t, cols], c.res[:, t, cols], ACT.Square,
                                       accum_out=squares[:, b, t:t + 1]))
    wait(c.V, squared)
    total = c.dve(c.V.tensor_tensor(squares[:, 0, :], squares[:, 0, :], squares[:, 1, :], ALU.add))
    wait(c.V, total)
    r = rsqrt(c, squares[:, 0, :], c.rs[:, :], 1e-6, c.tmp, 1.0 / D)
    wait(c.V, r, *normed[0], *normed[1])
    wait(c.A, r)
    scaled = []
    for b in range(2):
        cols = slice(b * 512, (b + 1) * 512)
        scaled.append((c.dve(c.V.tensor_scalar(h[:, 0, cols], c.res[:, 0, cols], c.rs[:, 0:1], None, ALU.mult)),
                       c.act(c.A.activation(h[:, 1, cols], c.res[:, 1, cols], ACT.Copy, scale=c.rs[:, 1:2]))))
    return transpose_in(c, lambda t, k: h[:, t, k * P:(k + 1) * P], KD, whole(c.xT[0]), whole(c.xT[1]),
                        [scaled[n // 2] for n in range(4)], weight=weight)


def hybrid_layer(c, d, out):
    ps, V, A, G, T = c.ps, c.V, c.A, c.G, c.T
    dve, act, pool, pe = c.dve, c.act, c.pool, c.pe
    everything = lambda: (pe.now(), dve.now(), act.now(), pool.now())
    pair = lambda b: b.rearrange("p (k s) -> p k s", k=2)
    QCOLS = (slice(0, P), slice(P, 3 * P))

    c.top = c.phase
    qk = c.place("c_qk", [P, NT, D + 256])
    v = c.place("c_v", [P, NT, 256])
    iq = c.place("c_iq", [P, NT, IH * ID])
    qT = c.place("c_qT", [P, KD, S])
    kz = c.place("c_kz", [P, HKV, S])
    iqT = c.place("c_iqT", [P, IH // 2, S])
    ikz = c.place("c_ikz", [P, 2, S])
    isc = c.place("c_isc", [P, NT, S])
    xc = c.place("c_xc", [P, KD, S])
    ig = c.place("c_ig", [P, KD, S])
    aa = c.place("c_aa", [P, KD, S])
    gel = c.place("c_gel", [P, KD, S])
    rgw = c.place("c_rgw", [P, 2, KD, P])
    g0 = c.place("c_g0", [P, KD, S])
    ikw = c.place("c_ikw", [P, NT, 2 * ID + IH])
    small = c.top
    rr = c.place("c_rr", [P, KD, S], at=c.at["c_qk"])
    ya = c.place("c_ya", [P, NT, D], at=c.at["c_qk"])
    rl = c.place("c_rl", [P, 2, 3 * P], at=c.at["c_iq"])
    wk = c.place("c_wk", [P, NT, S], at=c.at["c_iq"])
    eqs = c.place("c_eqs", [P, NT, S])
    ones = c.place("c_ones", [P, S], at=c.at["c_iqT"])
    cum = c.place("c_cum", [P, NT, S])
    pT = c.place("c_pT", [P, 4, 3 * P], at=c.at["c_iqT"])
    h = c.place("c_h", [P, NT, D], at=c.at["c_xc"])
    kw_raw = c.place("c_kw_raw", [P, KD, 2 * ID + IH], at=c.at["c_ig"])
    kw = [c.place("c_kw_hi", [P, KD, 2 * ID + IH], F32R), c.place("c_kw_lo", [P, KD, 2 * ID + IH], F32R)]
    junk = c.place("c_junk", [P, NT, D], at=c.at["c_gel"])
    yT = [c.place("c_yT_hi", [P, KD, S], F32R, at=c.at["c_xc"]), c.place("c_yT_lo", [P, KD, S], F32R)]
    zT = yT
    p = c.place("c_p", [P, 4, 3 * P], at=c.at["c_aa"])
    g1 = c.place("c_g1", [P, KD, S], at=c.at["c_rgw"])
    fT = [c.place("c_fT_hi", [P, DFF // P, S], F32R, at=c.phase), c.place("c_fT_lo", [P, DFF // P, S], F32R)]
    fr = c.place("c_fr", [P, 4, 2, S])
    junk2 = c.place("c_junk2", [P, NT, D], at=c.phase)
    c.top = small
    s_kw, s_rgw, s_columns, s_out0 = (c.nc.alloc_semaphore(n) for n in ("s_kw", "s_rgw", "s_columns", "s_out0"))
    columns = c.place("c_columns", [P, sum(n for _, n in COLUMNS_C)])
    vec, at = {}, 0
    for name, n in COLUMNS_C:
        vec[name], at = columns[:, at:at + n], at + n
    lam = c.place("c_lam", [P, 6, 8])
    hlam8, nlam8 = lam[:, 0, :], lam[:, 1, :]
    NH = HC + HKV + 1
    hs, hr, ht0, ht1 = (c.place(n, [P, NT, NH]) for n in ("c_hs", "c_hr", "c_ht0", "c_ht1"))
    few = c.place("c_few", [P, 54])
    squares = few[:, 0:4].rearrange("p (b t) -> p b t", b=2)
    m8 = few[:, 4:20].rearrange("p (t n) -> p t n", t=NT)
    cnt = few[:, 20:22]
    smx, ssum = (few[:, n:n + 8].rearrange("p (q r) -> p q r", q=2) for n in (22, 30))
    inverse = few[:, 38:54].rearrange("p (g q r) -> p g q r", g=2, q=2)

    wait(A, *everything())
    A.dma_start(columns[:, :], d["columns"]).then_inc(s_columns, 16)
    A.dma_start(kw_raw[:, :, :].rearrange("p k n -> p (k n)"), d["w_ikw"]).then_inc(s_kw, 16)
    A.dma_start(rgw[:, :, :, :].rearrange("p a k n -> p (a k n)"), d["rg_w"]).then_inc(s_rgw, 16)
    normed = yield

    wait(A, (s_columns, 16))
    wait(V, (s_columns, 16))
    transposed = rms_input(c, h, junk, squares, vec["norm1_w_2"], normed)
    c.split(AHEAD - 1)

    def prepare():
        wait(A, (s_kw, 16))
        kw_hi = act(A.activation(kw[0][:, :, :], kw_raw[:, :, :], ACT.Copy))
        softplus8(c, vec["rg_lambda_2"], hlam8, nlam8, [lam[:, 3 + n, :] for n in range(3)])
        dve(V.tensor_scalar(vec["gate_b_2"], vec["gate_b_2"], 0.5, None, ALU.mult))
        wait(V, kw_hi)
        return dve(V.tensor_tensor(kw[1][:, :, :], kw_raw[:, :, :], kw[0][:, :, :].bitcast(F32), ALU.subtract))

    drained = {}
    for b, name in enumerate(("q", "q", "kv", "iq")):
        block = [ps[:, 2 * (b % 2) + t, :] for t in range(NT)]
        if b >= 2:
            wait(T, *drained[b - 2])
        for half in range(2):
            j = 2 * b + half
            c.load(j, d["w_qkvi"][b, half])
            c.split(j + AHEAD)
            done = c.token_major(j, c.xT, 4 * half, 4, 512, block, half == 0, half == 1,
                                 transposed if b == 0 else ())
        wait(A, done)
        wait(V, done)
        for t in range(NT):
            copy = (lambda o, i: act(A.activation(o, i, ACT.Copy))) if t == 0 else (lambda o, i: dve(V.tensor_copy(o, i)))
            if name == "q":
                copy(qk[:, t, b * 512:(b + 1) * 512], block[t])
            elif name == "kv":
                copy(qk[:, t, D:D + 256], block[t][:, 0:256])
                copy(v[:, t, :], block[t][:, 256:512])
            else:
                copy(iq[:, t, :], block[t])
        drained[b] = (act.now(), dve.now())
        if b == 1:
            kw_in = prepare()
            wait(G, dve.now())
            G.memset(kz[:, :, :], 0.0)
            pool(G.memset(ikz[:, :, :], 0.0))
    c.advance(8)
    wait(T, kw_in)
    for k in range(KD):
        for t in range(NT):
            x = tuple(z[:, k, t * P:(t + 1) * P] for z in c.xT)
            m = c.mm3(ps[:, 4 + t, 0:2 * ID + IH], x, tuple(z[:, k, :] for z in kw), k == 0, k == KD - 1)
    done = pe(m)
    wait(A, done)
    for t in range(NT):
        ikw_in = act(A.activation(ikw[:, t, :], ps[:, 4 + t, 0:2 * ID + IH], ACT.Copy))

    wait(A, *drained[3], ikw_in)
    for t in range(NT):
        A.activation(junk[:, t, :], qk[:, t, 0:D], ACT.Square)
    A.activation(h[:, :, 0:256], qk[:, :, D:D + 256], ACT.Square)
    squared = act(A.activation(h[:, :, 256:256 + ID], ikw[:, :, 0:ID], ACT.Square))
    wait(V, squared)
    for t in range(NT):
        V.reduce_sum(hs[:, t, 0:HC], junk[:, t, :].rearrange("p (h n) -> p h n", n=DC), AX.X)
        a = dve(V.reduce_sum(hs[:, t, HC:NH], h[:, t, 0:256 + ID].rearrange("p (h n) -> p h n", n=DC), AX.X))
    flat = lambda t: t[:, :, :].rearrange("p t n -> p (t n)")
    wait(V, a)
    r = rsqrt(c, flat(hs), flat(hr), 1e-6, (flat(ht0), flat(ht1)), 1.0 / DC)
    wait(V, r)
    wait(G, r)
    for t, (eng, sig) in enumerate(((V, dve), (G, pool))):
        x = qk[:, t, :].rearrange("p (h n) -> p h n", n=DC)
        sig(eng.tensor_tensor(x, x, hr[:, t, 0:HC + HKV].unsqueeze(2).broadcast_to([P, HC + HKV, DC]), ALU.mult))
    for t in range(NT):
        dve(V.tensor_scalar(ikw[:, t, 0:2 * ID], ikw[:, t, 0:2 * ID], hr[:, t, NH - 1:NH], None, ALU.mult))
    heads = everything()

    cw, cb = vec["conv_w_2"], vec["conv_b_2"]

    def conv(n, bank, done, j):
        wait(A, done)
        for k in range(2):
            tile = 2 * n + k
            first = act(A.activation(xc[:, tile, :], bank[:, k, :], ACT.Identity, bias=cb[:, tile:tile + 1],
                                     scale=cw[:, 24 + tile:25 + tile]))
        wait(V, first)
        for s in (1, 2, 3):
            for k in range(2):
                tile = 2 * n + k
                a = dve(V.scalar_tensor_tensor(xc[:, tile, s:S], bank[:, k, 0:S - s], cw[:, (3 - s) * 8 + tile:(3 - s) * 8 + tile + 1],
                                               xc[:, tile, s:S], ALU.mult, ALU.add))
            if s < 3:
                wait(V, a)

    hn = vec["head_norms"]
    index_ready = []
    small_banks = [4, 5, 6, 7]
    bank_read = {b: (ikw_in,) for b in small_banks}

    def small_bank():
        b = small_banks.pop(0)
        small_banks.append(b)
        wait(T, *bank_read[b])
        return b, ps[:, b, :]

    def to_features(name, t0):
        b, bank = small_bank()
        for k in range(1 if name == "ik" else 2):
            for t in range(NT):
                src = {"q": lambda: qk[:, t, (t0 + k) * P:(t0 + k + 1) * P], "k": lambda: qk[:, t, D + k * P:D + (k + 1) * P],
                       "iq": lambda: iq[:, t, (t0 + k) * P:(t0 + k + 1) * P], "ik": lambda: ikw[:, t, 0:P]}[name]()
                m = T.transpose(bank[:, (2 * k + t) * P:(2 * k + t + 1) * P], src, c.ident[:, :])
        turned = pe(m)
        wait(A, turned)
        if name == "q":
            a = act(A.activation(qT[:, t0:t0 + 2, :], pair(bank), ACT.Copy, scale=hn[:, 0:1]))
        elif name == "iq":
            a = act(A.activation(iqT[:, t0:t0 + 2, :], pair(bank), ACT.Copy))
        elif name == "k":
            for g in range(HKV):
                rows = slice(64 * (g % 2), 64 * (g % 2) + 64)
                a = act(A.activation(kz[rows, g, :], bank[rows, (g // 2) * S:(g // 2 + 1) * S], ACT.Copy, scale=hn[rows, 1:2]))
        else:
            for g in range(2):
                rows = slice(64 * g, 64 * g + 64)
                a = act(A.activation(ikz[rows, g, :], bank[rows, 0:S], ACT.Copy, scale=hn[rows, 2:3]))
        bank_read[b] = (a,)

    def queries_of_index():
        to_features("iq", 0)
        to_features("iq", 2)

    def keys_to_features():
        wait(T, *heads)
        wait(A, *heads)
        to_features("ik", 0)
        index_ready.append(act.now())
        to_features("k", 0)

    feature_stage(c, None, 1, lambda n: d["w_rnn"][n], c.xT, conv, dve, drained[2] + drained[3], 6,
                  hooks={1: [queries_of_index], 3: [keys_to_features]}, on_pool=(1, 3))
    conv_in = dve.now()

    acc = {}

    def index_scores(heads_of_index):
        wait(T, *index_ready)
        for hd in heads_of_index:
            b, bank = small_bank()
            for q, cols in enumerate(QCOLS):
                m = T.matmul(bank[:, cols], iqT[:, hd // 2, q * P:(q + 1) * P], ikz[:, hd % 2, 0:(q + 1) * P],
                             start=q == 0, stop=True, skip_group_check=True)
            scored = pe(m)
            wait(A, scored)
            if hd >= 2:
                wait(A, acc[hd - 2])
            a = act(A.activation(rl[:, hd % 2, :], bank[:, 0:3 * P], ACT.Relu))
            bank_read[b] = (a,)
            wait(V, a)
            if hd:
                wait(V, acc[hd - 1])
            for q, cols in enumerate(QCOLS):
                o, w = isc[:, q, 0:(q + 1) * P], ikw[:, q, 2 * ID + hd:2 * ID + hd + 1]
                if hd == 0:
                    acc[hd] = dve(V.tensor_scalar(o, rl[:, 0, cols], w, None, ALU.mult))
                else:
                    acc[hd] = dve(V.scalar_tensor_tensor(o, rl[:, hd % 2, cols], w, o, ALU.mult, ALU.add))

    gates = {}

    def recurrence_gates(tiles):
        wait(T, conv_in, (s_rgw, 16))
        for n in tiles:
            b, bank = small_bank()
            T.matmul(bank[:, 0:S], rgw[:, 0, n, :], xc[:, n, :], start=True, stop=True, skip_group_check=True)
            gated = pe(T.matmul(bank[:, S:2 * S], rgw[:, 1, n, :], xc[:, n, :], start=False, stop=True, skip_group_check=True))
            wait(A, gated)
            A.activation(rr[:, n, :], bank[:, 0:S], ACT.Sigmoid, bias=vec["rg_ba_2"][:, n:n + 1])
            a = act(A.activation(ig[:, n, :], bank[:, S:2 * S], ACT.Sigmoid, bias=vec["rg_bx_2"][:, n:n + 1]))
            bank_read[b] = (a,)
        gates["in"], gates["made"] = a, gated

    made = {}

    def selection():
        widths = [(q, (q + 1) * P) for q in range(NT)]
        wait(V, acc[IH - 1])
        for q, n in widths:
            a = dve(V.tensor_scalar(isc[:, q, 0:n], isc[:, q, 0:n], IDX_SCALE, None, ALU.mult))
        wait(V, a)
        for q, n in widths:
            V.memset(isc[0:CH, q, n - CH:n], -1.0e30)
        a = dve(V.memset(ones[:, :], 1.0))
        for step in range(TOPK // 8):
            src = isc if step == 0 else wk
            wait(V, a)
            for q, n in widths:
                a = dve(V.max(m8[:, q, :], src[:, q, 0:n]))
            yield
            if step < TOPK // 8 - 1:
                wait(V, a)
                for q, n in widths:
                    a = dve(V.match_replace(out=wk[:, q, 0:n], in_to_replace=m8[:, q, :], in_values=src[:, q, 0:n],
                                            imm_value=-3.0e38))
                yield
        wait(V, a)
        for q, n in widths:
            V.tensor_scalar(eqs[:, q, 0:n], isc[:, q, 0:n], m8[:, q, 7:8], None, ALU.is_equal)
            a = dve(V.tensor_scalar(wk[:, q, 0:n], isc[:, q, 0:n], m8[:, q, 7:8], None, ALU.is_gt, ALU.add,
                                    accum_out=cnt[:, q:q + 1]))
        wait(V, a)
        dve(V.tensor_scalar(cnt[:, :], cnt[:, :], -1.0, float(TOPK), ALU.mult, ALU.add))
        for q, n in widths:
            a = dve(V.tensor_tensor_scan(cum[:, q, 0:n], ones[:, 0:n], eqs[:, q, 0:n], 0.0, ALU.mult, ALU.add))
        yield
        wait(V, a)
        for q, n in widths:
            a = dve(V.scalar_tensor_tensor(eqs[:, q, 0:n], cum[:, q, 0:n], cnt[:, q:q + 1], eqs[:, q, 0:n],
                                           ALU.is_le, ALU.mult))
        wait(V, a)
        for q, n in widths:
            a = dve(V.tensor_tensor(wk[:, q, 0:n], wk[:, q, 0:n], eqs[:, q, 0:n], ALU.add))
        wait(V, a)
        for q, n in widths:
            made["selected"] = dve(V.tensor_scalar(isc[:, q, 0:n], wk[:, q, 0:n], 1.0e30, -1.0e30, ALU.mult, ALU.add))
        yield

    def recurrence():
        wait(G, gates["in"], conv_in)
        ix = pool(G.tensor_tensor(ig[:, :, :], ig[:, :, :], xc[:, :, :], ALU.mult))
        wait(A, gates["in"])
        for n in range(KD):
            exps = act(A.activation(aa[:, n, :], rr[:, n, :], ACT.Exp, scale=nlam8[:, n:n + 1]))
        yield
        wait(A, exps)
        for n in range(KD):
            tanhs = act(A.activation(rr[:, n, :], rr[:, n, :], ACT.Tanh, scale=hlam8[:, n:n + 1]))
        yield
        wait(A, tanhs)
        root = act(A.activation(rr[:, :, :], rr[:, :, :], ACT.Sqrt))
        wait(V, exps, ix)
        a = dve(V.scalar_tensor_tensor(ig[:, :, :], aa[:, :, :], 1.0, ig[:, :, :], ALU.add, ALU.mult))
        wait(G, root, a)
        u = pool(G.tensor_tensor(ig[:, :, :], ig[:, :, :], rr[:, :, :], ALU.mult))
        yield
        wait(V, u, exps)
        for n in range(KD):
            scanned = dve(V.tensor_tensor_scan(rr[:, n, :], aa[:, n, :], ig[:, n, :], 0.0, ALU.mult, ALU.add))
            made["scanned"] = scanned
            if n % 2:
                yield
        wait(G, scanned, made["gelu"])
        y = made["y_unsplit"] = pool(G.tensor_tensor(gel[:, :, :], rr[:, :, :], gel[:, :, :], ALU.mult))
        yield
        wait(A, y, scanned)
        rounded = act(A.activation(yT[0][:, :, :], gel[:, :, :], ACT.Copy))
        wait(G, rounded)
        made["y"] = pool(G.tensor_tensor(yT[1][:, :, :], gel[:, :, :], yT[0][:, :, :].bitcast(F32), ALU.subtract))
        yield

    def scores(g):
        wait(T, *(made["scores_free"] if g else (gates["in"],)))
        for r in range(4):
            tile = 4 * (g // 2) + r
            T.matmul(ps[:, 4, r * P:(r + 1) * P], qT[:, tile, 0:P], kz[:, g, 0:P], start=r == 0, stop=True,
                     skip_group_check=True)
            m = T.matmul(ps[:, 5 + r // 2, (r % 2) * S:(r % 2 + 1) * S], qT[:, tile, P:2 * P], kz[:, g, :], start=r % 2 == 0,
                         stop=True, skip_group_check=True)
        scored = pe(m)
        wait(V, scored, made["selected"], *made.get("p_free", (made["scanned"],)))
        q0, q1 = p[:, :, 0:P], p[:, :, P:3 * P]
        bias = lambda q, n, heads: isc[:, q:q + 1, 0:n].broadcast_to([P, heads, n])
        dve(V.scalar_tensor_tensor(q0, ps[:, 4, :].rearrange("p (r n) -> p r n", r=4), SCALE_C, bias(0, P, 4),
                                   ALU.mult, ALU.add))
        for half in range(2):
            a = dve(V.scalar_tensor_tensor(q1[:, 2 * half:2 * half + 2, :], pair(ps[:, 5 + half, :]), SCALE_C,
                                           bias(1, S, 2), ALU.mult, ALU.add))
        made["scores_free"] = (a,)
        wait(V, a)
        V.tensor_reduce(smx[:, 0, :], q0, AX.X, ALU.max)
        a = dve(V.tensor_reduce(smx[:, 1, :], q1, AX.X, ALU.max))
        wait(V, a)
        a = dve(V.tensor_scalar(smx[:, :, :], smx[:, :, :], -1.0, None, ALU.mult))
        wait(A, a, *made.get("ssum_free", ()))
        for r in range(4):
            for q, cols in enumerate(QCOLS):
                a = act(A.activation(p[:, r, cols], p[:, r, cols], ACT.Exp, bias=smx[:, q, r:r + 1],
                                     accum_out=ssum[:, q, r:r + 1]))
        made["p"] = a

    def turn(g):
        wait(V, made["p"])
        made["inverse", g] = dve(V.reciprocal(inverse[:, g % 2, :, :], ssum[:, :, :]))
        made["ssum_free"] = (made["inverse", g],)
        turned_out = []
        for r in range(4):
            b = ps[:, (2, 3, 7, 2)[r], :]
            wait(T, made["p"], *(turned_out[0] if r == 3 else made.get("o_free" if r == 2 else "pT", (conv_in,))))
            for n in range(3):
                m = T.transpose(b[:, n * P:(n + 1) * P], p[:, r, n * P:(n + 1) * P], c.ident[:, :])
            turned = pe(m)
            wait(A, turned, *made.get("pT_free", ()))
            a = act(A.activation(pT[:, r, :], b[:, 0:3 * P], ACT.Copy))
            turned_out.append((a,))
        made["p_free"] = (turned,)
        made["pT"] = (a,)

    def values(g):
        wait(T, *made["pT"], *made.get("o_free", ()))
        for q in range(NT):
            for r in range(4):
                o = ps[:, 7, (4 * q + r) * DC:(4 * q + r + 1) * DC]
                for k in range(q + 1):
                    m = T.matmul(o, pT[:, r, (q + k) * P:(q + k + 1) * P], v[:, k, g * DC:(g + 1) * DC],
                                 start=q == 0 and r == 0, stop=k == q, skip_group_check=True)
        done = pe(m)
        made["pT_free"] = (done,)
        wait(V, made["inverse", g], done)
        if g == 0:
            wait(V, made["y_unsplit"])
        for q in range(NT):
            a = dve(V.tensor_tensor(ya[:, q, g * 4 * DC:(g + 1) * 4 * DC].rearrange("p (r n) -> p r n", r=4),
                                    ps[:, 7, 4 * q * DC:4 * (q + 1) * DC].rearrange("p (r n) -> p r n", r=4),
                                    inverse[:, g % 2, q, :].unsqueeze(2).broadcast_to([P, 4, DC]), ALU.mult))
        made["o_free"] = made["output", g] = (a,)

    chains = {"selection": selection(), "recurrence": recurrence()}

    def steps(name, n):
        for _ in range(n):
            next(chains[name], None)

    interludes = {0: [lambda: index_scores(range(0, 4))],
                  1: [lambda: index_scores(range(4, IH))]
                  + [lambda t0=t0: to_features("q", t0) for t0 in range(0, KD, 2)]
                  + [lambda: recurrence_gates(range(KD))]}
    plan = {1: (10, 1), 2: (6, 1), 3: (9, 1), 4: (0, 2), 5: (0, 2), 6: (0, 1), 9: (0, 1)}
    gb = vec["gate_b_2"]
    bank_free = {}
    for n in range(16):
        kind, t0 = n // 4, 2 * (n % 4)
        c.load(n, (d["w_rnn"][4 + n] if kind == 0 else d["w_gates"][n - 4] if kind < 3 else d["w_o_rnn"][n - 12]))
        c.split(n + AHEAD)
        for interlude in interludes.get(n, ()):
            interlude()
        for name, count in zip(chains, plan.get(n, (0, 0))):
            steps(name, count)
        if kind == 3:
            wait(T, made["y"])
        bank = ps[:, n % 2, :]
        wait(T, *(bank_free[n - 2] if n >= 2 else (conv_in,)))
        done = c.feature_major(n, yT if kind == 3 else c.xT, 0, KD, S, halves(bank), True, True)
        if n >= 8 and n % 2 == 0:
            turn((n - 8) // 2)
        if kind == 0:
            wait(A, done)
            a = act(A.activation(gel[:, t0:t0 + 2, :], pair(bank), ACT.Gelu_apprx_tanh))
            made["gelu"] = a
        elif kind < 3:
            wait(A, done)
            if kind == 2:
                wait(A, gates["made"])
            for k in range(2):
                a = act(A.activation((g0, g1)[kind - 1][:, t0 + k, :], bank[:, k * S:(k + 1) * S], ACT.Tanh, scale=0.5,
                                     bias=gb[:, 8 * (kind - 1) + t0 + k:8 * (kind - 1) + t0 + k + 1]))
        else:
            wait(V, done, act.now())
            a = dve(V.scalar_tensor_tensor(g0[:, t0:t0 + 2, :], g0[:, t0:t0 + 2, :], 1.0, pair(bank), ALU.add, ALU.mult))
        bank_free[n] = (a,)
        if 6 <= n < 14 and n % 2 == 0:
            scores((n - 6) // 2)
        if n >= 9 and n % 2:
            values((n - 9) // 2)
    c.advance(16)

    wait(A, c.w_used_now())
    wait(V, c.w_used_now())
    turned = transpose_in(c, lambda t, k: ya[:, t, k * P:(k + 1) * P], KD, whole(zT[0]), whole(zT[1]),
                          [made["output", g] for g in range(HKV)])
    mixed = {}

    def mix(n, bank, done, j):
        t = slice(2 * n, 2 * n + 2)
        wait(V, done)
        a = dve(V.scalar_tensor_tensor(g1[:, t, :], g1[:, t, :], 1.0, bank, ALU.add, ALU.mult))
        wait(V, a)
        a = dve(V.tensor_tensor(g0[:, t, :], g0[:, t, :], g1[:, t, :], ALU.add))
        wait(A, a)
        a = act(A.activation(c.xT[0][:, t, :], g0[:, t, :], ACT.Copy, scale=0.5))
        wait(V, a)
        mixed[n] = dve(V.scalar_tensor_tensor(c.xT[1][:, t, :], g0[:, t, :], 0.5, c.xT[0][:, t, :].bitcast(F32),
                                              ALU.mult, ALU.subtract))

    feature_stage(c, None, 1, lambda n: d["w_o_attn"][n], zT, mix, dve, bank_free[15], ready=turned)

    wait(T, *made["o_free"])
    added = []
    for half in range(2):
        for b in range(2):
            j = 2 * half + b
            block = [ps[:, 4 + 2 * b + t, :] for t in range(NT)]
            c.load(j, d["w_out"][b, half])
            c.split(j + AHEAD)
            wait(T, mixed[2 * half], mixed[2 * half + 1])
            done = c.token_major(j, c.xT, 4 * half, 4, 512, block, half == 0, half == 1)
            if half == 1:
                wait(V, done)
                for t in range(NT):
                    r = c.res[:, t, b * 512:(b + 1) * 512]
                    a = dve(V.tensor_tensor(r, r, block[t], ALU.add))
                added.append((a,))
    c.advance(4)

    transposed = transpose_in(c, lambda t, k: c.res[:, t, k * P:(k + 1) * P], KD, whole(c.xT[0]), whole(c.xT[1]),
                              [added[k // 2] for k in range(4)], banks=(0, 1, 2, 3), weight=vec["norm2_w_2"])
    wait(A, *added[0], *added[1])
    for t in range(NT):
        squared = act(A.activation(junk2[:, t, :], c.res[:, t, :], ACT.Square, accum_out=squares[:, 0, t:t + 1]))
    wait(V, squared)
    a = dve(V.tensor_scalar(squares[:, 1, :], squares[:, 0, :], 1.0 / D, 1e-6, ALU.mult, ALU.add))
    wait(V, a)
    a = dve(V.reciprocal(c.rs[:, :], squares[:, 1, :]))

    def relu2(n, bank, done, j):
        at = bass.ds(n * 2, 2)
        wait(A, done, pool.now(3))
        relu = act(A.activation(fr[:, j, :, :], bank, ACT.Relu))
        wait(V, relu)
        square = dve(V.tensor_tensor(fr[:, j, :, :], fr[:, j, :, :], fr[:, j, :, :], ALU.mult))
        wait(A, square)
        hi = act(A.activation(fT[0][:, at, :], fr[:, j, :, :], ACT.Copy))
        wait(G, hi)
        pool(G.tensor_tensor(fT[1][:, at, :], fr[:, j, :, :], fT[0][:, at, :].bitcast(F32), ALU.subtract))

    wait(A, a)
    feature_stage(c, "feed_forward", 4, lambda n: d["w_ff_in"][bass.ds(n, 1)], c.xT, relu2, act, (), 2, ready=transposed)

    last_tiles = (dve.now(), act.now(), pool.now())
    c.last_unit = 16
    for b in range(2):
        block = [ps[:, 4 + 2 * b + t, :] for t in range(NT)]
        for q in range(8):
            j = 8 * b + q
            c.load(j, d["w_ff_out"][b, q])
            c.split(j + AHEAD)
            wait(T, *(last_tiles if j == 6 else (pool.now(2),)))
            done = c.token_major(j, fT, 4 * q, 4, 512, block, q == 0, q == 7)
        wait(V, done)
        for t in range(NT):
            r = c.res[:, t, b * 512:(b + 1) * 512]
            a = dve(V.scalar_tensor_tensor(r, block[t], c.rs[:, t:t + 1], r, ALU.mult, ALU.add))
            queue = c.SP if b else c.G
            wait(queue, a)
            queue.dma_start(out[0, t * P:(t + 1) * P, b * 512:(b + 1) * 512], r).then_inc(c.s_out if b else s_out0, 16)
    c.SP.wait_ge(c.s_out, 32)
    G.wait_ge(s_out0, 32)
    yield


LOOPS = {
    "retention": dict(pe=8, dve=38, act=16, pool=4),
    "feed_forward": dict(pe=0, dve=4, act=8, pool=4),
    "attention": dict(pe=14, dve=32, act=20, pool=6),
}


def build(nc, d, out, stop=None):
    c = Core(nc)
    c.ps = nc.alloc_psum_tensor("ps", [P, 8, 512], F32)
    c.raw = [c.place(f"w_raw{r}", [P, SLOT]) for r in range(RING)]
    c.hi = c.place("w_hi_ring", [P, RING, SLOT], F32R)
    c.lo = c.place("w_lo_ring", [P, RING, SLOT], F32R)
    c.res = c.place("res", [P, NT, D])
    c.xT = [c.place("xT_hi", [P, KD, S], F32R), c.place("xT_lo", [P, KD, S], F32R)]
    c.st = c.place("st", [P, NT, 2, 6])
    c.mv = c.place("mv", [P, NT, 2])
    norms = c.place("norms", [P, 4, NT])
    c.shift = norms[:, 3, :]
    c.rs, c.tmp = norms[:, 0, :], [norms[:, 1 + n, :] for n in range(2)]
    c.s_out = nc.alloc_semaphore("s_out")

    s_x = [nc.alloc_semaphore(f"s_x{b}") for b in range(2)]
    for b in range(2):
        cols = slice(b * 512, (b + 1) * 512)
        c.SP.dma_start(c.res[:, :, cols], d["x"][0][:, cols].rearrange("(t p) n -> p t n", p=P)).then_inc(s_x[b], 16)
    c.ident, t_ident = table(c, c.A, "ident", d["k_ident"], [P, P])
    wait(c.T, t_ident)
    wait(c.V, *((sem, 16) for sem in s_x))
    c.phase = c.top
    transposed = transpose_in(c, lambda t, k: c.res[:, t, k * P:(k + 1) * P], KD, whole(c.xT[0]), whole(c.xT[1]),
                              [((s_x[k // 2], 16),) for k in range(4)])
    for j in range(AHEAD):
        c.split(j)
    oT, after, hooks = retention_layer(c, d, transposed)
    lnw = load_ln(c, 0, d, c.top, ())
    c.last_unit = 8 if stop == 1 else None
    tables = []
    hooks[7] = [lambda: tables.append(latent_tables(c, d))]
    normed = output(c, d["a_w_out"], oT, ALPHA, [lnw], after, hooks)
    if stop == 1:
        return store(c, out, normed)
    keep_warm(c, WARM[0])
    transposed = transpose_in(c, lambda t, k: c.res[:, t, k * P:(k + 1) * P], KD, whole(c.xT[0]), whole(c.xT[1]),
                              [normed[k // 2] for k in range(4)])
    c.split(AHEAD - 1)
    oT, after, hooks = latent_attention_layer(c, d, transposed, tables[0])
    c.last_unit = 8 if stop == 2 else None
    hybrid = hybrid_layer(c, d, out)
    lnw = []
    hooks[5] = [lambda: lnw.append(load_ln(c, 1, d, c.phase + 2 * 4 * HB * S, (c.pe.now(), c.dve.now()))),
                lambda: next(hybrid)]
    normed = output(c, d["b_w_out"], oT, ALPHA, lnw, after, hooks)
    if stop == 2:
        return store(c, out, normed)
    keep_warm(c, WARM[1])
    hybrid.send(normed)


def store(c, out, after):
    wait(c.SP, *after[0], *after[1])
    c.SP.dma_start(out[0].rearrange("(t p) n -> p t n", p=P), c.res[:, :, :]).then_inc(c.s_out, 16)
    c.SP.wait_ge(c.s_out, 16)


COLUMNS = ("b_q_norm", "kv_norm", "norm1_w_2", "rg_ba_2", "rg_bx_2", "rg_lambda_2", "conv_b_2", "gate_b_2", "norm2_w_2")
COLUMNS_C = (("norm1_w_2", 8), ("norm2_w_2", 8), ("rg_ba_2", 8), ("rg_bx_2", 8), ("rg_lambda_2", 8), ("conv_b_2", 8),
             ("conv_w_2", 32), ("gate_b_2", 16), ("head_norms", 3))


def units(w, k, n):
    K, N = w.shape
    w = w.reshape(K // (P * k), k, P, N // n, n).transpose(3, 0, 2, 1, 4)
    return np.ascontiguousarray(w).reshape(N // n, K // (P * k), P, k * n)


def layout(inputs):
    out = {name: np.asarray(a) for name, a in inputs.items()}
    for name in COLUMNS:
        out[name] = np.ascontiguousarray(out[name].reshape(-1, P).T)
    w = out["a_w_in"][0]
    at = np.cumsum([HA * DKA, HA * DKA, WA])
    q, k, v, g = np.split(w, at, 1)
    out["a_w_in"] = np.concatenate([units(q, KD, DKA), units(k, KD, DKA), units(v, 4, DVA), units(g, 4, DVA)], 1)
    out["a_w_out"] = units(out["a_w_out"][0], 4, 512)
    w = out.pop("b_w_in")[0]
    out["b_w_qlat"] = units(w[:, :QL], 4, 384)
    out["b_w_gate"] = units(w[:, QL:], KD, 2 * VH)[:, 0]
    w = out["kv_w_down"]
    out["kv_w_down"] = units(np.concatenate([w, w[:, KVL:]], 1), 2, KVL + 2 * ROPE)
    w = out["b_w_uq"][0].reshape(QL, HB // 2, 2, NOPE + ROPE)
    w = np.concatenate([w[..., :NOPE].reshape(QL, HB // 2, -1), w[..., NOPE:].reshape(QL, HB // 2, -1)], 2)
    out["b_w_uq"] = units(w.reshape(QL, -1), 3, 2 * (NOPE + ROPE))
    w = out["kv_w_up"].reshape(KVL, HB // 2, 2, NOPE + VH)
    w = np.concatenate([w[..., :NOPE].reshape(KVL, HB // 2, -1), w[..., NOPE:].reshape(KVL, HB // 2, -1)], 2)
    out["kv_w_up"] = units(w.reshape(KVL, -1), 4, 512)[:, 0]
    out["b_w_out"] = units(out["b_w_out"][0], 4, 512)

    w = out.pop("w_in_2")[0]
    rnn_x, rnn_g, q, k, v, iq, ik, iw, gates = np.split(w, np.cumsum([DR, DR, D, 256, 256, IH * ID, ID, IH]), 1)
    group = HC // HKV
    order = [(t // group * 2 + half) * group + t % group for t in range(HC // 2) for half in range(2)]
    q = q.reshape(D, HC, DC)[:, order].reshape(D, D)
    out["w_qkvi"] = units(np.concatenate([q, k, v, iq], 1), 4, 512)
    out["w_ikw"] = units(np.concatenate([ik, ik, iw], 1), KD, 2 * ID + IH)[0, 0]
    out["w_rnn"] = units(np.concatenate([rnn_x, rnn_g], 1), KD, S)[:, 0]
    out["w_gates"] = units(gates, KD, S)[:, 0]
    for name in ("w_o_rnn", "w_o_attn"):
        out[name] = units(out.pop(name + "_2")[0], KD, S)[:, 0]
    out["w_out"] = units(out.pop("w_out_2")[0], 4, 512)
    out["w_ff_in"] = units(out.pop("w_ff_in_2")[0], KD, S)[:, 0]
    out["w_ff_out"] = units(out.pop("w_ff_out_2")[0], 4, 512)
    out["conv_w_2"] = np.ascontiguousarray(out["conv_w_2"][0].reshape(4, KD, P).transpose(2, 0, 1)).reshape(P, 4 * KD)
    norms = [np.tile(out.pop(n)[0], 2) for n in ("q_norm_w_2", "k_norm_w_2", "idx_k_norm_w_2")]
    out["head_norms"] = np.ascontiguousarray(np.stack(norms, 1))
    out["columns"] = np.ascontiguousarray(np.concatenate([out.pop(name) for name, _ in COLUMNS_C], 1))
    wa, wx = out.pop("rg_wa_2")[0], out.pop("rg_wx_2")[0]
    rg = np.zeros((P, 2, KD, P), wa.dtype)
    for n, w in enumerate((wa, wx)):
        for half in range(2):
            rows = slice(64 * half, 64 * half + 64)
            rg[rows, n, :, rows] = w[half::2].transpose(1, 0, 2)
    out["rg_w"] = rg.reshape(P, -1)
    return out


def rope_angles(dim):
    f = np.float32
    inv = (f(10000.0) ** (-np.arange(dim // 2, dtype=f) / f(dim // 2))).astype(f)
    return np.arange(S, dtype=f)[None, :] * inv[:, None]


def constants():
    f = np.float32
    ang = rope_angles(DKA)
    out = {"k_ident": np.eye(P, dtype=f), "k_ropeA": np.stack([np.cos(ang), np.sin(ang)], 1).astype(f)}
    lg = np.log1p(-np.exp2(-5.0 - np.arange(HA)))
    e, n = np.arange(P)[:, None], np.arange(S)[None, :]
    m = np.where(n >= e, np.exp(np.maximum(n - e, 0)[None] * lg[:, None, None]), 0.0) / np.sqrt(DKA)
    m = np.concatenate([m, m[:, :, 0:P]], 2)
    out["k_decay"] = np.ascontiguousarray(m.transpose(1, 0, 2)).astype(f)
    ang = np.tile(rope_angles(ROPE), (2 * P // ROPE, 1))
    out["k_ropeB"] = np.stack([np.cos(ang), np.sin(ang)], 1).astype(f)
    rot = np.zeros((P, P), f)
    for r in range(P):
        half = ROPE // 2
        if r % ROPE < half:
            rot[r + half, r] = -1.0
        else:
            rot[r - half, r] = 1.0
    out["k_rotB"] = rot
    causal = np.where(np.arange(P)[None, :] <= np.arange(P)[:, None], 0.0, -1.0e30).astype(f)
    out["k_maskB"] = np.concatenate([causal, np.zeros((P, P), f), causal], 1)
    return out


def kernel(**inputs):
    import concourse.bacc as bacc
    from concourse.bass_utils import run_bass_kernel_spmd

    arrays = {**layout(inputs), **constants()}
    nc = bacc.Bacc("TRN2", target_bir_lowering=False, num_devices=1)
    d = {n: nc.dram_tensor("in_" + n, a.shape, mybir.dt.from_np(a.dtype), kind="ExternalInput").ap()
         for n, a in arrays.items()}
    out = nc.dram_tensor("out", (1, S, D), F32, kind="ExternalOutput").ap()
    build(nc, d, out)
    r = run_bass_kernel_spmd(nc, [{"in_" + n: a for n, a in arrays.items()}], core_ids=[0])
    return r.results[0]["out"]
```
